# Optimizing a Trainium2 kernel written in Bass

```python
import math
import jax
import jax.numpy as jnp
from jax import lax
import numpy as np
import jax, jax.numpy as jnp

D_MODEL = 1024
BATCH = 1
SEQ = 512
DEPTH = 1

N_HEADS_A = 8
HEAD_DIM = 64
WIDTH_A = N_HEADS_A * HEAD_DIM
KV_RANK = 128
IDX_HEADS = 8
IDX_DIM = 64
TOPK_MAX = 256
N_HEADS_B = 8
WIDTH_B = N_HEADS_B * HEAD_DIM
BLOCK_Q = 128
N_BUCKETS = 32
MAX_EXACT = N_BUCKETS // 2
MAX_DISTANCE = 128
ATTN_SCALE = HEAD_DIM ** -0.5
IDX_SCALE = (IDX_HEADS ** -0.5) * (IDX_DIM ** -0.5)
N_GROUPS = 4
EXPERTS_PER_GROUP = 8
N_EXPERTS = N_GROUPS * EXPERTS_PER_GROUP
D_EXPERT = 256
TOP_K_INNER = 2
PLE_DIM = 256
EPS = 1e-6

_COLS = [
    ("q_a", WIDTH_A),
    ("c_kv", KV_RANK),
    ("q_idx", IDX_HEADS * IDX_DIM),
    ("k_idx", IDX_DIM),
    ("w_idx", IDX_HEADS),
    ("qkv_b", 3 * WIDTH_B),
    ("gate_a", D_MODEL),
    ("gate_b", D_MODEL),
]
IN_COLS = sum(c for _, c in _COLS)


def _rmsnorm(x, g):
    xf = x.astype(jnp.float32)
    y = xf * lax.rsqrt(jnp.mean(xf * xf, axis=-1, keepdims=True) + EPS)
    return (y * g.astype(jnp.float32)).astype(x.dtype)

def _split_cols(proj):
    out = []
    start = 0
    for _, width in _COLS:
        out.append(proj[..., start:start + width])
        start += width
    return out

def _t5_bucket(dist):
    dist = jnp.maximum(dist, 0)
    d_f = jnp.maximum(dist, 1).astype(jnp.float32)
    large = MAX_EXACT + (jnp.log(d_f / MAX_EXACT) / math.log(MAX_DISTANCE / MAX_EXACT)
                         * (N_BUCKETS - MAX_EXACT)).astype(jnp.int32)
    large = jnp.minimum(large, N_BUCKETS - 1)
    return jnp.where(dist < MAX_EXACT, dist, large)

def _dsa_branch(q, c_kv, q_idx, k_idx, w_idx, w_uk, w_uv, rel_bias):
    b, s = q.shape[0], q.shape[1]
    n_sel = min(TOPK_MAX, s // 4)
    n_blocks = s // BLOCK_Q
    q_abs = jnp.einsum("bshd,hcd->bshc", q, w_uk)
    key_pos = jnp.arange(s, dtype=jnp.int32)
    gather = jax.vmap(lambda c, i: c[i])

    def block(i):
        start = i * BLOCK_Q
        t = start + jnp.arange(BLOCK_Q, dtype=jnp.int32)
        qa = lax.dynamic_slice_in_dim(q_abs, start, BLOCK_Q, axis=1)
        qi = lax.dynamic_slice_in_dim(q_idx, start, BLOCK_Q, axis=1)
        wi = lax.dynamic_slice_in_dim(w_idx, start, BLOCK_Q, axis=1).astype(jnp.float32)
        rel = jax.nn.relu(jnp.einsum("bqhe,bse->bqhs", qi, k_idx).astype(jnp.float32))
        score = jnp.einsum("bqhs,bqh->bqs", rel, wi)
        causal = key_pos[None, :] <= t[:, None]
        score = jnp.where(causal[None], score, -jnp.inf)
        _, idx = lax.top_k(score, n_sel)
        valid = idx <= t[None, :, None]
        c_sel = gather(c_kv, idx)
        logits = jnp.einsum("bqhc,bqkc->bhqk", qa, c_sel).astype(jnp.float32) * ATTN_SCALE
        bias = rel_bias[_t5_bucket(t[None, :, None] - idx)]
        logits = logits + jnp.transpose(bias, (0, 3, 1, 2)).astype(jnp.float32)
        logits = jnp.where(valid[:, None], logits, -jnp.inf)
        probs = jax.nn.softmax(logits, axis=-1).astype(c_sel.dtype)
        return jnp.einsum("bhqk,bqkc->bqhc", probs, c_sel)

    o = lax.map(block, jnp.arange(n_blocks, dtype=jnp.int32))
    o = jnp.moveaxis(o, 0, 1).reshape(b, s, N_HEADS_A, KV_RANK)
    return jnp.einsum("bshc,hcd->bshd", o, w_uv)

def _stick_breaking_branch(q, k, v):
    b, s = q.shape[0], q.shape[1]
    n_blocks = s // BLOCK_Q
    key_pos = jnp.arange(s, dtype=jnp.int32)

    def block(i):
        start = i * BLOCK_Q
        t = start + jnp.arange(BLOCK_Q, dtype=jnp.int32)
        qb = lax.dynamic_slice_in_dim(q, start, BLOCK_Q, axis=1)
        z = jnp.einsum("bqhd,bshd->bhqs", qb, k).astype(jnp.float32) * ATTN_SCALE
        mask = (key_pos[None, :] < t[:, None])[None, None]
        log_1m = jnp.where(mask, jax.nn.log_sigmoid(-z), 0.0)
        after = lax.cumsum(log_1m, axis=3, reverse=True) - log_1m
        log_a = jax.nn.log_sigmoid(z) + after
        a = jnp.where(mask, jnp.exp(log_a), 0.0).astype(v.dtype)
        return jnp.einsum("bhqs,bshd->bqhd", a, v)

    o = lax.map(block, jnp.arange(n_blocks, dtype=jnp.int32))
    return jnp.moveaxis(o, 0, 1).reshape(b, s, N_HEADS_B, HEAD_DIM)

def _hier_moe(h, w_r1, b_r1, w_r2, b_r2, w_gate, w_up, w_down):
    b, s, d = h.shape
    hf = h.reshape(b * s, d)
    n_tok = b * s
    g_logits = jnp.matmul(hf, w_r1).astype(jnp.float32) + b_r1.astype(jnp.float32)
    g_prob = jax.nn.softmax(g_logits, axis=-1)
    g_sel = jnp.argmax(g_logits, axis=-1)
    p_g = jnp.take_along_axis(g_prob, g_sel[:, None], axis=1)[:, 0]
    e_logits = jnp.einsum("nd,gde->nge", hf, w_r2).astype(jnp.float32) + b_r2.astype(jnp.float32)
    e_sel = jnp.take_along_axis(e_logits, g_sel[:, None, None], axis=1)[:, 0]
    top_v, top_i = lax.top_k(e_sel, TOP_K_INNER)
    w_inner = jax.nn.softmax(top_v, axis=-1)
    inner = jnp.sum(jax.nn.one_hot(top_i, EXPERTS_PER_GROUP, dtype=jnp.float32) * w_inner[..., None], axis=1)
    comb = (jax.nn.one_hot(g_sel, N_GROUPS, dtype=jnp.float32)[:, :, None]
            * inner[:, None, :] * p_g[:, None, None])
    comb = comb.reshape(n_tok, N_EXPERTS).astype(h.dtype)
    out = jnp.zeros_like(hf)
    for e in range(N_EXPERTS):
        hid = jax.nn.silu(jnp.matmul(hf, w_gate[e])) * jnp.matmul(hf, w_up[e])
        out = out + comb[:, e:e + 1] * jnp.matmul(hid, w_down[e])
    return out.reshape(b, s, d)

def first_inputs(seed: int = 0) -> dict:
    key = jax.random.key(seed)
    ks = jax.random.split(key, 24)
    f32 = jnp.float32

    def nrm(k, shape, fan_in):
        return jax.random.normal(k, shape, f32) * (fan_in ** -0.5)

    def gain(k, shape):
        return 1.0 + 0.05 * jax.random.normal(k, shape, f32)

    return {
        "x": jax.random.normal(ks[0], (BATCH, SEQ, D_MODEL), f32),
        "p": jax.random.normal(ks[1], (DEPTH, BATCH, SEQ, PLE_DIM), f32),
        "attn_norm": gain(ks[2], (DEPTH, D_MODEL)),
        "w_in": nrm(ks[3], (DEPTH, D_MODEL, IN_COLS), D_MODEL),
        "kv_norm": gain(ks[4], (DEPTH, KV_RANK)),
        "w_uk": nrm(ks[5], (DEPTH, N_HEADS_A, KV_RANK, HEAD_DIM), KV_RANK),
        "w_uv": nrm(ks[6], (DEPTH, N_HEADS_A, KV_RANK, HEAD_DIM), KV_RANK),
        "rel_bias": 0.5 * jax.random.normal(ks[7], (N_BUCKETS, N_HEADS_A), f32),
        "w_branch_a": nrm(ks[8], (DEPTH, WIDTH_A, D_MODEL), WIDTH_A),
        "w_branch_b": nrm(ks[9], (DEPTH, WIDTH_B, D_MODEL), WIDTH_B),
        "w_out": nrm(ks[10], (DEPTH, D_MODEL, D_MODEL), D_MODEL),
        "ffn_norm": gain(ks[11], (DEPTH, D_MODEL)),
        "w_r1": nrm(ks[12], (DEPTH, D_MODEL, N_GROUPS), D_MODEL),
        "b_r1": 0.01 * jax.random.normal(ks[13], (DEPTH, N_GROUPS), f32),
        "w_r2": nrm(ks[14], (DEPTH, N_GROUPS, D_MODEL, EXPERTS_PER_GROUP), D_MODEL),
        "b_r2": 0.01 * jax.random.normal(ks[15], (DEPTH, N_GROUPS, EXPERTS_PER_GROUP), f32),
        "w_gate": nrm(ks[16], (DEPTH, N_EXPERTS, D_MODEL, D_EXPERT), D_MODEL),
        "w_up": nrm(ks[17], (DEPTH, N_EXPERTS, D_MODEL, D_EXPERT), D_MODEL),
        "w_down": nrm(ks[18], (DEPTH, N_EXPERTS, D_EXPERT, D_MODEL), D_EXPERT),
        "ple_norm": gain(ks[19], (DEPTH, D_MODEL)),
        "w_ple_gate": nrm(ks[20], (DEPTH, D_MODEL, D_MODEL), D_MODEL),
        "w_ple": nrm(ks[21], (DEPTH, PLE_DIM, D_MODEL), PLE_DIM),
        "final_norm": gain(ks[22], (D_MODEL,)),
    }

def first_block(x, p, attn_norm, w_in, kv_norm, w_uk, w_uv, rel_bias, w_branch_a, w_branch_b,
              w_out, ffn_norm, w_r1, b_r1, w_r2, b_r2, w_gate, w_up, w_down,
              ple_norm, w_ple_gate, w_ple, final_norm):
    b, s, _ = x.shape
    for i in range(DEPTH):
        h = _rmsnorm(x, attn_norm[i])
        proj = jnp.matmul(h, w_in[i])
        q_a, c_kv, q_idx, k_idx, w_idx, qkv_b, gate_a, gate_b = _split_cols(proj)
        q_a = q_a.reshape(b, s, N_HEADS_A, HEAD_DIM)
        c_kv = _rmsnorm(c_kv, kv_norm[i])
        q_idx = q_idx.reshape(b, s, IDX_HEADS, IDX_DIM)
        w_idx = w_idx * IDX_SCALE
        q_b, k_b, v_b = jnp.split(qkv_b.reshape(b, s, 3, N_HEADS_B, HEAD_DIM), 3, axis=2)
        o_a = _dsa_branch(q_a, c_kv, q_idx, k_idx, w_idx, w_uk[i], w_uv[i], rel_bias)
        o_b = _stick_breaking_branch(q_b[:, :, 0], k_b[:, :, 0], v_b[:, :, 0])
        y_a = jnp.matmul(o_a.reshape(b, s, WIDTH_A), w_branch_a[i])
        y_b = jnp.matmul(o_b.reshape(b, s, WIDTH_B), w_branch_b[i])
        merged = jax.nn.sigmoid(gate_a) * y_a + jax.nn.sigmoid(gate_b) * y_b
        x = x + jnp.matmul(merged, w_out[i])
        h2 = _rmsnorm(x, ffn_norm[i])
        x = x + _hier_moe(h2, w_r1[i], b_r1[i], w_r2[i], b_r2[i], w_gate[i], w_up[i], w_down[i])
        h3 = _rmsnorm(x, ple_norm[i])
        x = x + jnp.matmul(p[i], w_ple[i]) * jax.nn.sigmoid(jnp.matmul(h3, w_ple_gate[i]))
    return _rmsnorm(x, final_norm)


DEPTH_2 = 2

N_META = 16
N_EVEN = (DEPTH_2 + 1) // 2
N_ODD = DEPTH_2 // 2

LRU_WIDTH = D_MODEL // 2
LRU_HEADS = 4
LRU_HEAD_DIM = LRU_WIDTH // LRU_HEADS
CONV_WIDTH = 4
LRU_C = 8.0

MLA_HEADS = 8
MLA_NOPE = 64
MLA_ROPE = 32
MLA_V = 64
MLA_Q_RANK = D_MODEL // 4
MLA_KV_RANK = D_MODEL // 8
ATTN_BLOCK = 128

EVEN_IN = 2 * LRU_WIDTH + MLA_Q_RANK + MLA_KV_RANK + MLA_ROPE
EVEN_MIX = LRU_WIDTH + MLA_HEADS * MLA_V

RET_HEADS = 4
RET_QK_DIM = D_MODEL // RET_HEADS
RET_V_DIM = 2 * RET_QK_DIM
RET_CHUNK = 128
RET_IN = 2 * RET_HEADS * RET_QK_DIM + 2 * RET_HEADS * RET_V_DIM
RET_MIX = RET_HEADS * RET_V_DIM

D_FF = 4 * D_MODEL
ROPE_BASE = 10000.0
DN_ALPHA = (2 * DEPTH_2) ** 0.25
DN_BETA = (8 * DEPTH_2) ** -0.25
EPS_2 = 1e-5
NEG_INF = -1e30


def _layernorm(x, g, b):
    xf = x.astype(jnp.float32)
    mu = jnp.mean(xf, axis=-1, keepdims=True)
    xc = xf - mu
    var = jnp.mean(jnp.square(xc), axis=-1, keepdims=True)
    return (xc * lax.rsqrt(var + EPS_2) * g + b).astype(x.dtype)

def _rmsnorm_2(x, g):
    xf = x.astype(jnp.float32)
    y = xf * lax.rsqrt(jnp.mean(jnp.square(xf), axis=-1, keepdims=True) + EPS_2)
    return (y * g).astype(x.dtype)

def _rope(x, pos):
    half = x.shape[-1] // 2
    inv = ROPE_BASE ** (-jnp.arange(half, dtype=jnp.float32) / half)
    ang = pos.astype(jnp.float32)[:, None] * inv[None, :]
    cos = jnp.cos(ang)[None, :, None, :].astype(x.dtype)
    sin = jnp.sin(ang)[None, :, None, :].astype(x.dtype)
    x1, x2 = x[..., :half], x[..., half:]
    return jnp.concatenate([x1 * cos - x2 * sin, x1 * sin + x2 * cos], axis=-1)

def _lru_combine(c1, c2):
    a1, b1 = c1
    a2, b2 = c2
    return a1 * a2, a2 * b1 + b2

def _rglru_group(p_gate, p_rec, conv_w, conv_b, w_rg_a, b_rg_a, w_rg_x, b_rg_x, lru_lambda):
    B, T, _ = p_rec.shape
    xc = lax.conv_general_dilated(
        p_rec, conv_w[:, None, :], window_strides=(1,), padding=[(CONV_WIDTH - 1, 0)],
        dimension_numbers=('NWC', 'WIO', 'NWC'), feature_group_count=LRU_WIDTH) + conv_b
    xh = xc.reshape(B, T, LRU_HEADS, LRU_HEAD_DIM)
    r = jax.nn.sigmoid(jnp.einsum('bthi,hij->bthj', xh, w_rg_a).reshape(B, T, LRU_WIDTH) + b_rg_a)
    i = jax.nn.sigmoid(jnp.einsum('bthi,hij->bthj', xh, w_rg_x).reshape(B, T, LRU_WIDTH) + b_rg_x)
    log_a = (-LRU_C * r * jax.nn.softplus(-lru_lambda)).astype(jnp.float32)
    a = jnp.exp(log_a)
    mult = jnp.sqrt(-jnp.expm1(2.0 * log_a))
    b = mult * (i * xc).astype(jnp.float32)
    _, h = lax.associative_scan(_lru_combine, (a, b), axis=1)
    return h.astype(p_rec.dtype) * jax.nn.gelu(p_gate)

def _attend(qb, qpos, k, v, kpos):
    scale = qb.shape[-1] ** -0.5
    s = jnp.einsum('bqhd,bkhd->bhqk', qb, k).astype(jnp.float32) * scale
    mask = kpos[None, :] <= qpos[:, None]
    s = jnp.where(mask[None, None], s, NEG_INF)
    p = jax.nn.softmax(s, axis=-1).astype(v.dtype)
    return jnp.einsum('bhqk,bkhd->bqhd', p, v)

def _causal_attention(q, k, v, pos):
    B, T, H, d = q.shape
    dv = v.shape[-1]
    out_meta = _attend(q[:, :N_META], pos[:N_META], k[:, :N_META], v[:, :N_META], pos[:N_META])
    nb = (T - N_META) // ATTN_BLOCK
    qr = q[:, N_META:].reshape(B, nb, ATTN_BLOCK, H, d).swapaxes(0, 1)
    pr = pos[N_META:].reshape(nb, ATTN_BLOCK)
    out_r = lax.map(lambda a: _attend(a[0], a[1], k, v, pos), (qr, pr))
    out_r = out_r.swapaxes(0, 1).reshape(B, T - N_META, H, dv)
    return jnp.concatenate([out_meta, out_r], axis=1)

def _mla_group(p_q, p_kv, p_kpe, pos, q_norm_g, w_uq, kv_norm_g, w_ukv):
    B, T, _ = p_q.shape
    q = (_rmsnorm_2(p_q, q_norm_g) @ w_uq).reshape(B, T, MLA_HEADS, MLA_NOPE + MLA_ROPE)
    q_nope, q_pe = q[..., :MLA_NOPE], _rope(q[..., MLA_NOPE:], pos)
    kv = (_rmsnorm_2(p_kv, kv_norm_g) @ w_ukv).reshape(B, T, MLA_HEADS, MLA_NOPE + MLA_V)
    k_nope, v = kv[..., :MLA_NOPE], kv[..., MLA_NOPE:]
    k_pe = _rope(p_kpe[:, :, None, :], pos)
    q = jnp.concatenate([q_nope, q_pe], axis=-1)
    k = jnp.concatenate([k_nope, jnp.broadcast_to(k_pe, (B, T, MLA_HEADS, MLA_ROPE))], axis=-1)
    o = _causal_attention(q, k, v, pos)
    return o.reshape(B, T, MLA_HEADS * MLA_V)

def _even_mixer(x, pos, w_in, conv_w, conv_b, w_rg_a, b_rg_a, w_rg_x, b_rg_x, lru_lambda,
                q_norm_g, w_uq, kv_norm_g, w_ukv, w_out):
    p = x @ w_in
    cuts = [LRU_WIDTH, 2 * LRU_WIDTH, 2 * LRU_WIDTH + MLA_Q_RANK,
            2 * LRU_WIDTH + MLA_Q_RANK + MLA_KV_RANK]
    p_gate, p_rec, p_q, p_kv, p_kpe = jnp.split(p, cuts, axis=-1)
    y_rec = _rglru_group(p_gate, p_rec, conv_w, conv_b, w_rg_a, b_rg_a, w_rg_x, b_rg_x, lru_lambda)
    y_att = _mla_group(p_q, p_kv, p_kpe, pos, q_norm_g, w_uq, kv_norm_g, w_ukv)
    return jnp.concatenate([y_rec, y_att], axis=-1) @ w_out

def _retention_chunk(q, k, v, s_prev, log_gamma):
    dt = q.dtype
    c = q.shape[2]
    idx = jnp.arange(c, dtype=jnp.float32)
    diff = idx[:, None] - idx[None, :]
    decay = jnp.where(diff >= 0, jnp.exp(log_gamma[:, None, None] * jnp.maximum(diff, 0.0)), 0.0).astype(dt)
    q_decay = jnp.exp(log_gamma[:, None] * (idx + 1.0))[None, :, :, None].astype(dt)
    k_decay = jnp.exp(log_gamma[:, None] * (c - 1.0 - idx))[None, :, :, None].astype(dt)
    chunk_decay = jnp.exp(log_gamma * c)[None, :, None, None].astype(dt)
    scores = jnp.einsum('bhid,bhjd->bhij', q, k) * decay
    o = jnp.einsum('bhij,bhjv->bhiv', scores, v) + q_decay * jnp.einsum('bhid,bhdv->bhiv', q, s_prev)
    s_new = chunk_decay * s_prev + jnp.einsum('bhjd,bhjv->bhdv', k * k_decay, v)
    return o, s_new

def _odd_mixer(x, pos, w_in, w_out):
    B, T, _ = x.shape
    qk = RET_HEADS * RET_QK_DIM
    p = x @ w_in
    q, k, v, g = jnp.split(p, [qk, 2 * qk, 2 * qk + RET_MIX], axis=-1)
    q = _rope(q.reshape(B, T, RET_HEADS, RET_QK_DIM), pos)
    k = _rope(k.reshape(B, T, RET_HEADS, RET_QK_DIM), pos) * (RET_QK_DIM ** -0.5)
    v = v.reshape(B, T, RET_HEADS, RET_V_DIM)
    q, k, v = (t.transpose(0, 2, 1, 3) for t in (q, k, v))
    log_gamma = jnp.log(1.0 - 2.0 ** (-5.0 - jnp.arange(RET_HEADS, dtype=jnp.float32)))
    s0 = jnp.zeros((B, RET_HEADS, RET_QK_DIM, RET_V_DIM), dtype=q.dtype)
    o_meta, s = _retention_chunk(q[:, :, :N_META], k[:, :, :N_META], v[:, :, :N_META], s0, log_gamma)
    nc = (T - N_META) // RET_CHUNK

    def to_chunks(t):
        return t[:, :, N_META:].reshape(B, RET_HEADS, nc, RET_CHUNK, t.shape[-1]).transpose(2, 0, 1, 3, 4)

    def body(state, qkv):
        qc, kc, vc = qkv
        o, state = _retention_chunk(qc, kc, vc, state, log_gamma)
        return state, o

    _, o_r = lax.scan(body, s, (to_chunks(q), to_chunks(k), to_chunks(v)))
    o_r = o_r.transpose(1, 2, 0, 3, 4).reshape(B, RET_HEADS, T - N_META, RET_V_DIM)
    o = jnp.concatenate([o_meta, o_r], axis=2)
    of = o.astype(jnp.float32)
    o = (of * lax.rsqrt(jnp.mean(jnp.square(of), axis=-1, keepdims=True) + EPS_2)).astype(x.dtype)
    y = o.transpose(0, 2, 1, 3).reshape(B, T, RET_MIX)
    return (jax.nn.silu(g) * y) @ w_out

def second_inputs(seed: int = 0) -> dict:
    key = jax.random.key(seed)
    ks = iter(jax.random.split(key, 40))
    f32 = jnp.float32

    def nrm(shape, scale):
        return jax.random.normal(next(ks), shape, f32) * scale

    u = jax.random.uniform(next(ks), (N_EVEN, LRU_WIDTH), f32, minval=0.9, maxval=0.999)
    a_base = u ** (1.0 / LRU_C)
    lru_lambda = jnp.log(a_base) - jnp.log1p(-a_base)
    return {
        'x': nrm((BATCH, SEQ, D_MODEL), 1.0),
        'meta_tokens': nrm((N_META, D_MODEL), 1.0),
        'ev_w_in': nrm((N_EVEN, D_MODEL, EVEN_IN), D_MODEL ** -0.5),
        'ev_conv_w': nrm((N_EVEN, CONV_WIDTH, LRU_WIDTH), CONV_WIDTH ** -0.5),
        'ev_conv_b': nrm((N_EVEN, LRU_WIDTH), 0.02),
        'ev_w_rg_a': nrm((N_EVEN, LRU_HEADS, LRU_HEAD_DIM, LRU_HEAD_DIM), LRU_HEAD_DIM ** -0.5),
        'ev_b_rg_a': nrm((N_EVEN, LRU_WIDTH), 0.02),
        'ev_w_rg_x': nrm((N_EVEN, LRU_HEADS, LRU_HEAD_DIM, LRU_HEAD_DIM), LRU_HEAD_DIM ** -0.5),
        'ev_b_rg_x': nrm((N_EVEN, LRU_WIDTH), 0.02),
        'ev_lru_lambda': lru_lambda,
        'ev_q_norm_g': 1.0 + nrm((N_EVEN, MLA_Q_RANK), 0.02),
        'ev_w_uq': nrm((N_EVEN, MLA_Q_RANK, MLA_HEADS * (MLA_NOPE + MLA_ROPE)), MLA_Q_RANK ** -0.5),
        'ev_kv_norm_g': 1.0 + nrm((N_EVEN, MLA_KV_RANK), 0.02),
        'ev_w_ukv': nrm((N_EVEN, MLA_KV_RANK, MLA_HEADS * (MLA_NOPE + MLA_V)), MLA_KV_RANK ** -0.5),
        'ev_w_out': nrm((N_EVEN, EVEN_MIX, D_MODEL), DN_BETA * EVEN_MIX ** -0.5),
        'od_w_in': nrm((N_ODD, D_MODEL, RET_IN), D_MODEL ** -0.5),
        'od_w_out': nrm((N_ODD, RET_MIX, D_MODEL), DN_BETA * RET_MIX ** -0.5),
        'ln_mix_g': 1.0 + nrm((DEPTH_2, D_MODEL), 0.02),
        'ln_mix_b': nrm((DEPTH_2, D_MODEL), 0.02),
        'mlp_w1': nrm((DEPTH_2, D_MODEL, D_FF), D_MODEL ** -0.5),
        'mlp_w2': nrm((DEPTH_2, D_FF, D_MODEL), DN_BETA * D_FF ** -0.5),
        'ln_mlp_g': 1.0 + nrm((DEPTH_2, D_MODEL), 0.02),
        'ln_mlp_b': nrm((DEPTH_2, D_MODEL), 0.02),
    }

def second_block(x, meta_tokens, ev_w_in, ev_conv_w, ev_conv_b, ev_w_rg_a, ev_b_rg_a, ev_w_rg_x,
              ev_b_rg_x, ev_lru_lambda, ev_q_norm_g, ev_w_uq, ev_kv_norm_g, ev_w_ukv, ev_w_out,
              od_w_in, od_w_out, ln_mix_g, ln_mix_b, mlp_w1, mlp_w2, ln_mlp_g, ln_mlp_b):
    B = x.shape[0]
    meta = jnp.broadcast_to(meta_tokens[None].astype(x.dtype), (B, N_META, D_MODEL))
    h = jnp.concatenate([meta, x], axis=1)
    pos = jnp.arange(h.shape[1], dtype=jnp.int32)
    for l in range(DEPTH_2):
        if l % 2 == 0:
            e = l // 2
            mix = _even_mixer(h, pos, ev_w_in[e], ev_conv_w[e], ev_conv_b[e], ev_w_rg_a[e], ev_b_rg_a[e],
                              ev_w_rg_x[e], ev_b_rg_x[e], ev_lru_lambda[e], ev_q_norm_g[e], ev_w_uq[e],
                              ev_kv_norm_g[e], ev_w_ukv[e], ev_w_out[e])
        else:
            o = l // 2
            mix = _odd_mixer(h, pos, od_w_in[o], od_w_out[o])
        h = _layernorm(DN_ALPHA * h + mix, ln_mix_g[l], ln_mix_b[l])
        f = jnp.square(jax.nn.relu(h @ mlp_w1[l])) @ mlp_w2[l]
        h = _layernorm(DN_ALPHA * h + f, ln_mlp_g[l], ln_mlp_b[l])
    return h[:, N_META:]


def setup_inputs(seed=0):
    out = dict(first_inputs(seed))
    for name, value in second_inputs(seed + 1).items():
        if name != "x":
            out[name + "_2"] = value
    return out


def reference(
    x, p, attn_norm, w_in, kv_norm, w_uk, w_uv, rel_bias, w_branch_a, w_branch_b, w_out,
    ffn_norm, w_r1, b_r1, w_r2, b_r2, w_gate, w_up, w_down, ple_norm, w_ple_gate, w_ple,
    final_norm, meta_tokens_2, ev_w_in_2, ev_conv_w_2, ev_conv_b_2, ev_w_rg_a_2, ev_b_rg_a_2,
    ev_w_rg_x_2, ev_b_rg_x_2, ev_lru_lambda_2, ev_q_norm_g_2, ev_w_uq_2, ev_kv_norm_g_2,
    ev_w_ukv_2, ev_w_out_2, od_w_in_2, od_w_out_2, ln_mix_g_2, ln_mix_b_2, mlp_w1_2, mlp_w2_2,
    ln_mlp_g_2, ln_mlp_b_2,
):
    x = first_block(
        x, p, attn_norm, w_in, kv_norm, w_uk, w_uv, rel_bias, w_branch_a, w_branch_b, w_out,
        ffn_norm, w_r1, b_r1, w_r2, b_r2, w_gate, w_up, w_down, ple_norm, w_ple_gate, w_ple,
        final_norm,
    )
    return second_block(
        x, meta_tokens_2, ev_w_in_2, ev_conv_w_2, ev_conv_b_2, ev_w_rg_a_2, ev_b_rg_a_2,
        ev_w_rg_x_2, ev_b_rg_x_2, ev_lru_lambda_2, ev_q_norm_g_2, ev_w_uq_2, ev_kv_norm_g_2,
        ev_w_ukv_2, ev_w_out_2, od_w_in_2, od_w_out_2, ln_mix_g_2, ln_mix_b_2, mlp_w1_2,
        mlp_w2_2, ln_mlp_g_2, ln_mlp_b_2,
    )


_drawn_inputs = setup_inputs


def setup_inputs(seed=0):
    import zlib

    import numpy as np

    out = dict(_drawn_inputs(seed))
    spreads = {}
    factors = {'kv_norm': 2.809,
     'b_r1': 7.657,
     'b_r2': 6.272,
     'ple_norm': 5.872,
     'ev_conv_b_2': 27.248,
     'ev_b_rg_a_2': 200.0,
     'ev_b_rg_x_2': 200.0,
     'ev_q_norm_g_2': 8.0,
     'ev_kv_norm_g_2': 8.0,
     'ev_w_rg_a_2': 32.384,
     'ev_lru_lambda_2': 23.232,
     'ev_conv_w_2': 8.0,
     'ev_w_rg_x_2': 8.0}
    for name, (base, spread) in spreads.items():
        noise = np.random.default_rng([zlib.crc32(name.encode()), seed]).standard_normal(out[name].shape)
        drawn = base * np.exp(spread * noise) if base else spread * noise
        out[name] = jnp.asarray(drawn.astype(out[name].dtype))
    for name, factor in factors.items():
        out[name] = (out[name] * factor).astype(out[name].dtype)
    return out
```

```python
import math
from contextlib import ExitStack, contextmanager

import numpy as np
import concourse.bass as bass
from concourse import mybir

F32 = mybir.dt.float32
ALU = mybir.AluOpType
ACT = mybir.ActivationFunctionType
AX = mybir.AxisListType.X
ds = bass.ds

P = 128
D = 1024
DT = D // P
SEQ = 512
META = 16
T2 = SEQ + META
HALF = T2 // 2
QT = SEQ // P
HEADS = 8
HD = 64
PAIRS = HEADS // 2
KV_RANK = 128
N_SEL = min(256, SEQ // 4)
IDX_SCALE = (8 ** -0.5) * (64 ** -0.5)
QK_SCALE = HD ** -0.5
N_BUCKETS = 32
GROUPS, PER_GROUP = 4, 8
EXPERTS = GROUPS * PER_GROUP
EPS1, EPS2 = 1e-6, 1e-5
ALPHA = 4.0 ** 0.25
MLA_SCALE = 96 ** -0.5
RET_HEADS = 4
LRU_C = 8.0
FF = 4 * D
NEG = -1.0e30
LOW = -1.0e38
TAKEN = -3.0e38

CHUNKS = [("kv", 2), ("qidx", 4), ("qa", 4), ("qb", 4), ("kb", 4), ("vb", 4), ("gates", 16), ("ukuv", 1),
          ("merge", 8), ("wout", 8), ("moe", 6 * EXPERTS), ("ple", 10),
          ("evin", 13), ("rg", 1), ("uq", 3), ("ukv", 1), ("evout", 8), ("up0", 32), ("down0", 32),
          ("odqk", 16), ("odv", 16), ("odg", 16), ("odout", 16), ("up1", 32), ("down1", 32)]
N_CHUNKS = sum(n for _, n in CHUNKS)
SLOTS = 8

VECS = [("attn_norm", 8), ("kv_norm", 1), ("ffn_norm", 8), ("ple_norm", 8), ("final_norm", 8),
        ("conv_w", 16), ("conv_b", 4), ("b_rg_a", 4), ("b_rg_x", 4), ("lam", 4), ("q_norm", 2), ("kv_norm2", 1),
        ("ln_mix_g", 16), ("ln_mix_b", 16), ("ln_mlp_g", 16), ("ln_mlp_b", 16)]
VEC_AT, _n = {}, 0
for _name, _w in VECS:
    VEC_AT[_name] = _n
    _n += _w
N_VEC = _n

TOK2 = [(0, META)] + [(META + P * i, P) for i in range(QT)]
BIAS_W = SEQ + P


class Counts:

    def __init__(self, eng):
        self.eng = eng
        self.base, self.local, self.per, self.i = {}, {}, {}, None

    def value(self, name, back=0):
        at = self.base.get(name, 0) + self.local.get(name, 0) - back
        return at if self.i is None or not self.per.get(name) else self.i * self.per[name] + at

    def count(self, name, k=1):
        assert self.i is None or name in self.per, name
        self.local[name] = self.local.get(name, 0) + k

    def next(self, name, k=1):
        self.count(name, k)
        return self.value(name)

    def counted(self, name, back=0):
        return self.base.get(name, 0) + self.local.get(name, 0) > back

    @contextmanager
    def loop(self, times, **per):
        for n, k in self.local.items():
            self.base[n] = self.base.get(n, 0) + k
        self.local, self.per = {}, per
        with self.eng.Fori(0, times) as i:
            self.i = i
            yield i
        self.i = None
        assert {n: k for n, k in self.local.items() if k} == {n: k for n, k in per.items() if k}, (self.local, per)
        for n, k in per.items():
            self.base[n] = self.base.get(n, 0) + k * times
        self.local, self.per = {}, {}


def build(nc, a):
    ctx = ExitStack()
    with ctx:
        def sb(name, shape):
            return ctx.enter_context(nc.sbuf_tensor(name, shape, F32))

        X = sb("residual", [P, DT, T2])
        HN = sb("normed", [P, DT, T2])
        RING = sb("weights", [P, SLOTS, D])
        AREA = sb("area", [P, 34688])
        V = sb("vectors", [P, N_VEC])
        CM = sb("matrices", [P, 5, P])
        R = sb("rstd", [P, T2])
        ps = ctx.enter_context(nc.psum_tensor("ps", [P, 8, 512], F32))
        IDENT, ONES, FLIP, NTRI, NONES = (CM[:, j] for j in range(5))

        def area(off, *shape):
            n = int(np.prod(shape))
            assert off + n <= 34688, (off, n)
            v = AREA[:, off:off + n]
            if len(shape) == 2:
                v = v.rearrange("p (a b) -> p a b", a=shape[0])
            if len(shape) == 3:
                v = v.rearrange("p (a b c) -> p a b c", a=shape[0], b=shape[1])
            return v

        CKV, KI = area(0, SEQ), area(512, SEQ)
        QA, QI = area(1024, PAIRS, SEQ), area(3072, PAIRS, SEQ)
        QB, KB = area(5120, PAIRS, SEQ), area(7168, PAIRS, SEQ)
        VB = area(9216, QT, SEQ)
        GATES = area(11264, 16, SEQ)
        KA, VA = area(19456, PAIRS, SEQ), area(21504, QT, SEQ)
        BIAS = area(23552, HEADS, SEQ)
        SCORE_OFF = [27648 + o for o in (0, 128, 384, 768)]
        SCORES = [area(o, P * (t + 1)) for t, o in enumerate(SCORE_OFF)]
        MASKS = [area(o + 1280, P * (t + 1)) for t, o in enumerate(SCORE_OFF)]
        TMP = 30208
        LG = [area(TMP, 512), area(TMP + 512, 512)]
        EX = [area(TMP + 1024, 512), area(TMP + 1536, 512)]
        PT = [area(TMP + 2048, 4, P), area(TMP + 2560, 4, P)]
        DG = [area(33280, P), area(33408, P)]
        ST1, ST2 = area(33536, 512), area(34048, 512)
        MERGED = area(7168, DT, SEQ)
        BIAS_FLIPPED = area(11264, HEADS, SEQ)
        SPT = [area(27648, 512), area(28160, 512)]
        SPP = [area(28672, 1280), area(29952, 1280)]
        SPA = [area(31232, 512), area(31744, 512)]
        ST3 = area(32256, 512)
        SMALL = sb("small", [P, 448])
        WIDX = area(19456, DT, 8)
        WROUT = area(0, DT, 36)
        SP_OFF = [0, 512, 896, 1152]
        HOT, RELB = area(27648, BIAS_W)[0:N_BUCKETS], area(28288, HEADS)[0:N_BUCKETS]
        BVEC = area(28928, BIAS_W)[0:HEADS]
        BR = area(288, QT, 36)
        LAM = sb("lambda", [P, 24])
        SG = [area(1024, 512), area(1536, 512)]
        HT = [area(2048, 512), area(2560, 512)]
        HID = [area(3072, 2, 512), area(4096, 2, 512)]
        CB = [area(5120, 512), area(5632, 512)]
        PX = area(6144, 2, SEQ)
        COMBT = area(7168, 512)

        N2 = T2
        PG, PREC = area(0, 4, N2), area(2112, 4, N2 + 3)
        PQ, PKV, KPE, KPW = area(4236, 2, N2), area(5292, N2), area(5820, N2), area(6348, N2)
        XC, RA, RX = area(6876, 4, N2), area(8988, 4, N2), area(11100, 4, N2)
        QN, QP, QW, KN = area(13212, 4, N2), area(15324, 4, N2), area(17436, 4, N2), area(19548, 4, N2)
        V2 = area(21660, 5, 512)
        Y2 = area(24220, 8, N2)
        GELU = area(26332, 4, N2)
        LRU_T = area(2112, 4, N2)
        MASKW, ROPE_C, ROPE_S = area(28444, N2), area(28972, N2), area(29500, N2)
        LG2 = [area(30028, N2), area(30556, N2)]
        EX2 = [area(31084, N2), area(31612, N2)]
        PT2 = [area(32140, 5, P), area(32780, 5, P)]
        DG2 = [area(33420, P), area(33548, P)]
        SQN, SQP, SKN, SV2 = area(6876, N2), area(7404, N2), area(7932, N2), area(8460, 5, P)
        FFH = area(0, 32, N2)
        RK, RV, RG = area(0, 8, N2), area(4224, 5, 2048), area(14464, 16, N2)
        SRK, SRV, RSC = area(22912, 2, N2), area(23968, 5, 512), area(26528, 1808)
        RSC_OFF = [0, 528, 1040, 1424, 1680]
        DECAY, COS, SIN = area(28336, 4, N2), area(30448, N2), area(30976, N2)
        ROT, RSQ = area(30448, 4, N2), area(32560, 4, N2)

        names = """x_in consts norm_sq norm_sum norm_var norm_sd norm_out ctr act_ops dve_ops pool_ops
            tile_done act_evac dve_evac chunk_begun rel_done rel_sb rel_used score_sum score_cut score_mask
            bias_vec bias_dram bias_rows bias_flip small_in logits smax expd diag tr pt o_done o_evac staged
            z_done soft sp sp_masked c_done a_raw a_masked merged flip_done
            route_done route_ev route_e comb_tr comb_ev comb_dram cb0 cb1 sg gu_done gu_evac hid dn_done dn_evac
            p_in meta_in out_done ln_cent ln_out c2_in c3_in hot_in bvec_out wr_in route_x lam_exp gelu_in gelu_th
            gelu_done lru_t pad_zero lru_x lru_r lru_done hidden ret_s ret_used ret_o ret_y""".split()
        S = {n: ctx.enter_context(nc.semaphore(n)) for n in names}
        chunk_full = [ctx.enter_context(nc.semaphore(f"chunk_full{s}")) for s in range(SLOTS)]
        bias_scratch = nc.dram_tensor("bias_scratch", (HEADS, BIAS_W), F32, kind="Internal")
        comb_scratch = nc.dram_tensor("comb_scratch", (EXPERTS, SEQ), F32, kind="Internal")

        B1 = slice(META, T2)
        XA, HA = X[:, :, B1], HN[:, :, B1]

        def vec(name, j=0):
            return V[:, VEC_AT[name] + j:VEC_AT[name] + j + 1]

        def halves(bank):
            return ps[:, bank:bank + 2, 0:HALF]

        def two(v):
            return v.rearrange("p (h c) -> p h c", h=2)

        block = ctx.enter_context(nc.Block())

        @block.sync
        def _(sp):
            w = Counts(sp)
            sp.dma_start(XA, a["x"]).then_inc(S["x_in"], 16)
            sp.dma_start(V[:], a["vecs"]).then_inc(S["consts"], 16)
            sp.dma_start(CM[:], a["mats"]).then_inc(S["consts"], 16)
            sp.dma_start(X[:, :, 0:META], a["meta"]).then_inc(S["meta_in"], 16)

            def load(slot, chunk):
                sp.dma_start(RING[:, slot:slot + 1, :],
                             a["weights"][chunk].rearrange("a p n -> p a n")).then_inc(chunk_full[slot], 16)

            for c in range(SLOTS):
                load(c, slice(c, c + 1))
            times = (N_CHUNKS - SLOTS) // SLOTS
            with sp.Fori(0, times) as i:
                for s in range(SLOTS):
                    sp.wait_ge(S["chunk_begun"], i * SLOTS + s + 2)
                    load(s, ds(i * SLOTS + s + SLOTS, 1))
            for c in range(SLOTS * (times + 1), N_CHUNKS):
                sp.wait_ge(S["chunk_begun"], c - SLOTS + 2)
                load(c % SLOTS, slice(c, c + 1))
            sp.wait_ge(S["ln_out"], 32)
            sp.dma_start(a["out"], X[:, :, B1]).then_inc(S["out_done"], 16)
            sp.wait_ge(S["out_done"], 16)

        @block.tensor
        def _(pe):
            w = Counts(pe)
            mm = nc.tensor.matmul
            chunk = {"base": 0, "local": 0, "i": None, "per": 0}

            @contextmanager
            def pe_loop(times, chunks, **per):
                assert chunks % SLOTS == 0
                chunk["base"] += chunk["local"]
                chunk["local"], chunk["per"] = 0, chunks
                with w.loop(times, **per) as i:
                    chunk["i"] = i
                    yield i
                assert chunk["local"] == chunks
                chunk["i"], chunk["local"] = None, 0
                chunk["base"] += chunks * times

            def take():
                n = chunk["base"] + chunk["local"]
                chunk["local"] += 1
                fill = n // SLOTS + 1
                if chunk["i"] is not None:
                    fill = chunk["i"] * (chunk["per"] // SLOTS) + fill
                pe.wait_ge(chunk_full[n % SLOTS], fill * 16)
                return RING[:, n % SLOTS, :].rearrange("p (k c) -> p k c", k=DT)

            def begun(ins):
                ins.then_inc(S["chunk_begun"], 1)

            stage = {"n": 0, "evac": "act_evac", "nb": 4}

            def begin_stage(evac, nb=4):
                if w.counted("act_evac"):
                    pe.wait_ge(S["act_evac"], w.value("act_evac"))
                if w.counted("dve_evac"):
                    pe.wait_ge(S["dve_evac"], w.value("dve_evac"))
                stage.update(n=0, evac=evac, nb=nb)

            def bank():
                n = stage["n"]
                stage["n"] += 1
                if n >= stage["nb"] or w.i is not None:
                    if w.counted(stage["evac"], stage["nb"] - 1):
                        pe.wait_ge(S[stage["evac"]], w.value(stage["evac"], stage["nb"] - 1))
                w.count(stage["evac"])
                return n % stage["nb"]

            def linear(rhs, wt):
                b = bank()
                for k in range(DT):
                    ins = mm(ps[:, b], wt[:, k], rhs(k), start=k == 0, stop=k == DT - 1)
                    if k == 0:
                        begun(ins)
                ins.then_inc(S["tile_done"], 1)

            def norm_sum(n, T, b, src, waited=False):
                for t in range(n):
                    if not waited:
                        pe.wait_ge(S["norm_sq"], w.next("norm_sq"))
                    parts = [(0, META, SEQ)] if T == SEQ else [(0, 0, HALF), (1, HALF, HALF)]
                    for h, c, width in parts:
                        ins = mm(ps[:, b + h, 0:width], ONES, src(t)[:, c:c + width], start=t == 0, stop=t == n - 1)
                ins.then_inc(S["norm_sum"], 1)

            def body():
                pe.wait_ge(S["consts"], 32)
                norm_sum(8, SEQ, 7, lambda t: HN[:, t])
                pe.wait_ge(S["norm_out"], w.next("norm_out", 8))
                hn = lambda k: HA[:, k]
                begin_stage("act_evac")
                for _ in range(6):
                    linear(hn, take())
                pe.wait_ge(S["small_in"], w.next("small_in", 16))
                w.count("dve_evac")
                b = 2
                if w.counted("act_evac", 3):
                    pe.wait_ge(S["act_evac"], w.value("act_evac", 3))
                for t in range(QT):
                    for k in range(DT):
                        ins = mm(ps[:, b, 8 * t:8 * t + 8], HA[:, k, P * t:P * t + P], WIDX[:, k],
                                 start=k == 0, stop=k == DT - 1)
                ins.then_inc(S["tile_done"], 1)
                pe.wait_ge(S["norm_sq"], w.next("norm_sq"))
                mm(ps[:, 7], ONES, R[:, 0:SEQ], start=True, stop=True).then_inc(S["norm_sum"], 1)
                pe.wait_ge(S["hot_in"], w.next("hot_in", 32))
                for j in range(2):
                    ins = mm(ps[0:HEADS, 6, 0:BIAS_W // 2] if j == 0 else ps[0:HEADS, 5, 0:BIAS_W // 2],
                             RELB, HOT[:, j * (BIAS_W // 2):(j + 1) * (BIAS_W // 2)], start=True, stop=True)
                ins.then_inc(S["bias_vec"], 1)
                if w.counted("act_evac"):
                    pe.wait_ge(S["act_evac"], w.value("act_evac"))
                for n, (t, h) in enumerate((t, h) for t in range(1, QT) for h in range(HEADS)):
                    if n == 0:
                        pe.wait_ge(S["bias_dram"], w.next("bias_dram", 1))
                    if n >= 2:
                        pe.wait_ge(S["rel_sb"], w.next("rel_sb"))
                    r = slice(HD * (h % 2), HD * (h % 2) + HD)
                    mm(ps[:, 4 + n % 2, 0:P * (t + 1)], QI[r, h // 2, P * t:P * t + P], KI[r, 0:P * (t + 1)],
                       start=True, stop=True).then_inc(S["rel_done"], 1)
                pe.wait_ge(S["rel_sb"], w.next("rel_sb", 2))
                pe.wait_ge(S["bias_rows"], w.next("bias_rows", 16))
                for h in range(HEADS):
                    if h >= 2:
                        pe.wait_ge(S["bias_flip"], w.next("bias_flip"))
                    mm(ps[:, 4 + h % 2], FLIP, BIAS_FLIPPED[:, h], start=True, stop=True).then_inc(S["flip_done"], 1)
                pe.wait_ge(S["bias_flip"], w.next("bias_flip", 2))
                begin_stage("act_evac")
                for _ in range(12):
                    linear(hn, take())
                for _ in range(4):
                    wt, b = take(), bank()
                    for t in range(QT):
                        for k in range(DT):
                            ins = mm(ps[:, b, P * t:P * t + P], HA[:, k, P * t:P * t + P], wt[:, k],
                                     start=k == 0, stop=k == DT - 1)
                            if t == k == 0:
                                begun(ins)
                    ins.then_inc(S["tile_done"], 1)
                stage["n"] = 0
                if w.counted("act_evac"):
                    pe.wait_ge(S["act_evac"], w.value("act_evac"))
                with pe_loop(2, 8, act_evac=8):
                    for _ in range(8):
                        linear(hn, take())
                pe.wait_ge(S["norm_out"], w.next("norm_out"))
                wt = take()
                for n in range(PAIRS):
                    ins = mm(ps[:, bank()], wt[:, n], CKV, start=True, stop=True)
                    ins.then_inc(S["tile_done"], 1)
                wv = wt[:, PAIRS:].rearrange("p k c -> p (k c)")
                for t in range(QT):
                    b = bank()
                    if t == 0:
                        begun(mm(ps[:, b, 0:256], CKV[:, 0:P], wv[:, 0:256], start=True, stop=True))
                        ins = mm(ps[:, b, 256:512], CKV[:, 0:P], wv[:, 256:512], start=True, stop=True)
                    else:
                        ins = mm(ps[:, b], CKV[:, P * t:P * t + P], wv, start=True, stop=True)
                    ins.then_inc(S["tile_done"], 1)
                if w.counted("act_evac"):
                    pe.wait_ge(S["act_evac"], w.value("act_evac"))
                pe_dsa()
                pe_stick()
                if w.counted("o_evac"):
                    pe.wait_ge(S["o_evac"], w.value("o_evac"))
                begin_stage("dve_evac", 4)
                for n in range(DT):
                    wt, b = take(), 2 * bank()
                    for k in range(PAIRS):
                        ins = mm(ps[:, b], wt[:, k], QA[:, k], start=k == 0, stop=k == PAIRS - 1)
                        if k == 0:
                            begun(ins)
                    for k in range(PAIRS):
                        ins = mm(ps[:, b + 1], wt[:, PAIRS + k], QB[:, k], start=k == 0, stop=k == PAIRS - 1)
                    ins.then_inc(S["tile_done"], 1)
                pe.wait_ge(S["merged"], w.next("merged", DT))
                begin_stage("dve_evac")
                for _ in range(DT):
                    linear(lambda k: MERGED[:, k], take())
                begin_stage("dve_evac")
                norm_sum(8, SEQ, 7, lambda t: HN[:, t])
                pe.wait_ge(S["norm_out"], w.next("norm_out", 8))
                pe.wait_ge(S["wr_in"], w.next("wr_in", 32))
                for t in range(QT):
                    for k in range(DT):
                        ins = mm(ps[:, 6, 36 * t:36 * t + 36], HA[:, k, P * t:P * t + P], WROUT[:, k],
                                 start=k == 0, stop=k == DT - 1)
                ins.then_inc(S["route_done"], 1)
                pe.wait_ge(S["route_ev"], w.next("route_ev"))
                for t in range(QT):
                    ins = mm(ps[0:EXPERTS, 6, P * t:P * t + P], SMALL[:, 288 + 32 * t:288 + 32 * t + 32], IDENT,
                             is_transpose=True, start=True, stop=True)
                ins.then_inc(S["comb_tr"], 1)
                pe.wait_ge(S["comb_ev"], w.next("comb_ev"))
                pe_moe()
                norm_sum(8, SEQ, 7, lambda t: HN[:, t])
                pe.wait_ge(S["norm_out"], w.next("norm_out", 8))
                pe.wait_ge(S["p_in"], w.next("p_in", 16))
                begin_stage("dve_evac", 4)
                for g in range(2):
                    wp = take()
                    for n in range(4):
                        b = bank()
                        for k in range(2):
                            ins = mm(ps[:, b], wp[:, 2 * n + k], PX[:, k], start=k == 0, stop=k == 1)
                            if n == k == 0:
                                begun(ins)
                    for n in range(4):
                        wt = take()
                        for k in range(DT):
                            ins = mm(ps[:, 4 + n], wt[:, k], HA[:, k], start=k == 0, stop=k == DT - 1)
                            if k == 0:
                                begun(ins)
                        ins.then_inc(S["tile_done"], 1)
                begin_stage("dve_evac")
                norm_sum(8, SEQ, 7, lambda t: HN[:, t])
                pe.wait_ge(S["norm_out"], w.next("norm_out", 8))
                pe.wait_ge(S["meta_in"], w.next("meta_in", 16))
                begin_stage("act_evac")
                xk = lambda k: X[:, k]
                for _ in range(13):
                    linear2([take()], xk, DT)
                wt = take()
                for n in range(8):
                    if n < 4:
                        pe.wait_ge(S["lru_x"], w.next("lru_x"))
                    b = 2 * bank()
                    for h in range(2):
                        ins = mm(ps[:, b + h, 0:HALF], wt[:, n], XC[:, n % 4, HALF * h:HALF * h + HALF], start=True, stop=True)
                        if n == h == 0:
                            begun(ins)
                    ins.then_inc(S["tile_done"], 1)
                begin_stage("act_evac", 3)
                norm_sum(2, T2, 6, lambda t: R2(t))
                norm_sum(1, T2, 6, lambda t: R2(t))
                pe.wait_ge(S["norm_out"], w.next("norm_out", 3))
                for c in range(3):
                    wt = take()
                    for n in range(4):
                        b = 2 * bank()
                        for k in range(2):
                            for h in range(2):
                                ins = mm(ps[:, b + h, 0:HALF], wt[:, 2 * n + k], PQ[:, k, HALF * h:HALF * h + HALF],
                                         start=k == 0, stop=k == 1)
                                if n == k == h == 0:
                                    begun(ins)
                        ins.then_inc(S["tile_done"], 1)
                wt = take()
                for n in range(4):
                    b = 2 * bank()
                    for h in range(2):
                        ins = mm(ps[:, b + h, 0:HALF], wt[:, n], PKV[:, HALF * h:HALF * h + HALF], start=True, stop=True)
                        if n == h == 0:
                            begun(ins)
                    ins.then_inc(S["tile_done"], 1)
                wv = wt[:, 4:].rearrange("p k c -> p (k c)")
                for c, width in TOK2:
                    ins = mm(ps[0:width, 2 * bank()], PKV[:, c:c + width], wv, start=True, stop=True)
                    ins.then_inc(S["tile_done"], 1)
                begin_stage("act_evac")
                pe_mla()
                pe.wait_ge(S["lru_done"], w.next("lru_done", 4))
                begin_stage("dve_evac")
                for _ in range(8):
                    linear2([take()], lambda k: Y2[:, k], DT)
                layer_norm()
                pe_mlp()
                layer_norm()
                begin_stage("act_evac")
                for _ in range(16):
                    linear2([take()], xk, DT)
                begin_stage("act_evac")
                with pe_loop(2, 8, act_evac=8):
                    for _ in range(8):
                        wt, b = take(), 2 * bank()
                        for j, (c, width) in enumerate(TOK2):
                            o = ps[0:META, b + 1, 0:P] if j == 0 else ps[:, b, P * (j - 1):P * j]
                            for k in range(DT):
                                ins = mm(o, X[:, k, c:c + width], wt[:, k], start=k == 0, stop=k == DT - 1)
                                if j == k == 0:
                                    begun(ins)
                        ins.then_inc(S["tile_done"], 1)
                begin_stage("act_evac")
                with pe_loop(2, 8, act_evac=8):
                    for _ in range(8):
                        linear2([take()], xk, DT)
                begin_stage("act_evac")
                pe_retention()
                begin_stage("dve_evac")
                with pe_loop(2, 8, dve_evac=4):
                    for _ in range(4):
                        linear2([take, take], lambda k: RG[:, k], DT)
                layer_norm()
                pe_mlp()
                layer_norm()

            def R2(t):
                return GELU[:, t]

            def linear2(chunks, rhs, kts):
                b = 2 * bank()
                for m, wt in enumerate(chunks):
                    if callable(wt):
                        wt = wt()
                    for k in range(kts):
                        for h in range(2):
                            ins = mm(ps[:, b + h, 0:HALF], wt[:, k], rhs(m * DT + k)[:, HALF * h:HALF * h + HALF],
                                     start=m == k == 0, stop=m == len(chunks) - 1 and k == kts - 1)
                            if k == h == 0:
                                begun(ins)
                ins.then_inc(S["tile_done"], 1)

            def layer_norm():
                begin_stage("dve_evac")
                for t in range(DT):
                    for h in range(2):
                        ins = mm(ps[:, 6 + h, 0:HALF], ONES, X[:, t, HALF * h:HALF * h + HALF], start=t == 0, stop=t == DT - 1)
                ins.then_inc(S["norm_sum"], 1)
                norm_sum(8, T2, 6, lambda t: X[:, t])
                pe.wait_ge(S["ln_out"], w.next("ln_out", 8))

            def pe_mlp():
                begin_stage("act_evac")
                with pe_loop(4, 8, act_evac=8):
                    for _ in range(8):
                        linear2([take()], lambda k: X[:, k], DT)
                begin_stage("dve_evac", 2)
                pe.wait_ge(S["hidden"], w.next("hidden", 32))
                with pe_loop(4, 8, dve_evac=2):
                    for _ in range(2):
                        linear2([take] * 4, lambda k: FFH[:, k], DT)

            def pe_mla():
                units = [(h, t) for h in range(2) for t in range(5)]
                flat = ps[:, :, :].rearrange("p b c -> p (b c)")
                with w.loop(PAIRS, staged=4, smax=10, diag=10, pt=10, o_evac=1):
                    def logits(u):
                        h, t = units[u]
                        c, width = TOK2[t]
                        keys = c + width
                        r = slice(HD * h, HD * h + HD)
                        if u >= 2:
                            pe.wait_ge(S["smax"], w.next("smax"))
                            if t == 0:
                                pe.nop(nofuse=True)
                        for lo, hi in ((0, min(keys, 512)), (512, keys)):
                            if hi <= lo:
                                continue
                            o = flat[0:width, 1024 * (u % 2) + lo:1024 * (u % 2) + hi]
                            mm(o, SQN[r, c:c + width], SKN[r, lo:hi], start=True, stop=False)
                            ins = mm(o, SQP[r, c:c + width], KPE[r, lo:hi], start=False, stop=True)
                        ins.then_inc(S["logits"], 1)

                    def transposed(u):
                        h, t = units[u]
                        width = TOK2[t][1]
                        pe.wait_ge(S["diag"], w.next("diag"))
                        if t == 0:
                            pe.nop(nofuse=True)
                        for j, (kc, kw) in enumerate(TOK2[:t + 1]):
                            o = ps[0:META, 5, 0:width] if j == 0 else ps[:, 4, P * (j - 1):P * j]
                            ins = mm(o, EX2[u % 2][0:width, kc:kc + kw], DG2[u % 2][0:width, 0:width], start=True, stop=True)
                        ins.then_inc(S["tr"], 1)

                    def values(u):
                        h, t = units[u]
                        c, width = TOK2[t]
                        pe.wait_ge(S["pt"], w.next("pt"))
                        r = slice(HD * h, HD * h + HD)
                        o = ps[r, 7, 0:META] if t == 0 else ps[r, 6, P * (t - 1):P * t]
                        for j, (kc, kw) in enumerate(TOK2[:t + 1]):
                            ins = mm(o, SV2[0:kw, j, HD * h:HD * h + HD], PT2[u % 2][0:kw, j, 0:width],
                                     start=j == 0, stop=j == t)
                        return ins

                    pe.wait_ge(S["staged"], w.next("staged", 4))
                    pe.nop(nofuse=True)
                    logits(0)
                    for u in range(10):
                        if u < 9:
                            logits(u + 1)
                        if u:
                            values(u - 1)
                        transposed(u)
                    pe.wait_ge(S["smax"], w.next("smax", 2))
                    values(9).then_inc(S["o_done"], 1)
                    pe.wait_ge(S["o_evac"], w.next("o_evac"))

            def pe_retention():
                flat = ps[:, :, :].rearrange("p b c -> p (b c)")
                with w.loop(RET_HEADS, staged=2, ret_s=5, ret_used=4, ret_y=1) as i:
                    pe.wait_ge(S["staged"], w.next("staged", 2))
                    for j, (c, kw) in enumerate(TOK2):
                        if j >= 2:
                            pe.wait_ge(S["ret_s"], w.next("ret_s"))
                        for lo, hi in ((0, min(T2 - c, 512)), (512, T2 - c)):
                            if hi <= lo:
                                continue
                            o = flat[0:kw, 1024 * (j % 2) + lo:1024 * (j % 2) + hi].rearrange("p (a c) -> p a c", a=1)
                            for k in range(2):
                                ins = mm(o, SRK[:, k, c:c + kw], HN[:, ds(i * 2 + k, 1), c + lo:c + hi], start=k == 0, stop=k == 1)
                        ins.then_inc(S["logits"], 1)
                    pe.wait_ge(S["ret_s"], w.next("ret_s", 2))
                    for v in range(4):
                        if v >= 2:
                            pe.wait_ge(S["ret_used"], w.next("ret_used"))
                        for h in range(2):
                            for j, (c, kw) in enumerate(TOK2):
                                lo, hi = max(c, HALF * h), HALF * (h + 1)
                                if lo >= hi:
                                    continue
                                ins = mm(ps[:, 4 + 2 * (v % 2) + h, lo - HALF * h:HALF], SRV[0:kw, j, P * v:P * v + P],
                                         RSC[0:kw, RSC_OFF[j] + lo - c:RSC_OFF[j] + hi - c],
                                         start=j == 0, stop=True, skip_group_check=True)
                        ins.then_inc(S["ret_o"], 1)
                    pe.wait_ge(S["ret_used"], w.next("ret_used", 2))
                    norm_sum(4, T2, 0, lambda t: RSQ[:, t], waited=True)
                    pe.wait_ge(S["ret_y"], w.next("ret_y"))

            def pe_dsa():
                units = [(h, t) for h in range(2) for t in range(QT)]
                with w.loop(PAIRS, staged=3, smax=8, diag=8, pt=8, o_evac=1):
                    def logits(u):
                        h, t = units[u]
                        r = slice(HD * h, HD * h + HD)
                        if u >= 2:
                            pe.wait_ge(S["smax"], w.next("smax"))
                        mm(ps[:, u % 2, 0:P * (t + 1)], ST1[r, P * t:P * t + P], ST2[r, 0:P * (t + 1)],
                           start=True, stop=True).then_inc(S["logits"], 1)

                    def transposed(u):
                        h, t = units[u]
                        pe.wait_ge(S["diag"], w.next("diag"))
                        for k in range(t + 1):
                            ins = mm(ps[:, 2 + u % 2, P * k:P * k + P], EX[u % 2][:, P * k:P * k + P], DG[u % 2],
                                     start=True, stop=True)
                        ins.then_inc(S["tr"], 1)

                    def values(u):
                        h, t = units[u]
                        pe.wait_ge(S["pt"], w.next("pt"))
                        for k in range(t + 1):
                            ins = mm(ps[HD * h:HD * h + HD, 4, P * t:P * t + P],
                                     KI[:, P * k + HD * h:P * k + HD * h + HD], PT[u % 2][:, k],
                                     start=k == 0, stop=k == t)
                        return ins

                    pe.wait_ge(S["staged"], w.next("staged", 3))
                    logits(0)
                    for u in range(8):
                        if u < 7:
                            logits(u + 1)
                        transposed(u)
                        if u:
                            values(u - 1)
                    pe.wait_ge(S["smax"], w.next("smax", 2))
                    values(7).then_inc(S["o_done"], 1)
                    pe.wait_ge(S["o_evac"], w.next("o_evac"))

            def pe_stick():
                units = [(h, t) for h in range(2) for t in reversed(range(QT))]
                with w.loop(PAIRS, staged=3, sp_masked=8, a_masked=8, a_raw=8, o_evac=1):
                    def width(t):
                        return SEQ - P * t

                    def z(u):
                        h, t = units[u]
                        r = slice(HD * h, HD * h + HD)
                        if u >= 6:
                            pe.wait_ge(S["a_raw"], w.next("a_raw"))
                        mm(ps[:, u % 6, 0:width(t)], ST2[r, P * t:P * t + P], ST1[r, P * t:SEQ],
                           start=True, stop=True).then_inc(S["z_done"], 1)

                    def after(u):
                        h, t = units[u]
                        pe.wait_ge(S["sp_masked"], w.next("sp_masked"))
                        for t2 in range(QT - 1, t - 1, -1):
                            o = SP_OFF[t2]
                            ins = mm(ps[:, u % 6, P * (t2 - t):width(t)], NTRI if t2 == t else NONES,
                                     SPP[h][:, o:o + width(t2)], start=False, stop=True, skip_group_check=True)
                        ins.then_inc(S["c_done"], 1)

                    def values(u):
                        h, t = units[u]
                        pe.wait_ge(S["a_masked"], w.next("a_masked"))
                        return mm(ps[HD * h:HD * h + HD, 6, P * t:SEQ], ST3[:, P * t + HD * h:P * t + HD * h + HD],
                                  SPA[u % 2][:, 0:width(t)], start=t == QT - 1, stop=True, skip_group_check=True)

                    pe.wait_ge(S["staged"], w.next("staged", 3))
                    for u in range(4):
                        z(u)
                    for u in range(8):
                        if u + 4 < 8:
                            z(u + 4)
                        after(u)
                        if u:
                            values(u - 1)
                    values(7).then_inc(S["o_done"], 1)
                    pe.wait_ge(S["a_raw"], w.next("a_raw", 6))
                    pe.wait_ge(S["o_evac"], w.next("o_evac"))

            def pe_moe():
                def gate_up(first=False):
                    for f in range(2):
                        for g in range(2):
                            if not first and g == 0:
                                pe.wait_ge(S["gu_evac"], w.next("gu_evac"))
                            wt = take()
                            for k in range(DT):
                                ins = mm(ps[:, 2 * f + g], wt[:, k], HA[:, k], start=k == 0, stop=k == DT - 1)
                                if k == 0:
                                    begun(ins)
                            ins.then_inc(S["gu_done"], 1)

                def down(e, first=False):
                    pe.wait_ge(S["hid"], w.next("hid", 2))
                    for n in range(DT):
                        if n % 4 == 0:
                            wt = take()
                        if not (first and n < 4):
                            pe.wait_ge(S["dn_evac"], w.next("dn_evac"))
                        for k in range(2):
                            ins = mm(ps[:, 4 + n % 4], wt[:, 2 * (n % 4) + k], HID[e % 2][:, k], start=k == 0, stop=k == 1)
                            if n % 4 == 0 and k == 0:
                                begun(ins)
                        ins.then_inc(S["dn_done"], 1)

                w.count("gu_evac", 0)
                gate_up(first=True)
                for e in range(4):
                    gate_up()
                    down(e, first=e == 0)
                with pe_loop(6, 24, gu_evac=8, hid=8, dn_evac=32):
                    for e in range(4):
                        gate_up()
                        down(e)
                for e in range(4):
                    if e < 3:
                        gate_up()
                    down(e)
                pe.wait_ge(S["gu_evac"], w.next("gu_evac", 2))
                pe.wait_ge(S["dn_evac"], w.next("dn_evac", 4))

            body()

        @block.scalar
        def _(act):
            w = Counts(act)
            fn = nc.scalar.activation

            def step(ins):
                ins.then_inc(S["act_ops"], 1)
                act.wait_ge(S["act_ops"], w.next("act_ops"))

            def squares(n, src, dst):
                for t in range(n):
                    fn(dst(t), src(t), ACT.Square).then_inc(S["norm_sq"], 1)

            def deviation(v):
                act.wait_ge(S["norm_var"], w.next("norm_var"))
                fn(v, v, ACT.Sqrt).then_inc(S["norm_sd"], 1)

            def evac(out, in_, f=ACT.Copy, **kw):
                act.wait_ge(S["tile_done"], w.next("tile_done"))
                fn(out, in_, f, **kw).then_inc(S["act_evac"], 1)

            def bank(n, nb=4):
                return ps[:, n % nb]

            def body():
                R1 = R[:, 0:SEQ]
                act.wait_ge(S["x_in"], 16)
                act.wait_ge(S["consts"], 32)
                step(fn(LAM[:, 0:4], V[:, VEC_AT["lam"]:VEC_AT["lam"] + 4], ACT.Abs))
                fn(LAM[:, 0:4], LAM[:, 0:4], ACT.Exp, scale=-1.0).then_inc(S["lam_exp"], 1)
                squares(8, lambda t: XA[:, t], lambda t: HA[:, t])
                deviation(R1)
                for n, out in enumerate([CKV, KI] + [QI[:, j] for j in range(4)]):
                    evac(out, bank(n))
                if w.counted("tile_done"):
                    act.wait_ge(S["tile_done"], w.value("tile_done"))
                w.count("tile_done")
                squares(1, lambda t: CKV, lambda t: R1)
                deviation(R1)
                act.wait_ge(S["bias_vec"], w.next("bias_vec"))
                fn(BVEC[:, 0:BIAS_W // 2], ps[0:HEADS, 6, 0:BIAS_W // 2], ACT.Copy)
                fn(BVEC[:, BIAS_W // 2:], ps[0:HEADS, 5, 0:BIAS_W // 2], ACT.Copy).then_inc(S["bias_dram"], 1)
                for n, (t, h) in enumerate((t, h) for t in range(1, QT) for h in range(HEADS)):
                    act.wait_ge(S["rel_done"], w.next("rel_done"))
                    if n >= 2:
                        act.wait_ge(S["rel_used"], w.next("rel_used"))
                    fn(LG[n % 2][:, 0:P * (t + 1)], ps[:, 4 + n % 2, 0:P * (t + 1)], ACT.Relu).then_inc(S["rel_sb"], 1)
                w.count("rel_used", 2)
                for h in range(HEADS):
                    act.wait_ge(S["flip_done"], w.next("flip_done"))
                    fn(BIAS[:, h], ps[:, 4 + h % 2], ACT.Copy).then_inc(S["bias_flip"], 1)
                n = 0
                for j in range(4):
                    evac(QA[:, j], bank(n + j), scale=QK_SCALE)
                for j in range(4):
                    evac(QB[:, j], bank(n + 4 + j), scale=QK_SCALE)
                for j in range(4):
                    evac(KB[:, j], bank(n + 8 + j))
                for j in range(4):
                    evac(VB[:, :, P * j:P * j + P], bank(n + 12 + j).rearrange("p (t c) -> p t c", t=QT))
                with w.loop(2, tile_done=8) as i:
                    for j in range(8):
                        evac(GATES[:, ds(i * 8 + j, 1), :], ps[:, j % 4:j % 4 + 1], ACT.Sigmoid)
                for j in range(PAIRS):
                    evac(KA[:, j], bank(j))
                for t in range(QT):
                    evac(VA[:, t], bank(t))
                softmax_pairs(PAIRS, [t for _ in range(2) for t in range(QT)], [(P * (t + 1), P) for t in range(QT)],
                              LG, EX, 1.0, copy_first)
                act_stick()
                w.count("tile_done", 16)
                act.wait_ge(S["dve_evac"], w.next("dve_evac", 1 + 16))
                squares(8, lambda t: XA[:, t], lambda t: HA[:, t])
                deviation(R1)
                for _ in range(2):
                    act.wait_ge(S["route_e"], w.next("route_e"))
                    src = SMALL[:, 176:192] if _ == 0 else SMALL[:, 200:204]
                    fn(src, src, ACT.Exp).then_inc(S["route_x"], 1)
                act.wait_ge(S["comb_tr"], w.next("comb_tr"))
                fn(COMBT[0:EXPERTS], ps[0:EXPERTS, 6], ACT.Copy).then_inc(S["comb_ev"], 1)

                def silu_parts(ring_full):
                    for f in range(2):
                        if ring_full:
                            act.wait_ge(S["gu_evac"], w.next("gu_evac"))
                        act.wait_ge(S["gu_done"], w.next("gu_done"))
                        fn(SG[f], ps[:, 2 * f], ACT.Sigmoid).then_inc(S["sg"], 1)
                        act.wait_ge(S["gu_done"], w.next("gu_done"))

                silu_parts(False)
                for _ in range(3):
                    silu_parts(True)
                with w.loop(7, gu_evac=8, gu_done=16):
                    for _ in range(4):
                        silu_parts(True)
                w.count("gu_evac", 2)
                act.wait_ge(S["dn_evac"], w.next("dn_evac", 8 * EXPERTS))
                squares(8, lambda t: XA[:, t], lambda t: HA[:, t])
                deviation(R1)
                for n in range(8):
                    act.wait_ge(S["tile_done"], w.next("tile_done"))
                    fn(SG2[n % 2], ps[:, 4 + n % 4], ACT.Sigmoid).then_inc(S["sg"], 1)
                    if n >= 1:
                        act.wait_ge(S["dve_evac"], w.next("dve_evac"))
                act.wait_ge(S["dve_evac"], w.next("dve_evac"))
                squares(8, lambda t: XA[:, t], lambda t: HA[:, t])
                deviation(R1)
                ev = [PG[:, j] for j in range(4)] + [PREC[:, j, 3:] for j in range(4)] + [PQ[:, j] for j in range(2)] + [PKV, KPE, KPW]
                act.wait_ge(S["norm_out"], w.next("norm_out", 8 + 1 + 24))
                for n, out in enumerate(ev):
                    evac(two(out), halves(2 * (n % 4)))
                for n in range(8):
                    out, bias = (RA, "b_rg_a") if n < 4 else (RX, "b_rg_x")
                    evac(two(out[:, n % 4]), halves(2 * ((n + 13) % 4)), ACT.Sigmoid, bias=vec(bias, n % 4))
                act_lru()
                squares(2, lambda t: PQ[:, t], lambda t: GELU[:, t])
                deviation(R[:, :])
                act.wait_ge(S["norm_out"], w.next("norm_out", 2))
                squares(1, lambda t: PKV, lambda t: GELU[:, t])
                deviation(R[:, :])
                act.wait_ge(S["norm_out"], w.next("norm_out", 1))
                for n, out in enumerate([QN[:, j] for j in range(4)] + [QP[:, j] for j in range(4)] + [QW[:, j] for j in range(4)]
                                        + [KN[:, j] for j in range(4)]):
                    evac(two(out), halves(2 * (n % 3)))
                for j, (c, width) in enumerate(TOK2):
                    evac(V2[0:width, j], ps[0:width, 2 * ((16 + j) % 3)])
                softmax_pairs(PAIRS, [t for _ in range(2) for t in range(5)], [(c + width, width) for c, width in TOK2],
                              LG2, EX2, MLA_SCALE, copy_second)
                w.count("tile_done", 8)
                act.wait_ge(S["dve_evac"], w.next("dve_evac", 8))
                layer_norm("mix", 0)
                mlp(0)
                for n in range(8):
                    evac(two(HN[:, n]), halves(2 * (n % 4)))
                for n in range(8):
                    evac(two(RK[:, n]), halves(2 * (n % 4)), scale=1.0 / 16)
                with w.loop(2, tile_done=8) as i:
                    for n in range(8):
                        act.wait_ge(S["tile_done"], w.next("tile_done"))
                        b = 2 * (n % 4)
                        fn(RV[:, 1:5, ds(i * 1024 + P * n, P)], ps[:, b].rearrange("p (t c) -> p t c", t=4), ACT.Copy)
                        fn(RV[0:META, 0, ds(i * 1024 + P * n, P)], ps[0:META, b + 1, 0:P], ACT.Copy).then_inc(S["act_evac"], 1)
                with w.loop(2, tile_done=8) as i:
                    for n in range(8):
                        act.wait_ge(S["tile_done"], w.next("tile_done"))
                        b = 2 * (n % 4)
                        fn(RG[:, ds(i * 8 + n, 1), :].rearrange("p a (h c) -> p (a h) c", h=2), halves(b), ACT.Silu).then_inc(S["act_evac"], 1)
                with w.loop(RET_HEADS, ret_o=4, norm_var=1, ret_y=1):
                    for v in range(4):
                        act.wait_ge(S["ret_o"], w.next("ret_o"))
                        b = 4 + 2 * (v % 2)
                        fn(two(ROT[:, v]), halves(b), ACT.Copy)
                        fn(two(RSQ[:, v]), halves(b), ACT.Square).then_inc(S["ret_used"], 1)
                    deviation(R[:, :])
                    act.wait_ge(S["ret_y"], w.next("ret_y"))
                w.count("tile_done", 8)
                act.wait_ge(S["dve_evac"], w.next("dve_evac", 8))
                layer_norm("mix", 1)
                mlp(1)

            def copy_first(u, t):
                fn(PT[u % 2][:, 0:t + 1], ps[:, 2 + u % 2, 0:P * (t + 1)].rearrange("p (k c) -> p k c", k=t + 1),
                   ACT.Copy).then_inc(S["pt"], 1)

            def copy_second(u, t):
                width = TOK2[t][1]
                ins = fn(PT2[u % 2][0:META, 0, 0:width], ps[0:META, 5, 0:width], ACT.Copy)
                if t:
                    ins = fn(PT2[u % 2][:, 1:t + 1], ps[:, 4, 0:P * t].rearrange("p (k c) -> p k c", k=t), ACT.Copy)
                ins.then_inc(S["pt"], 1)

            def softmax_pairs(pairs, order, sizes, lg, ex, scale, copy):
                n = len(order)
                with w.loop(pairs, smax=n, tr=n, act_ops=n, o_done=1) as i:
                    def exponentials(u):
                        keys, rows = sizes[order[u]]
                        act.wait_ge(S["smax"], w.next("smax"))
                        st = SMALL[0:rows, 8 * (u % 2):8 * (u % 2) + 8]
                        step(nc.scalar.mul(st[:, 1:2], st[:, 0:1], -scale))
                        fn(ex[u % 2][0:rows, 0:keys], lg[u % 2][0:rows, 0:keys], ACT.Exp, bias=st[:, 1:2], scale=scale,
                           accum_out=st[:, 2:3]).then_inc(S["expd"], 1)

                    exponentials(0)
                    for u in range(n):
                        if u + 1 < n:
                            exponentials(u + 1)
                        act.wait_ge(S["tr"], w.next("tr"))
                        copy(u, order[u])
                    act.wait_ge(S["o_done"], w.next("o_done"))
                    if copy is copy_first:
                        fn(QA[:, ds(i, 1), :], ps[:, 4:5], ACT.Copy).then_inc(S["o_evac"], 1)
                    else:
                        fn(Y2[:, ds(i + 4, 1), META:], ps[:, 6:7], ACT.Copy)
                        fn(Y2[:, ds(i + 4, 1), 0:META], ps[:, 7:8, 0:META], ACT.Copy).then_inc(S["o_evac"], 1)

            def act_stick():
                units = [(h, t) for h in range(2) for t in reversed(range(QT))]
                with w.loop(PAIRS, z_done=8, act_ops=16, sp=8, c_done=8, o_done=1) as i:
                    def soft(u):
                        h, t = units[u]
                        m = SPT[u % 2][:, 0:SEQ - P * t]
                        act.wait_ge(S["z_done"], w.next("z_done"))
                        if u >= 2:
                            act.wait_ge(S["sp"], w.next("sp"))
                        step(fn(m, ps[:, u % 6, 0:SEQ - P * t], ACT.Abs))
                        step(fn(m, m, ACT.Exp, scale=-1.0))
                        fn(m, m, ACT.Ln, bias=1.0).then_inc(S["soft"], 1)

                    def weights(u):
                        h, t = units[u]
                        act.wait_ge(S["c_done"], w.next("c_done"))
                        fn(SPA[u % 2][:, 0:SEQ - P * t], ps[:, u % 6, 0:SEQ - P * t], ACT.Exp).then_inc(S["a_raw"], 1)

                    soft(0)
                    soft(1)
                    for u in range(8):
                        if u + 2 < 8:
                            soft(u + 2)
                        weights(u)
                    act.wait_ge(S["sp"], w.next("sp", 2))
                    act.wait_ge(S["o_done"], w.next("o_done"))
                    fn(QB[:, ds(i, 1), :], ps[:, 6:7], ACT.Copy).then_inc(S["o_evac"], 1)

            def act_lru():
                for j in range(4):
                    act.wait_ge(S["lru_r"], w.next("lru_r"))
                    fn(LRU_T[:, j], RA[:, j], ACT.Tanh)
                    fn(RA[:, j], RA[:, j], ACT.Exp, scale=-1.0).then_inc(S["lru_t"], 1)
                for j in range(4):
                    act.wait_ge(S["gelu_in"], w.next("gelu_in"))
                    fn(GELU[:, j], GELU[:, j], ACT.Tanh, scale=math.sqrt(2 / math.pi)).then_inc(S["gelu_th"], 1)
                for j in range(4):
                    act.wait_ge(S["lru_r"], w.next("lru_r"))
                    fn(LRU_T[:, j], LRU_T[:, j], ACT.Sqrt).then_inc(S["lru_t"], 1)
                act.wait_ge(S["lru_done"], w.next("lru_done", 4))

            def layer_norm(kind, l):
                for t in range(DT):
                    act.wait_ge(S["ln_cent"], w.next("ln_cent"))
                    fn(X[:, t], HN[:, t], ACT.Square).then_inc(S["norm_sq"], 1)
                deviation(R[:, :])
                for t in range(DT):
                    act.wait_ge(S["norm_out"], w.next("norm_out"))
                    fn(X[:, t], HN[:, t], ACT.Identity, bias=vec(f"ln_{kind}_b", 8 * l + t)).then_inc(S["ln_out"], 1)

            def mlp(l):
                with w.loop(4, tile_done=8) as i:
                    for n in range(8):
                        act.wait_ge(S["tile_done"], w.next("tile_done"))
                        fn(FFH[:, ds(i * 8 + n, 1), :].rearrange("p a (h c) -> p (a h) c", h=2), halves(2 * (n % 4)),
                           ACT.Relu).then_inc(S["act_evac"], 1)
                w.count("tile_done", 8)
                act.wait_ge(S["dve_evac"], w.next("dve_evac", 8))
                layer_norm("mlp", l)

            SG2 = [area(1024, 512), area(1536, 512)]
            body()

        @block.vector
        def _(dve):
            w = Counts(dve)
            v = nc.vector

            def step(ins):
                ins.then_inc(S["dve_ops"], 1)
                dve.wait_ge(S["dve_ops"], w.next("dve_ops"))

            def bc(x, *shape):
                return x.unsqueeze(2).to_broadcast([P, *shape])

            def inverse_deviation(T, dim, eps, b):
                pv, rv = (ps[:, 7], R[:, 0:SEQ]) if T == SEQ else (halves(6), two(R[:, :]))
                dve.wait_ge(S["norm_sum"], w.next("norm_sum"))
                v.tensor_scalar(rv, pv, 1.0 / dim, eps, ALU.mult, ALU.add).then_inc(S["norm_var"], 1)
                dve.wait_ge(S["norm_sd"], w.next("norm_sd"))
                step(v.reciprocal(R[:, 0:T], R[:, 0:T]))

            def rms(n, T, dim, eps, gain, src, dst):
                inverse_deviation(T, dim, eps, 7)
                for t in range(n):
                    v.scalar_tensor_tensor(out=dst(t), in0=src(t), scalar=vec(gain, t), in1=R[:, 0:T],
                                           op0=ALU.mult, op1=ALU.mult).then_inc(S["norm_out"], 1)

            def accumulate(out, in_, scale):
                if scale == 1.0:
                    ins = v.tensor_tensor(out, out, in_, ALU.add)
                else:
                    ins = v.scalar_tensor_tensor(out=out, in0=out, scalar=scale, in1=in_, op0=ALU.mult, op1=ALU.add)
                ins.then_inc(S["dve_evac"], 1)

            def layer_norm(kind, l):
                dve.wait_ge(S["norm_sum"], w.next("norm_sum"))
                step(v.tensor_scalar(two(R[:, :]), halves(6), 1.0 / D, None, ALU.mult))
                for t in range(DT):
                    v.tensor_tensor(HN[:, t], X[:, t], R[:, :], ALU.subtract).then_inc(S["ln_cent"], 1)
                inverse_deviation(T2, D, EPS2, 6)
                for t in range(DT):
                    v.scalar_tensor_tensor(out=HN[:, t], in0=HN[:, t], scalar=vec(f"ln_{kind}_g", 8 * l + t), in1=R[:, :],
                                           op0=ALU.mult, op1=ALU.mult).then_inc(S["norm_out"], 1)

            def body():
                dve.wait_ge(S["consts"], 32)
                rms(8, SEQ, D, EPS1, "attn_norm", lambda t: XA[:, t], lambda t: HA[:, t])
                w.count("tile_done", 6)
                dve.wait_ge(S["tile_done"], w.next("tile_done"))
                v.tensor_scalar(WI, ps[:, 2, 0:32], IDX_SCALE, None, ALU.mult).then_inc(S["dve_evac"], 1)
                dve.wait_ge(S["dve_evac"], w.next("dve_evac"))
                rms(1, SEQ, KV_RANK, EPS1, "kv_norm", lambda t: CKV, lambda t: CKV)
                for t in range(1, QT):
                    for h in range(HEADS):
                        dve.wait_ge(S["rel_sb"], w.next("rel_sb"))
                        rel, scalar = LG[((t - 1) * HEADS + h) % 2][:, 0:P * (t + 1)], WI[:, 8 * t + h:8 * t + h + 1]
                        if h == 0:
                            ins = v.tensor_scalar(SCORES[t], rel, scalar, None, ALU.mult)
                        else:
                            ins = v.scalar_tensor_tensor(out=SCORES[t], in0=rel, scalar=scalar, in1=SCORES[t],
                                                         op0=ALU.mult, op1=ALU.add)
                        ins.then_inc(S["rel_used"], 1)
                        dve.wait_ge(S["rel_used"], w.next("rel_used"))
                dve.wait_ge(S["bias_rows"], w.next("bias_rows", 16))
                top = SMALL[:, 16:24]
                for t in range(1, QT):
                    dve.wait_ge(S["score_cut"], w.next("score_cut"))
                    for _ in range(N_SEL // 8):
                        step(v.max(top, SCORES[t]))
                        step(v.match_replace(out=SCORES[t], in_to_replace=top, in_values=SCORES[t], imm_value=TAKEN))
                    step(v.tensor_scalar(MASKS[t], SCORES[t], TAKEN, NEG, ALU.not_equal, ALU.mult))
                dve.wait_ge(S["act_evac"], w.next("act_evac", 46))
                dve.wait_ge(S["score_mask"], w.next("score_mask"))
                dve.wait_ge(S["bias_flip"], w.next("bias_flip", 8))
                softmax_pairs(PAIRS, [t for _ in range(2) for t in range(QT)], stage_first, maximum_first,
                              DG, [P] * QT, 3, 2 * 8)
                dve_stick()
                w.count("tile_done", 46 - 6)
                dve.wait_ge(S["o_evac"], w.next("o_evac", 8))
                for n in range(DT):
                    dve.wait_ge(S["tile_done"], w.next("tile_done"))
                    b = 2 * (n % 4)
                    v.tensor_tensor(GATES[:, n], GATES[:, n], ps[:, b], ALU.mult)
                    v.tensor_tensor(GATES[:, DT + n], GATES[:, DT + n], ps[:, b + 1], ALU.mult).then_inc(S["dve_evac"], 1)
                for n in range(DT):
                    dve.wait_ge(S["tile_done"], w.next("tile_done"))
                    accumulate(XA[:, n], ps[:, n % 4], 1.0)
                dve.wait_ge(S["dve_evac"], w.next("dve_evac", 16))
                rms(8, SEQ, D, EPS1, "ffn_norm", lambda t: XA[:, t], lambda t: HA[:, t])
                router()
                dve_moe()
                rms(8, SEQ, D, EPS1, "ple_norm", lambda t: XA[:, t], lambda t: HA[:, t])
                for n in range(DT):
                    dve.wait_ge(S["tile_done"], w.next("tile_done"))
                    dve.wait_ge(S["sg"], w.next("sg"))
                    step(v.tensor_tensor(HT[n % 2], SG[n % 2], ps[:, n % 4], ALU.mult))
                    accumulate(XA[:, n], HT[n % 2], 1.0)
                dve.wait_ge(S["dve_evac"], w.next("dve_evac", 8))
                rms(8, SEQ, D, EPS1, "final_norm", lambda t: XA[:, t], lambda t: XA[:, t])
                dve_lru()
                rms(2, T2, 256, EPS2, "q_norm", lambda t: PQ[:, t], lambda t: PQ[:, t])
                rms(1, T2, 128, EPS2, "kv_norm2", lambda t: PKV, lambda t: PKV)
                dve.wait_ge(S["c2_in"], w.next("c2_in", 48))
                dve.wait_ge(S["act_evac"], w.next("act_evac", 4 + 8))
                for x, swapped in [(QP[:, j], QW[:, j]) for j in range(4)] + [(KPE, KPW)]:
                    v.tensor_tensor(x, x, ROPE_C, ALU.mult)
                    step(v.tensor_tensor(swapped, swapped, ROPE_S, ALU.mult))
                    step(v.tensor_tensor(x, x, swapped, ALU.add))
                dve.wait_ge(S["act_evac"], w.next("act_evac", 4 + 5))
                softmax_pairs(PAIRS, [t for _ in range(2) for t in range(5)], stage_second, maximum_second,
                              DG2, [width for _, width in TOK2], 4, 10)
                w.count("tile_done", 13 + 8 + 16 + 5)
                for n in range(DT):
                    dve.wait_ge(S["tile_done"], w.next("tile_done"))
                    accumulate(two(X[:, n]), halves(2 * (n % 4)), ALPHA)
                layer_norm("mix", 0)
                mlp(0)
                dve.wait_ge(S["c3_in"], w.next("c3_in", 48))
                for x in (HN, RK):
                    for h in range(RET_HEADS):
                        dve.wait_ge(S["act_evac"], w.next("act_evac", 2))
                        x1, x2, t1, t2 = x[:, 2 * h], x[:, 2 * h + 1], SRK[:, 0], SRK[:, 1]
                        v.tensor_tensor(t1, x1, SIN, ALU.mult)
                        step(v.tensor_tensor(t2, x2, SIN, ALU.mult))
                        v.tensor_tensor(x1, x1, COS, ALU.mult)
                        step(v.tensor_tensor(x2, x2, COS, ALU.mult))
                        v.tensor_tensor(x1, x1, t2, ALU.subtract)
                        step(v.tensor_tensor(x2, x2, t1, ALU.add))
                dve.wait_ge(S["act_evac"], w.next("act_evac", 32))
                flat = ps[:, :, :].rearrange("p b c -> p (b c)")
                if w.counted("staged"):
                    dve.wait_ge(S["staged"], w.value("staged"))
                with w.loop(RET_HEADS, logits=5, norm_sum=1, norm_sd=1, dve_ops=5, ret_y=1) as i:
                    v.tensor_copy(SRK, RK[:, ds(i * 2, 2), :]).then_inc(S["staged"], 1)
                    v.tensor_copy(SRV[:, 1:5], RV[:, 1:5, ds(i * 512, 512)])
                    v.tensor_copy(SRV[0:META, 0], RV[0:META, 0, ds(i * 512, 512)]).then_inc(S["staged"], 1)
                    for j, (c, kw) in enumerate(TOK2):
                        dve.wait_ge(S["logits"], w.next("logits"))
                        lo = 1024 * (j % 2)
                        v.tensor_tensor(RSC[0:kw, RSC_OFF[j]:RSC_OFF[j] + T2 - c].unsqueeze(1),
                                        flat[0:kw, lo:lo + T2 - c].unsqueeze(1),
                                        DECAY[0:kw, ds(i, 1), 0:T2 - c], ALU.mult).then_inc(S["ret_s"], 1)
                    dve.wait_ge(S["norm_sum"], w.next("norm_sum"))
                    v.tensor_scalar(two(R[:, :]), ps[:, 0:2, 0:HALF], 1.0 / 512, EPS2, ALU.mult, ALU.add).then_inc(S["norm_var"], 1)
                    dve.wait_ge(S["norm_sd"], w.next("norm_sd"))
                    step(v.reciprocal(R[:, :], R[:, :]))
                    for n in range(4):
                        step(v.tensor_tensor(ROT[:, n], ROT[:, n], R[:, :], ALU.mult))
                        g = RG[:, ds(i * 4 + n, 1), :]
                        ins = v.tensor_tensor(g, g, ROT[:, n:n + 1], ALU.mult)
                    ins.then_inc(S["ret_y"], 1)
                    dve.wait_ge(S["ret_y"], w.next("ret_y"))
                w.count("tile_done", 48)
                with w.loop(2, tile_done=4) as i:
                    for n in range(4):
                        dve.wait_ge(S["tile_done"], w.next("tile_done"))
                        accumulate(X[:, ds(i * 4 + n, 1), :].rearrange("p a (h c) -> p (a h) c", h=2), halves(2 * n), ALPHA)
                layer_norm("mix", 1)
                mlp(1)

            def mlp(l):
                with w.loop(4, act_evac=8) as i:
                    for n in range(8):
                        dve.wait_ge(S["act_evac"], w.next("act_evac"))
                        f = FFH[:, ds(i * 8 + n, 1), :]
                        v.tensor_tensor(f, f, f, ALU.mult).then_inc(S["hidden"], 1)
                w.count("tile_done", 32)
                with w.loop(4, tile_done=2) as i:
                    for n in range(2):
                        dve.wait_ge(S["tile_done"], w.next("tile_done"))
                        accumulate(X[:, ds(i * 2 + n, 1), :].rearrange("p a (h c) -> p (a h) c", h=2), halves(2 * n), ALPHA)
                layer_norm("mlp", l)

            def stage_first(i):
                for out, src in ((ST1, QA), (ST2, KA)):
                    v.tensor_copy(out.unsqueeze(1), src[:, ds(i, 1), :]).then_inc(S["staged"], 1)
                v.tensor_copy(KI.rearrange("p (t c) -> p t c", t=QT), VA[:, :, ds(i * P, P)]).then_inc(S["staged"], 1)

            def stage_second(i):
                for out, src in ((SQN, QN), (SQP, QP), (SKN, KN)):
                    v.tensor_copy(out.unsqueeze(1), src[:, ds(i, 1), :]).then_inc(S["staged"], 1)
                v.tensor_copy(SV2[0:META, 0], V2[0:META, 0, ds(i * P, P)])
                v.tensor_copy(SV2[:, 1:5], V2[:, 1:5, ds(i * P, P)]).then_inc(S["staged"], 1)

            def settle(ins=None):
                if ins is not None:
                    step(ins)
                v.nop(nofuse=True)

            def maximum_first(i, u, h, t):
                keys = P * (t + 1)
                lg = LG[u % 2][:, 0:keys]
                settle(v.tensor_tensor(lg.unsqueeze(1), ps[:, u % 2:u % 2 + 1, 0:keys],
                                     BIAS[:, ds(i * 2 + h, 1), SEQ - keys:SEQ], ALU.add))
                v.tensor_tensor_reduce(out=lg, in0=lg, in1=MASKS[t], scale=1.0, scalar=TAKEN, op0=ALU.add, op1=ALU.max,
                                       accum_out=SMALL[:, 8 * (u % 2):8 * (u % 2) + 1]).then_inc(S["smax"], 1)

            def maximum_second(i, u, h, t):
                c, rows = TOK2[t]
                keys = c + rows
                flat = ps[:, :, :].rearrange("p b c -> p (b c)")
                first = T2 - P if t == 0 else T2 - keys
                settle()
                v.tensor_tensor_reduce(out=LG2[u % 2][0:rows, 0:keys], in0=flat[0:rows, 1024 * (u % 2):1024 * (u % 2) + keys],
                                       in1=MASKW[0:rows, first:first + keys], scale=1.0, scalar=TAKEN, op0=ALU.add,
                                       op1=ALU.max, accum_out=SMALL[0:rows, 8 * (u % 2):8 * (u % 2) + 1]).then_inc(S["smax"], 1)

            def softmax_pairs(pairs, order, stage, maximum, dg, rows_of, n_staged, steps):
                n = len(order)
                with w.loop(pairs, logits=n, expd=n, dve_ops=steps, o_done=1) as i:
                    stage(i)
                    def largest(u):
                        dve.wait_ge(S["logits"], w.next("logits"))
                        maximum(i, u, u // (n // 2), order[u])

                    def scale(u):
                        rows = rows_of[order[u]]
                        st = SMALL[0:rows, 8 * (u % 2):8 * (u % 2) + 8]
                        dve.wait_ge(S["expd"], w.next("expd"))
                        step(v.reciprocal(st[:, 3:4], st[:, 2:3]))
                        v.tensor_scalar(dg[u % 2][0:rows, 0:rows], IDENT[0:rows, 0:rows], st[:, 3:4], None, ALU.mult)\
                            .then_inc(S["diag"], 1)

                    largest(0)
                    for u in range(n):
                        if u + 1 < n:
                            largest(u + 1)
                        scale(u)
                    dve.wait_ge(S["o_done"], w.next("o_done"))

            def dve_stick():
                units = [(h, t) for h in range(2) for t in reversed(range(QT))]
                with w.loop(PAIRS, soft=8, o_done=1) as i:
                    for out, src in ((ST1, QB), (ST2, KB)):
                        v.tensor_copy(out.unsqueeze(1), src[:, ds(i, 1), :]).then_inc(S["staged"], 1)
                    v.tensor_copy(ST3.rearrange("p (t c) -> p t c", t=QT), VB[:, :, ds(i * P, P)]).then_inc(S["staged"], 1)
                    for u, (h, t) in enumerate(units):
                        width = SEQ - P * t
                        dve.wait_ge(S["soft"], w.next("soft"))
                        v.scalar_tensor_tensor(out=SPP[h][:, SP_OFF[t]:SP_OFF[t] + width], in0=ps[:, u % 6, 0:width], scalar=0.0,
                                               in1=SPT[u % 2][:, 0:width], op0=ALU.max, op1=ALU.add).then_inc(S["sp"], 1)
                    dve.wait_ge(S["o_done"], w.next("o_done"))

            def first_of(eq, onehot, run):
                step(v.tensor_copy(run, eq[:, :, 0]))
                step(v.tensor_copy(onehot[:, :, 0], eq[:, :, 0]))
                for j in range(1, eq.shape[2]):
                    step(v.tensor_tensor(onehot[:, :, j], eq[:, :, j], run, ALU.is_gt))
                    step(v.tensor_tensor(run, run, eq[:, :, j], ALU.max))

            def small(off, *shape):
                n = int(np.prod(shape))
                x = SMALL[:, off:off + n]
                return x.rearrange("p (a b) -> p a b", a=shape[0]) if len(shape) == 2 else x

            def router():
                lt, gm, sh, eq = small(16, 4, 36), small(160, 4), small(176, 4, 4), small(204, 4, 4)
                run, oh, es = small(220, 4), small(224, 4, 4), small(240, 4, 8)
                prod = SMALL[:, 288:416].rearrange("p (t g e) -> p t g e", t=4, g=4)
                m1, m2, pg, diff = small(164, 4), small(168, 4), small(172, 4), small(200, 4)
                w1, w2 = small(272, 4), small(276, 4)
                dve.wait_ge(S["route_done"], w.next("route_done"))
                dve.wait_ge(S["wr_in"], w.next("wr_in", 32))
                step(v.tensor_tensor(lt, ps[:, 6, 0:144].rearrange("p (t c) -> p t c", t=4), BR, ALU.add))
                g = lt[:, :, 0:4]
                step(v.tensor_reduce(gm, g, AX, ALU.max))
                v.tensor_tensor(sh, g, bc(gm, 4, 4), ALU.subtract).then_inc(S["route_e"], 1)
                step(v.tensor_tensor(eq, g, bc(gm, 4, 4), ALU.is_equal))
                first_of(eq, oh, run)
                for n in range(GROUPS):
                    step(v.tensor_tensor(prod[:, :, n], lt[:, :, 4 + 8 * n:12 + 8 * n],
                                         oh[:, :, n].unsqueeze(2).to_broadcast([P, 4, 8]), ALU.mult))
                step(v.tensor_reduce(es, prod.rearrange("p t g e -> p t e g"), AX, ALU.add))
                eq8, oh1, oh2, es2 = small(16, 4, 8), small(48, 4, 8), small(80, 4, 8), small(112, 4, 8)
                step(v.tensor_reduce(m1, es, AX, ALU.max))
                step(v.tensor_tensor(eq8, es, bc(m1, 4, 8), ALU.is_equal))
                first_of(eq8, oh1, run)
                step(v.scalar_tensor_tensor(out=es2, in0=oh1, scalar=TAKEN, in1=es, op0=ALU.mult, op1=ALU.add))
                step(v.tensor_reduce(m2, es2, AX, ALU.max))
                v.tensor_tensor(diff, m2, m1, ALU.subtract).then_inc(S["route_e"], 1)
                step(v.tensor_tensor(eq8, es2, bc(m2, 4, 8), ALU.is_equal))
                first_of(eq8, oh2, run)
                dve.wait_ge(S["route_x"], w.next("route_x", 2))
                step(v.tensor_reduce(pg, sh, AX, ALU.add))
                step(v.reciprocal(pg, pg))
                step(v.tensor_scalar(w1, diff, 1.0, None, ALU.add))
                step(v.reciprocal(w1, w1))
                step(v.tensor_tensor(w1, w1, pg, ALU.mult))
                step(v.tensor_tensor(w2, w1, diff, ALU.mult))
                step(v.tensor_tensor(oh1, oh1, bc(w1, 4, 8), ALU.mult))
                step(v.tensor_tensor(oh2, oh2, bc(w2, 4, 8), ALU.mult))
                step(v.tensor_tensor(es2, oh1, oh2, ALU.add))
                for n in range(GROUPS):
                    ins = v.tensor_tensor(prod[:, :, n], es2, oh[:, :, n].unsqueeze(2).to_broadcast([P, 4, 8]), ALU.mult)
                ins.then_inc(S["route_ev"], 1)

            def dve_moe():
                def hidden(e):
                    for f in range(2):
                        dve.wait_ge(S["sg"], w.next("sg"))
                        dve.wait_ge(S["gu_done"], w.next("gu_done", 2))
                        step(v.tensor_tensor(HT[f], SG[f], ps[:, 2 * f], ALU.mult))
                        v.tensor_tensor(HT[f], HT[f], ps[:, 2 * f + 1], ALU.mult).then_inc(S["gu_evac"], 1)
                        dve.wait_ge(S["gu_evac"], w.next("gu_evac"))
                        if f == 0:
                            dve.wait_ge(S[f"cb{e % 2}"], w.next(f"cb{e % 2}") * 16)
                        v.tensor_tensor(HID[e % 2][:, f], HT[f], CB[e % 2], ALU.mult).then_inc(S["hid"], 1)

                def down():
                    for n in range(DT):
                        dve.wait_ge(S["dn_done"], w.next("dn_done"))
                        v.tensor_tensor(XA[:, n], XA[:, n], ps[:, 4 + n % 4], ALU.add).then_inc(S["dn_evac"], 1)

                hidden(0)
                for e in range(4):
                    hidden(e + 1)
                    down()
                    w.count("dn_evac", 8)
                with w.loop(6, sg=8, gu_done=16, gu_evac=8, cb0=2, cb1=2, dn_done=32, dn_evac=32, dve_ops=8):
                    for e in range(4):
                        hidden(e + 1)
                        down()
                        w.count("dn_evac", 8)
                for e in range(4):
                    if e < 3:
                        hidden(e + 1)
                    down()
                    w.count("dn_evac", 8)
                if w.counted("dn_evac"):
                    dve.wait_ge(S["dn_evac"], w.value("dn_evac"))

            def dve_lru():
                e, s, s2, acc, sp8 = (LAM[:, 4 * j:4 * j + 4] for j in range(5))
                lam = V[:, VEC_AT["lam"]:VEC_AT["lam"] + 4]
                dve.wait_ge(S["lam_exp"], w.next("lam_exp"))
                step(v.tensor_scalar(s, e, 2.0, None, ALU.add))
                step(v.reciprocal(s, s))
                step(v.tensor_tensor(s, s, e, ALU.mult))
                step(v.tensor_tensor(s2, s, s, ALU.mult))
                step(v.tensor_scalar(acc, s2, 1.0 / 15, 1.0 / 13, ALU.mult, ALU.add))
                for k in (11, 9, 7, 5, 3, 1):
                    step(v.tensor_tensor(acc, acc, s2, ALU.mult))
                    step(v.tensor_scalar(acc, acc, 1.0 / k, None, ALU.add))
                step(v.tensor_tensor(acc, acc, s, ALU.mult))
                step(v.tensor_scalar(sp8, lam, -1.0, 0.0, ALU.mult, ALU.max))
                step(v.scalar_tensor_tensor(out=sp8, in0=acc, scalar=2.0, in1=sp8, op0=ALU.mult, op1=ALU.add))
                step(v.tensor_scalar(sp8, sp8, LRU_C, None, ALU.mult))
                dve.wait_ge(S["pad_zero"], w.next("pad_zero"))
                dve.wait_ge(S["act_evac"], w.next("act_evac", 4))
                for j in range(4):
                    dve.wait_ge(S["act_evac"], w.next("act_evac"))
                    step(v.tensor_scalar(XC[:, j], PREC[:, j, 3:3 + N2], vec("conv_w", 12 + j), vec("conv_b", j), ALU.mult, ALU.add))
                    for k in (2, 1, 0):
                        ins = v.scalar_tensor_tensor(out=XC[:, j], in0=PREC[:, j, k:k + N2], scalar=vec("conv_w", 4 * k + j),
                                                     in1=XC[:, j], op0=ALU.mult, op1=ALU.add)
                        if k:
                            step(ins)
                    ins.then_inc(S["lru_x"], 1)
                dve.wait_ge(S["act_evac"], w.next("act_evac", 5))
                for j in range(4):
                    dve.wait_ge(S["act_evac"], w.next("act_evac"))
                    v.tensor_scalar(RA[:, j], RA[:, j], sp8[:, j:j + 1], None, ALU.mult).then_inc(S["lru_r"], 1)
                dve.wait_ge(S["act_evac"], w.next("act_evac", 4))
                for j in range(4):
                    dve.wait_ge(S["lru_t"], w.next("lru_t"))
                    step(v.tensor_tensor(RX[:, j], RX[:, j], XC[:, j], ALU.mult))
                    step(v.tensor_scalar(XC[:, j], LRU_T[:, j], 1.0, None, ALU.add))
                    step(v.reciprocal(XC[:, j], XC[:, j]))
                    step(v.scalar_tensor_tensor(out=LRU_T[:, j], in0=LRU_T[:, j], scalar=2.0, in1=XC[:, j], op0=ALU.mult, op1=ALU.mult))
                    v.tensor_scalar(LRU_T[:, j], LRU_T[:, j], 2.0 ** -116, None, ALU.max).then_inc(S["lru_r"], 1)
                for j in range(4):
                    dve.wait_ge(S["lru_t"], w.next("lru_t"))
                    step(v.scalar_tensor_tensor(out=RX[:, j], in0=LRU_T[:, j], scalar=-2.0 ** -58, in1=RX[:, j],
                                                op0=ALU.add, op1=ALU.mult))
                    step(v.tensor_tensor_scan(Y2[:, j], RA[:, j], RX[:, j], 0.0, ALU.mult, ALU.add))
                    dve.wait_ge(S["gelu_done"], w.next("gelu_done"))
                    v.tensor_tensor(Y2[:, j], Y2[:, j], PG[:, j], ALU.mult).then_inc(S["lru_done"], 1)

            WI = SMALL[:, 416:448]
            body()

        @block.gpsimd
        def _(pool):
            w = Counts(pool)
            g = nc.gpsimd

            def step(ins):
                ins.then_inc(S["pool_ops"], 1)
                pool.wait_ge(S["pool_ops"], w.next("pool_ops"))

            def keep(out, compare, fill):
                return g.affine_select(out=out, in_=out, **compare, fill=fill)

            CAUSAL = dict(compare_op=ALU.is_ge, base=0, pattern=[[-1, P]], channel_multiplier=1)
            BEFORE = dict(compare_op=ALU.is_gt, base=0, pattern=[[1, P]], channel_multiplier=-1)

            def body():
                pool.dma_start(HOT, a["onehot"]).then_inc(S["hot_in"], 16)
                pool.dma_start(RELB, a["rel_bias"]).then_inc(S["hot_in"], 16)
                pool.dma_start(WIDX, a["w_idx"]).then_inc(S["small_in"], 16)
                pool.wait_ge(S["bias_dram"], w.next("bias_dram"))
                pool.dma_start(bias_scratch.ap(), BVEC).then_inc(S["bvec_out"], 16)
                pool.wait_ge(S["bvec_out"], w.next("bvec_out", 16))
                rows = bass.AP(bias_scratch, 0, [[1, P], [BIAS_W, HEADS], [1, SEQ]])
                pool.dma_start(BIAS_FLIPPED, rows).then_inc(S["bias_rows"], 16)
                pool.wait_ge(S["bias_rows"], w.next("bias_rows", 16))
                step(g.memset(MASKS[0], 0.0))
                keep(MASKS[0], CAUSAL, NEG).then_inc(S["score_mask"], 1)
                for t in range(1, QT):
                    pool.wait_ge(S["rel_used"], w.next("rel_used", HEADS))
                    keep(SCORES[t][:, P * t:P * t + P], CAUSAL, LOW).then_inc(S["score_cut"], 1)
                pool.wait_ge(S["staged"], w.next("staged", 3))
                pool.dma_start(WROUT, a["w_router"]).then_inc(S["wr_in"], 16)
                pool.dma_start(BR, a["b_router"]).then_inc(S["wr_in"], 16)
                units = [(h, t) for h in range(2) for t in reversed(range(QT))]
                with w.loop(PAIRS, sp=8, a_raw=8):
                    def mask_p(u):
                        h, t = units[u]
                        pool.wait_ge(S["sp"], w.next("sp"))
                        g.nop(nofuse=True)
                        keep(SPP[h][:, SP_OFF[t]:SP_OFF[t] + P], BEFORE, 0.0).then_inc(S["sp_masked"], 1)

                    def mask_a(u):
                        pool.wait_ge(S["a_raw"], w.next("a_raw"))
                        g.nop(nofuse=True)
                        keep(SPA[u % 2][:, 0:P], BEFORE, 0.0).then_inc(S["a_masked"], 1)

                    mask_p(0)
                    mask_p(1)
                    for u in range(8):
                        if u + 2 < 8:
                            mask_p(u + 2)
                        mask_a(u)
                w.count("dve_evac")
                for n in range(DT):
                    pool.wait_ge(S["dve_evac"], w.next("dve_evac"))
                    g.tensor_tensor(MERGED[:, n], GATES[:, n], GATES[:, DT + n], ALU.add).then_inc(S["merged"], 1)
                pool.wait_ge(S["comb_ev"], w.next("comb_ev"))
                pool.dma_start(PX, a["p"]).then_inc(S["p_in"], 16)
                pool.dma_start(comb_scratch.ap(), COMBT[0:EXPERTS]).then_inc(S["comb_dram"], 16)
                pool.wait_ge(S["comb_dram"], w.next("comb_dram", 16))

                def broadcast(e, row):
                    pool.dma_start(CB[e % 2].unsqueeze(1), comb_scratch.ap()[row, :].partition_broadcast(P))\
                        .then_inc(S[f"cb{e % 2}"], 16)

                for e in range(2):
                    broadcast(e, slice(e, e + 1))
                with w.loop(15, hid=4) as i:
                    for e in range(2):
                        pool.wait_ge(S["hid"], w.next("hid", 2))
                        broadcast(e, ds(i * 2 + (2 + e), 1))
                w.count("hid", 4)
                pool.wait_ge(S["norm_out"], w.next("norm_out", 33))
                pool.dma_start(MASKW, a["causal"]).then_inc(S["c2_in"], 16)
                pool.dma_start(ROPE_C, a["mla_cos"]).then_inc(S["c2_in"], 16)
                pool.dma_start(ROPE_S, a["mla_sin"]).then_inc(S["c2_in"], 16)
                g.memset(PREC[:, :, 0:3], 0.0).then_inc(S["pad_zero"], 1)
                w.count("act_evac", 46)
                for j in range(4):
                    pool.wait_ge(S["act_evac"], w.next("act_evac"))
                    step(g.tensor_tensor(GELU[:, j], PG[:, j], PG[:, j], ALU.mult))
                    step(g.tensor_scalar(GELU[:, j], GELU[:, j], 0.044715, 1.0, ALU.mult, ALU.add))
                    g.tensor_tensor(GELU[:, j], GELU[:, j], PG[:, j], ALU.mult).then_inc(S["gelu_in"], 1)
                for j in range(4):
                    pool.wait_ge(S["gelu_th"], w.next("gelu_th"))
                    step(g.tensor_scalar(GELU[:, j], GELU[:, j], 0.5, 0.5, ALU.mult, ALU.add))
                    g.tensor_tensor(PG[:, j], PG[:, j], GELU[:, j], ALU.mult).then_inc(S["gelu_done"], 1)
                pool.wait_ge(S["dve_evac"], w.next("dve_evac", 8 + 8 + 8))
                pool.dma_start(DECAY, a["decay"]).then_inc(S["c3_in"], 16)
                pool.dma_start(COS, a["cos"]).then_inc(S["c3_in"], 16)
                pool.dma_start(SIN, a["sin"]).then_inc(S["c3_in"], 16)

            body()


def bucket(dist):
    dist = np.maximum(dist, 0)
    exact = N_BUCKETS // 2
    d = np.maximum(dist, 1).astype(np.float32)
    large = exact + (np.log(d / exact) / math.log(128 / exact) * (N_BUCKETS - exact)).astype(np.int32)
    return np.where(dist < exact, dist, np.minimum(large, N_BUCKETS - 1))


def constants():
    f = np.float32
    i = np.arange(P)
    mats = np.stack([np.eye(P), np.ones((P, P)), np.eye(P)[::-1], -(i[:, None] >= i[None, :]).astype(f), -np.ones((P, P))], 1)
    hot = np.zeros((N_BUCKETS, BIAS_W), f)
    hot[bucket(SEQ - 1 - np.arange(BIAS_W)), np.arange(BIAS_W)] = 1
    causal = np.where(np.arange(T2)[None, :] - (T2 - P) > i[:, None], NEG, 0.0)
    pos = np.arange(T2, dtype=f)

    def angles(half):
        inv = (f(10000.0) ** (-np.arange(half, dtype=f) / half)).astype(f)
        ang = (pos[None, :] * inv[:, None]).astype(f)
        return np.cos(ang), np.sin(ang)

    c, s = angles(16)
    rope = np.zeros((2, P, T2), f)
    for at in (0, HD):
        rope[0, at:at + 32] = np.concatenate([c, c])
        rope[1, at:at + 32] = np.concatenate([-s, s])
    cos, sin = angles(P)
    log_gamma = np.log(f(1.0) - f(2.0) ** (f(-5.0) - np.arange(RET_HEADS, dtype=f)))
    diff = np.arange(T2)[None, :] - i[:, None]
    decay = np.where(diff[:, None] >= 0, np.exp(log_gamma[None, :, None] * np.maximum(diff, 0)[:, None]), 0)
    out = dict(mats=mats, onehot=hot, causal=causal, mla_cos=rope[0], mla_sin=rope[1], cos=cos, sin=sin, decay=decay)
    return {k: np.ascontiguousarray(v, dtype=f) for k, v in out.items()}


def blocks(w):
    k, n = w.shape
    return w.reshape(k // P, P, n // P, P).transpose(2, 1, 0, 3)


def layout(i):
    f = np.float32
    cut = np.cumsum([0, 512, 128, 512, 64, 8, 1536, 1024, 1024])
    w_in = i["w_in"][0]
    qa, ckv, qidx, kidx, widx, qkv, ga, gb = (w_in[:, a:b] for a, b in zip(cut[:-1], cut[1:]))
    chunks = [blocks(x) for x in (ckv, np.concatenate([kidx, kidx], 1), qidx, qa, qkv, ga, gb)]
    uk = np.moveaxis(i["w_uk"][0], 0, 1).reshape(P, 512)
    uv = np.moveaxis(i["w_uv"][0], 0, 1).reshape(P, 512)
    chunks.append(np.concatenate([uk, uv], 1).reshape(1, P, 8, P))
    chunks.append(np.concatenate([blocks(i["w_branch_a"][0]), blocks(i["w_branch_b"][0])], 2))
    chunks.append(blocks(i["w_out"][0]))
    gate = [blocks(i["w_gate"][0, e]) for e in range(EXPERTS)]
    up = [blocks(i["w_up"][0, e]) for e in range(EXPERTS)]
    down = [blocks(i["w_down"][0, e]).transpose(1, 0, 2, 3).reshape(P, 2, 8, P).transpose(1, 0, 2, 3) for e in range(EXPERTS)]
    for e in range(EXPERTS + 1):
        if e < EXPERTS:
            chunks += [gate[e][:1], up[e][:1], gate[e][1:], up[e][1:]]
        if e:
            chunks.append(down[e - 1])
    ple = blocks(i["w_ple"][0]).transpose(1, 0, 2, 3).reshape(P, 2, 8, P).transpose(1, 0, 2, 3)
    pleg = blocks(i["w_ple_gate"][0])
    chunks += [ple[:1], pleg[:4], ple[1:], pleg[4:]]
    ev = i["ev_w_in_2"][0]
    kpe = ev[:, 1408:1440]
    swap = lambda x: np.concatenate([x[..., 16:], x[..., :16]], -1)
    zero = np.zeros((D, 32), f)
    chunks.append(blocks(np.concatenate([ev[:, :1408], kpe, zero, kpe, zero, swap(kpe), zero, swap(kpe), zero], 1)))
    rg = np.concatenate([i["ev_w_rg_a_2"][0], i["ev_w_rg_x_2"][0]], 0)
    chunks.append(rg.transpose(1, 0, 2)[None])
    uq = i["ev_w_uq_2"][0].reshape(256, HEADS, 96)
    z = np.zeros((256, HEADS, 32), f)
    nope = uq[:, :, :64].reshape(256, 512)
    pe = np.concatenate([uq[:, :, 64:], z], 2).reshape(256, 512)
    pw = np.concatenate([swap(uq[:, :, 64:]), z], 2).reshape(256, 512)
    chunks += [blocks(x).transpose(1, 0, 2, 3).reshape(1, P, 8, P) for x in (nope, pe, pw)]
    ukv = i["ev_w_ukv_2"][0].reshape(P, HEADS, 2, 64)
    chunks.append(np.concatenate([ukv[:, :, 0].reshape(P, 512), ukv[:, :, 1].reshape(P, 512)], 1).reshape(1, P, 8, P))
    chunks.append(blocks(i["ev_w_out_2"][0]))

    def deep(w):
        b = blocks(w)
        return b.reshape(b.shape[0], P, -1, 8, P).transpose(0, 2, 1, 3, 4).reshape(-1, P, 8, P)

    for l in range(2):
        if l:
            chunks += [blocks(i["od_w_in_2"][0]), deep(i["od_w_out_2"][0])]
        chunks += [blocks(i["mlp_w1_2"][l]), deep(i["mlp_w2_2"][l])]
    weights = np.concatenate([np.asarray(c, f).reshape(-1, P, D) for c in chunks], 0)
    assert weights.shape[0] == N_CHUNKS, (weights.shape, N_CHUNKS)

    col = lambda x: np.asarray(x, f).reshape(-1, P).T
    vecs = [i["attn_norm"], i["kv_norm"], i["ffn_norm"], i["ple_norm"], i["final_norm"], i["ev_conv_w_2"], i["ev_conv_b_2"],
            i["ev_b_rg_a_2"], i["ev_b_rg_x_2"], i["ev_lru_lambda_2"], i["ev_q_norm_g_2"], i["ev_kv_norm_g_2"],
            i["ln_mix_g_2"], i["ln_mix_b_2"], i["ln_mlp_g_2"], i["ln_mlp_b_2"]]
    tiles = lambda x: np.asarray(x, f).T.reshape(-1, P, x.shape[0]).transpose(1, 0, 2)
    rows = lambda x: np.asarray(x, f).reshape(DT, P, -1).transpose(1, 0, 2)
    router = np.concatenate([i["w_r1"][0], np.moveaxis(i["w_r2"][0], 0, 1).reshape(D, EXPERTS)], 1)
    b_router = np.concatenate([i["b_r1"][0], i["b_r2"][0].reshape(-1)])
    out = dict(x=tiles(i["x"][0]), meta=tiles(i["meta_tokens_2"]), p=tiles(i["p"][0, 0]), weights=weights,
               vecs=np.concatenate([col(v) for v in vecs], 1), w_idx=rows(widx), w_router=rows(router),
               b_router=np.broadcast_to(b_router, (P, QT, 36)), rel_bias=i["rel_bias"])
    return {k: np.ascontiguousarray(v, dtype=f) for k, v in (out | constants()).items()}


def kernel(**inputs):
    import concourse.bacc as bacc
    from concourse.bass_utils import run_bass_kernel_spmd

    arrays = layout({k: np.asarray(v) for k, v in inputs.items()})
    nc = bacc.Bacc("TRN2", target_bir_lowering=False, num_devices=1)
    aps = {k: nc.dram_tensor(f"in_{k}", v.shape, F32, kind="ExternalInput").ap() for k, v in arrays.items()}
    aps["out"] = nc.dram_tensor("out_tiles", (P, DT, SEQ), F32, kind="ExternalOutput").ap()
    build(nc, aps)
    r = run_bass_kernel_spmd(nc, [{f"in_{k}": v for k, v in arrays.items()}], core_ids=[0])
    out = r.results[0]["out_tiles"]
    return np.ascontiguousarray(out.transpose(2, 1, 0).reshape(1, SEQ, D))
```

```python
import math
from contextlib import ExitStack, contextmanager

import numpy as np
import concourse.bass as bass
from concourse import mybir

F32 = mybir.dt.float32
ALU = mybir.AluOpType
ACT = mybir.ActivationFunctionType
AX = mybir.AxisListType.X
ds = bass.ds

P = 128
D = 1024
DT = D // P
SEQ = 512
META = 16
T2 = SEQ + META
HALF = T2 // 2
QT = SEQ // P
HEADS = 8
HD = 64
PAIRS = HEADS // 2
KV_RANK = 128
N_SEL = min(256, SEQ // 4)
IDX_SCALE = (8 ** -0.5) * (64 ** -0.5)
QK_SCALE = HD ** -0.5
N_BUCKETS = 32
GROUPS, PER_GROUP = 4, 8
EXPERTS = GROUPS * PER_GROUP
EPS1, EPS2 = 1e-6, 1e-5
ALPHA = 4.0 ** 0.25
MLA_SCALE = 96 ** -0.5
RET_HEADS = 4
LRU_C = 8.0
FF = 4 * D
NEG = -1.0e30
LOW = -1.0e38
TAKEN = -3.0e38

CHUNKS = [("kv", 2), ("qidx", 4), ("qa", 4), ("qb", 4), ("kb", 4), ("vb", 4), ("gates", 16), ("ukuv", 1),
          ("merge", 8), ("wout", 8), ("moe", 6 * EXPERTS), ("ple", 10),
          ("evin", 13), ("rg", 1), ("uq", 3), ("ukv", 1), ("evout", 8), ("up0", 32), ("down0", 32),
          ("odqk", 16), ("odv", 16), ("odg", 16), ("odout", 16), ("up1", 32), ("down1", 32)]
N_CHUNKS = sum(n for _, n in CHUNKS)
MOE_AT = sum(n for _, n in CHUNKS[:[name for name, _ in CHUNKS].index("moe")])
TOP_K = 2
PAIRED = TOP_K * SEQ
PAIR_T = PAIRED // P
WINDOWS = (PAIRED - EXPERTS) // P + EXPERTS
WIDE = PAIRED + P
TAB = WINDOWS + 1
MOE_USES = 6 * WINDOWS
N_USES = N_CHUNKS + MOE_USES - 6 * EXPERTS
SLOTS = 8

VECS = [("attn_norm", 8), ("kv_norm", 1), ("ffn_norm", 8), ("ple_norm", 8), ("final_norm", 8),
        ("conv_w", 16), ("conv_b", 4), ("b_rg_a", 4), ("b_rg_x", 4), ("lam", 4), ("q_norm", 2), ("kv_norm2", 1),
        ("ln_mix_g", 16), ("ln_mix_b", 16), ("ln_mlp_g", 16), ("ln_mlp_b", 16), ("row", 1)]
VEC_AT, _n = {}, 0
for _name, _w in VECS:
    VEC_AT[_name] = _n
    _n += _w
N_VEC = _n

TOK2 = [(0, META)] + [(META + P * i, P) for i in range(QT)]
BIAS_W = SEQ + P


class Counts:

    def __init__(self, eng):
        self.eng = eng
        self.base, self.local, self.per, self.i = {}, {}, {}, None

    def value(self, name, back=0):
        at = self.base.get(name, 0) + self.local.get(name, 0) - back
        return at if self.i is None or not self.per.get(name) else self.i * self.per[name] + at

    def count(self, name, k=1):
        assert self.i is None or name in self.per, name
        self.local[name] = self.local.get(name, 0) + k

    def next(self, name, k=1):
        self.count(name, k)
        return self.value(name)

    def counted(self, name, back=0):
        return self.base.get(name, 0) + self.local.get(name, 0) > back

    @contextmanager
    def loop(self, times, **per):
        for n, k in self.local.items():
            self.base[n] = self.base.get(n, 0) + k
        self.local, self.per = {}, per
        with self.eng.Fori(0, times) as i:
            self.i = i
            yield i
        self.i = None
        assert {n: k for n, k in self.local.items() if k} == {n: k for n, k in per.items() if k}, (self.local, per)
        for n, k in per.items():
            self.base[n] = self.base.get(n, 0) + k * times
        self.local, self.per = {}, {}


def build(nc, a):
    ctx = ExitStack()
    with ctx:
        def sb(name, shape):
            return ctx.enter_context(nc.sbuf_tensor(name, shape, F32))

        X = sb("residual", [P, DT, T2])
        HN = sb("normed", [P, DT, T2])
        RING = sb("weights", [P, SLOTS, D])
        AREA = sb("area", [P, 34688])
        V = sb("vectors", [P, N_VEC])
        CM = sb("matrices", [P, 5, P])
        R = sb("rstd", [P, T2])
        ps = ctx.enter_context(nc.psum_tensor("ps", [P, 8, 512], F32))
        IDENT, ONES, FLIP, NTRI, NONES = (CM[:, j] for j in range(5))

        def area(off, *shape):
            n = int(np.prod(shape))
            assert off + n <= 34688, (off, n)
            v = AREA[:, off:off + n]
            if len(shape) == 2:
                v = v.rearrange("p (a b) -> p a b", a=shape[0])
            if len(shape) == 3:
                v = v.rearrange("p (a b c) -> p a b c", a=shape[0], b=shape[1])
            return v

        CKV, KI = area(0, SEQ), area(512, SEQ)
        QA, QI = area(1024, PAIRS, SEQ), area(3072, PAIRS, SEQ)
        QB, KB = area(5120, PAIRS, SEQ), area(7168, PAIRS, SEQ)
        VB = area(9216, QT, SEQ)
        GATES = area(11264, 16, SEQ)
        KA, VA = area(19456, PAIRS, SEQ), area(21504, QT, SEQ)
        BIAS = area(23552, HEADS, SEQ)
        SCORE_OFF = [27648 + o for o in (0, 128, 384, 768)]
        SCORES = [area(o, P * (t + 1)) for t, o in enumerate(SCORE_OFF)]
        MASKS = [area(o + 1280, P * (t + 1)) for t, o in enumerate(SCORE_OFF)]
        TMP = 30208
        LG = [area(TMP, 512), area(TMP + 512, 512)]
        EX = [area(TMP + 1024, 512), area(TMP + 1536, 512)]
        PT = [area(TMP + 2048, 4, P), area(TMP + 2560, 4, P)]
        DG = [area(33280, P), area(33408, P)]
        ST1, ST2 = area(33536, 512), area(34048, 512)
        MERGED = area(7168, DT, SEQ)
        BIAS_FLIPPED = area(11264, HEADS, SEQ)
        SPT = [area(27648, 512), area(28160, 512)]
        SPP = [area(28672, 1280), area(29952, 1280)]
        SPA = [area(31232, 512), area(31744, 512)]
        ST3 = area(32256, 512)
        SMALL = sb("small", [P, 448])
        WIDX = area(19456, DT, 8)
        WROUT = area(0, DT, 36)
        SP_OFF = [0, 512, 896, 1152]
        HOT, RELB = area(27648, BIAS_W)[0:N_BUCKETS], area(28288, HEADS)[0:N_BUCKETS]
        BVEC = area(28928, BIAS_W)[0:HEADS]
        BR = area(288, QT, 36)
        LAM = sb("lambda", [P, 24])
        SG = [area(1024, 512), area(1536, 512)]
        HT = [area(2048, 512), area(2560, 512)]
        PICK1, PICK2, PICKED, PRODUCT = (area(512 + 128 * j, QT, EXPERTS) for j in range(4))
        TABLE = area(1024, 12, EXPERTS)
        SLOT, COLUMN = area(1408, 2, QT), area(1416, 2)
        DIAGS = area(1424, 2, P)
        HID = [area(3072, 2, P), area(3328, 2, P)]
        SILU = [area(3584, 2, P), area(3840, 2, P)]
        XW = [area(4096, DT, P), area(5120, DT, P)]
        HTOK, PICK = area(6144, QT, D), area(10240, QT, PAIRED)
        YS = area(6144, DT, WIDE)
        WEIGH = area(15360, QT, PAIRED)
        XS = area(19456, DT, WIDE)
        YPAIR = area(19456, PAIR_T, D)
        PX = area(28672, 2, SEQ)
        WPAIR = area(29696, PAIR_T, SEQ)
        IOTA = area(33664, PAIRED)
        PAIR_TMP = area(2048, PAIRED)
        WTAB = ctx.enter_context(nc.sbuf_tensor("windows", [P, 2 * TAB], mybir.dt.int32))[0:1]

        N2 = T2
        PG, PREC = area(0, 4, N2), area(2112, 4, N2 + 3)
        PQ, PKV, KPE, KPW = area(4236, 2, N2), area(5292, N2), area(5820, N2), area(6348, N2)
        XC, RA, RX = area(6876, 4, N2), area(8988, 4, N2), area(11100, 4, N2)
        QN, QP, QW, KN = area(13212, 4, N2), area(15324, 4, N2), area(17436, 4, N2), area(19548, 4, N2)
        V2 = area(21660, 5, 512)
        Y2 = area(24220, 8, N2)
        GELU = area(26332, 4, N2)
        LRU_T = area(2112, 4, N2)
        MASKW, ROPE_C, ROPE_S = area(28444, N2), area(28972, N2), area(29500, N2)
        LG2 = [area(30028, N2), area(30556, N2)]
        EX2 = [area(31084, N2), area(31612, N2)]
        PT2 = [area(32140, 5, P), area(32780, 5, P)]
        DG2 = [area(33420, P), area(33548, P)]
        SQN, SQP, SKN, SV2 = area(6876, N2), area(7404, N2), area(7932, N2), area(8460, 5, P)
        FFH = area(0, 32, N2)
        RK, RV, RG = area(0, 8, N2), area(4224, 5, 2048), area(14464, 16, N2)
        SRK, SRV, RSC = area(22912, 2, N2), area(23968, 5, 512), area(26528, 1808)
        RSC_OFF = [0, 528, 1040, 1424, 1680]
        DECAY, COS, SIN = area(28336, 4, N2), area(30448, N2), area(30976, N2)
        ROT, RSQ = area(30448, 4, N2), area(32560, 4, N2)

        names = """x_in consts norm_sq norm_sum norm_var norm_sd norm_out ctr act_ops dve_ops pool_ops
            tile_done act_evac dve_evac chunk_begun rel_done rel_sb rel_used score_sum score_cut score_mask
            bias_vec bias_dram bias_rows bias_flip small_in logits smax expd diag tr pt o_done o_evac staged
            z_done soft sp sp_masked c_done a_raw a_masked merged flip_done
            route_done route_ev route_e rank_done table_in table_rows table iota_in pad_in pick_in weigh_in
            tokens_in sg gu_done hid dn_done dn_evac
            p_in meta_in out_done ln_cent ln_out c2_in c3_in hot_in bvec_out wr_in route_x lam_exp gelu_in gelu_th
            gelu_done lru_t pad_zero lru_x lru_r lru_done hidden ret_s ret_used ret_o ret_y""".split()
        S = {n: ctx.enter_context(nc.semaphore(n)) for n in names}
        chunk_full = [ctx.enter_context(nc.semaphore(f"chunk_full{s}")) for s in range(SLOTS)]
        bias_scratch = nc.dram_tensor("bias_scratch", (HEADS, BIAS_W), F32, kind="Internal")

        B1 = slice(META, T2)
        XA, HA = X[:, :, B1], HN[:, :, B1]

        def vec(name, j=0):
            return V[:, VEC_AT[name] + j:VEC_AT[name] + j + 1]

        def halves(bank):
            return ps[:, bank:bank + 2, 0:HALF]

        def two(v):
            return v.rearrange("p (h c) -> p h c", h=2)

        block = ctx.enter_context(nc.Block())

        @block.sync
        def _(sp):
            w = Counts(sp)
            sp.dma_start(XA, a["x"]).then_inc(S["x_in"], 16)
            sp.dma_start(V[:], a["vecs"]).then_inc(S["consts"], 16)
            sp.dma_start(CM[:], a["mats"]).then_inc(S["consts"], 16)
            sp.dma_start(X[:, :, 0:META], a["meta"]).then_inc(S["meta_in"], 16)

            def load(slot, chunk):
                sp.dma_start(RING[:, slot:slot + 1, :],
                             a["weights"][chunk].rearrange("a p n -> p a n")).then_inc(chunk_full[slot], 16)

            for c in range(SLOTS):
                load(c, slice(c, c + 1))

            def refill(use, chunk, back=0):
                sp.wait_ge(S["chunk_begun"], back + use - SLOTS + 2)
                load(use % SLOTS, chunk)

            def stream(first, last, shift):
                times = (last - first) // SLOTS
                with sp.Fori(0, times) as i:
                    for s in range(SLOTS):
                        refill(first + s, ds(i * SLOTS + (first + s - shift), 1), i * SLOTS)
                for u in range(first + SLOTS * times, last):
                    refill(u, slice(u - shift, u - shift + 1))

            stream(SLOTS, MOE_AT, 0)
            sp.wait_ge(S["table"], w.next("table"))

            def window(use, at, back=0):
                gate_up = sp.value_load(WTAB[:, at(0)], min_val=MOE_AT, max_val=MOE_AT + 6 * (EXPERTS - 1))
                for j in range(4):
                    refill(use + j, ds(gate_up + j, 1), back)
                down(use + 4, at(-1), back)

            def down(use, at, back=0):
                first = sp.value_load(WTAB[:, at], min_val=MOE_AT, max_val=MOE_AT + 6 * (EXPERTS - 1))
                for j in range(2):
                    refill(use + j, ds(first + (4 + j), 1), back)

            first = sp.value_load(WTAB[:, 0:1], min_val=MOE_AT, max_val=MOE_AT + 6 * (EXPERTS - 1))
            for j in range(4):
                refill(MOE_AT + j, ds(first + j, 1))
            for n in (1, 2):
                window(MOE_AT + 6 * n - 2, lambda b: slice(n + b, n + b + 1))
            with sp.Fori(0, (WINDOWS - 3) // 4) as i:
                for n in range(4):
                    window(MOE_AT + 6 * (n + 3) - 2, lambda b: ds(i * 4 + (n + 3 + b), 1), i * 24)
            down(MOE_AT + MOE_USES - 2, slice(WINDOWS - 1, WINDOWS))
            stream(MOE_AT + MOE_USES, N_USES, MOE_USES - 6 * EXPERTS)
            sp.wait_ge(S["ln_out"], 32)
            sp.dma_start(a["out"], X[:, :, B1]).then_inc(S["out_done"], 16)
            sp.wait_ge(S["out_done"], 16)

        @block.tensor
        def _(pe):
            w = Counts(pe)
            mm = nc.tensor.matmul
            chunk = {"base": 0, "local": 0, "i": None, "per": 0}

            @contextmanager
            def pe_loop(times, chunks, **per):
                assert chunks % SLOTS == 0
                chunk["base"] += chunk["local"]
                chunk["local"], chunk["per"] = 0, chunks
                with w.loop(times, **per) as i:
                    chunk["i"] = i
                    yield i
                assert chunk["local"] == chunks
                chunk["i"], chunk["local"] = None, 0
                chunk["base"] += chunks * times

            def take():
                n = chunk["base"] + chunk["local"]
                chunk["local"] += 1
                fill = n // SLOTS + 1
                if chunk["i"] is not None:
                    fill = chunk["i"] * (chunk["per"] // SLOTS) + fill
                pe.wait_ge(chunk_full[n % SLOTS], fill * 16)
                return RING[:, n % SLOTS, :].rearrange("p (k c) -> p k c", k=DT)

            def begun(ins):
                ins.then_inc(S["chunk_begun"], 1)

            stage = {"n": 0, "evac": "act_evac", "nb": 4}

            def begin_stage(evac, nb=4):
                if w.counted("act_evac"):
                    pe.wait_ge(S["act_evac"], w.value("act_evac"))
                if w.counted("dve_evac"):
                    pe.wait_ge(S["dve_evac"], w.value("dve_evac"))
                stage.update(n=0, evac=evac, nb=nb)

            def bank():
                n = stage["n"]
                stage["n"] += 1
                if n >= stage["nb"] or w.i is not None:
                    if w.counted(stage["evac"], stage["nb"] - 1):
                        pe.wait_ge(S[stage["evac"]], w.value(stage["evac"], stage["nb"] - 1))
                w.count(stage["evac"])
                return n % stage["nb"]

            def linear(rhs, wt):
                b = bank()
                for k in range(DT):
                    ins = mm(ps[:, b], wt[:, k], rhs(k), start=k == 0, stop=k == DT - 1)
                    if k == 0:
                        begun(ins)
                ins.then_inc(S["tile_done"], 1)

            def norm_sum(n, T, b, src, waited=False):
                for t in range(n):
                    if not waited:
                        pe.wait_ge(S["norm_sq"], w.next("norm_sq"))
                    parts = [(0, META, SEQ)] if T == SEQ else [(0, 0, HALF), (1, HALF, HALF)]
                    for h, c, width in parts:
                        ins = mm(ps[:, b + h, 0:width], ONES, src(t)[:, c:c + width], start=t == 0, stop=t == n - 1)
                ins.then_inc(S["norm_sum"], 1)

            def body():
                pe.wait_ge(S["consts"], 32)
                norm_sum(8, SEQ, 7, lambda t: HN[:, t])
                pe.wait_ge(S["norm_out"], w.next("norm_out", 8))
                hn = lambda k: HA[:, k]
                begin_stage("act_evac")
                for _ in range(6):
                    linear(hn, take())
                pe.wait_ge(S["small_in"], w.next("small_in", 16))
                w.count("dve_evac")
                b = 2
                if w.counted("act_evac", 3):
                    pe.wait_ge(S["act_evac"], w.value("act_evac", 3))
                for t in range(QT):
                    for k in range(DT):
                        ins = mm(ps[:, b, 8 * t:8 * t + 8], HA[:, k, P * t:P * t + P], WIDX[:, k],
                                 start=k == 0, stop=k == DT - 1)
                ins.then_inc(S["tile_done"], 1)
                pe.wait_ge(S["norm_sq"], w.next("norm_sq"))
                mm(ps[:, 7], ONES, R[:, 0:SEQ], start=True, stop=True).then_inc(S["norm_sum"], 1)
                pe.wait_ge(S["hot_in"], w.next("hot_in", 32))
                for j in range(2):
                    ins = mm(ps[0:HEADS, 6, 0:BIAS_W // 2] if j == 0 else ps[0:HEADS, 5, 0:BIAS_W // 2],
                             RELB, HOT[:, j * (BIAS_W // 2):(j + 1) * (BIAS_W // 2)], start=True, stop=True)
                ins.then_inc(S["bias_vec"], 1)
                if w.counted("act_evac"):
                    pe.wait_ge(S["act_evac"], w.value("act_evac"))
                for n, (t, h) in enumerate((t, h) for t in range(1, QT) for h in range(HEADS)):
                    if n == 0:
                        pe.wait_ge(S["bias_dram"], w.next("bias_dram", 1))
                    if n >= 2:
                        pe.wait_ge(S["rel_sb"], w.next("rel_sb"))
                    r = slice(HD * (h % 2), HD * (h % 2) + HD)
                    mm(ps[:, 4 + n % 2, 0:P * (t + 1)], QI[r, h // 2, P * t:P * t + P], KI[r, 0:P * (t + 1)],
                       start=True, stop=True).then_inc(S["rel_done"], 1)
                pe.wait_ge(S["rel_sb"], w.next("rel_sb", 2))
                pe.wait_ge(S["bias_rows"], w.next("bias_rows", 16))
                for h in range(HEADS):
                    if h >= 2:
                        pe.wait_ge(S["bias_flip"], w.next("bias_flip"))
                    mm(ps[:, 4 + h % 2], FLIP, BIAS_FLIPPED[:, h], start=True, stop=True).then_inc(S["flip_done"], 1)
                pe.wait_ge(S["bias_flip"], w.next("bias_flip", 2))
                begin_stage("act_evac")
                for _ in range(12):
                    linear(hn, take())
                for _ in range(4):
                    wt, b = take(), bank()
                    for t in range(QT):
                        for k in range(DT):
                            ins = mm(ps[:, b, P * t:P * t + P], HA[:, k, P * t:P * t + P], wt[:, k],
                                     start=k == 0, stop=k == DT - 1)
                            if t == k == 0:
                                begun(ins)
                    ins.then_inc(S["tile_done"], 1)
                stage["n"] = 0
                if w.counted("act_evac"):
                    pe.wait_ge(S["act_evac"], w.value("act_evac"))
                with pe_loop(2, 8, act_evac=8):
                    for _ in range(8):
                        linear(hn, take())
                pe.wait_ge(S["norm_out"], w.next("norm_out"))
                wt = take()
                for n in range(PAIRS):
                    ins = mm(ps[:, bank()], wt[:, n], CKV, start=True, stop=True)
                    ins.then_inc(S["tile_done"], 1)
                wv = wt[:, PAIRS:].rearrange("p k c -> p (k c)")
                for t in range(QT):
                    b = bank()
                    if t == 0:
                        begun(mm(ps[:, b, 0:256], CKV[:, 0:P], wv[:, 0:256], start=True, stop=True))
                        ins = mm(ps[:, b, 256:512], CKV[:, 0:P], wv[:, 256:512], start=True, stop=True)
                    else:
                        ins = mm(ps[:, b], CKV[:, P * t:P * t + P], wv, start=True, stop=True)
                    ins.then_inc(S["tile_done"], 1)
                if w.counted("act_evac"):
                    pe.wait_ge(S["act_evac"], w.value("act_evac"))
                pe_dsa()
                pe_stick()
                if w.counted("o_evac"):
                    pe.wait_ge(S["o_evac"], w.value("o_evac"))
                begin_stage("dve_evac", 4)
                for n in range(DT):
                    wt, b = take(), 2 * bank()
                    for k in range(PAIRS):
                        ins = mm(ps[:, b], wt[:, k], QA[:, k], start=k == 0, stop=k == PAIRS - 1)
                        if k == 0:
                            begun(ins)
                    for k in range(PAIRS):
                        ins = mm(ps[:, b + 1], wt[:, PAIRS + k], QB[:, k], start=k == 0, stop=k == PAIRS - 1)
                    ins.then_inc(S["tile_done"], 1)
                pe.wait_ge(S["merged"], w.next("merged", DT))
                begin_stage("dve_evac")
                for _ in range(DT):
                    linear(lambda k: MERGED[:, k], take())
                begin_stage("dve_evac")
                norm_sum(8, SEQ, 7, lambda t: HN[:, t])
                pe.wait_ge(S["norm_out"], w.next("norm_out", 8))
                pe.wait_ge(S["wr_in"], w.next("wr_in", 32))
                for t in range(QT):
                    for k in range(DT):
                        ins = mm(ps[:, 6, 36 * t:36 * t + 36], HA[:, k, P * t:P * t + P], WROUT[:, k],
                                 start=k == 0, stop=k == DT - 1)
                ins.then_inc(S["route_done"], 1)
                begin_stage("act_evac")
                for t in range(QT):
                    for j in range(2):
                        b = bank()
                        for k in range(4):
                            ins = mm(ps[:, b, P * k:P * k + P], HA[:, 4 * j + k, P * t:P * t + P], IDENT,
                                     is_transpose=True, start=True, stop=True)
                        ins.then_inc(S["tile_done"], 1)
                pe.wait_ge(S["route_ev"], w.next("route_ev"))
                for t in range(QT + 1):
                    o = ps[:, 6, EXPERTS * t:EXPERTS * t + EXPERTS]
                    for t2 in range(min(t + 1, QT)):
                        ins = mm(o, ONES, PICKED[:, t2], start=t2 == 0, stop=t == QT and t2 == QT - 1)
                    if t < QT:
                        ins = mm(o, NTRI, PICKED[:, t], start=False, stop=True)
                ins.then_inc(S["rank_done"], 1)
                pe.wait_ge(S["table_in"], w.next("table_in"))
                for j in range(2):
                    ins = mm(ps[:, 6, P * j:P * j + P], ONES, DIAGS[:, j], start=True, stop=True)
                ins.then_inc(S["table_rows"], 1)
                if w.counted("act_evac"):
                    pe.wait_ge(S["act_evac"], w.value("act_evac"))
                pe.wait_ge(S["pick_in"], w.next("pick_in", QT))
                begin_stage("act_evac")
                for k in range(DT):
                    for h in range(2):
                        b = bank()
                        for t in range(QT):
                            ins = mm(ps[:, b], HTOK[:, t, P * k:P * k + P], PICK[:, t, SEQ * h:SEQ * h + SEQ],
                                     start=t == 0, stop=t == QT - 1)
                        ins.then_inc(S["tile_done"], 1)
                pe.wait_ge(S["weigh_in"], w.next("weigh_in", QT))
                for n in range(PAIR_T):
                    b = bank()
                    for t in range(QT):
                        ins = mm(ps[:, b, P * t:P * t + P], WEIGH[:, t, P * n:P * n + P], IDENT,
                                 is_transpose=True, start=True, stop=True)
                    ins.then_inc(S["tile_done"], 1)
                if w.counted("act_evac"):
                    pe.wait_ge(S["act_evac"], w.value("act_evac"))
                pe_moe()
                begin_stage("act_evac")
                pe.wait_ge(S["dn_evac"], w.next("dn_evac", 4))
                for n in range(PAIR_T):
                    for j in range(2):
                        b = bank()
                        for k in range(4):
                            ins = mm(ps[:, b, P * k:P * k + P], YS[:, 4 * j + k, P * n:P * n + P], IDENT,
                                     is_transpose=True, start=True, stop=True)
                        ins.then_inc(S["tile_done"], 1)
                begin_stage("dve_evac")
                for k in range(DT):
                    b = bank()
                    for n in range(PAIR_T):
                        ins = mm(ps[:, b], YPAIR[:, n, P * k:P * k + P], WPAIR[:, n], start=n == 0, stop=n == PAIR_T - 1)
                    ins.then_inc(S["tile_done"], 1)
                norm_sum(8, SEQ, 7, lambda t: HN[:, t])
                pe.wait_ge(S["norm_out"], w.next("norm_out", 8))
                pe.wait_ge(S["p_in"], w.next("p_in", 16))
                begin_stage("dve_evac", 4)
                for g in range(2):
                    wp = take()
                    for n in range(4):
                        b = bank()
                        for k in range(2):
                            ins = mm(ps[:, b], wp[:, 2 * n + k], PX[:, k], start=k == 0, stop=k == 1)
                            if n == k == 0:
                                begun(ins)
                    for n in range(4):
                        wt = take()
                        for k in range(DT):
                            ins = mm(ps[:, 4 + n], wt[:, k], HA[:, k], start=k == 0, stop=k == DT - 1)
                            if k == 0:
                                begun(ins)
                        ins.then_inc(S["tile_done"], 1)
                begin_stage("dve_evac")
                norm_sum(8, SEQ, 7, lambda t: HN[:, t])
                pe.wait_ge(S["norm_out"], w.next("norm_out", 8))
                pe.wait_ge(S["meta_in"], w.next("meta_in", 16))
                begin_stage("act_evac")
                xk = lambda k: X[:, k]
                for _ in range(13):
                    linear2([take()], xk, DT)
                wt = take()
                for n in range(8):
                    if n < 4:
                        pe.wait_ge(S["lru_x"], w.next("lru_x"))
                    b = 2 * bank()
                    for h in range(2):
                        ins = mm(ps[:, b + h, 0:HALF], wt[:, n], XC[:, n % 4, HALF * h:HALF * h + HALF], start=True, stop=True)
                        if n == h == 0:
                            begun(ins)
                    ins.then_inc(S["tile_done"], 1)
                begin_stage("act_evac", 3)
                norm_sum(2, T2, 6, lambda t: R2(t))
                norm_sum(1, T2, 6, lambda t: R2(t))
                pe.wait_ge(S["norm_out"], w.next("norm_out", 3))
                for c in range(3):
                    wt = take()
                    for n in range(4):
                        b = 2 * bank()
                        for k in range(2):
                            for h in range(2):
                                ins = mm(ps[:, b + h, 0:HALF], wt[:, 2 * n + k], PQ[:, k, HALF * h:HALF * h + HALF],
                                         start=k == 0, stop=k == 1)
                                if n == k == h == 0:
                                    begun(ins)
                        ins.then_inc(S["tile_done"], 1)
                wt = take()
                for n in range(4):
                    b = 2 * bank()
                    for h in range(2):
                        ins = mm(ps[:, b + h, 0:HALF], wt[:, n], PKV[:, HALF * h:HALF * h + HALF], start=True, stop=True)
                        if n == h == 0:
                            begun(ins)
                    ins.then_inc(S["tile_done"], 1)
                wv = wt[:, 4:].rearrange("p k c -> p (k c)")
                for c, width in TOK2:
                    ins = mm(ps[0:width, 2 * bank()], PKV[:, c:c + width], wv, start=True, stop=True)
                    ins.then_inc(S["tile_done"], 1)
                begin_stage("act_evac")
                pe_mla()
                pe.wait_ge(S["lru_done"], w.next("lru_done", 4))
                begin_stage("dve_evac")
                for _ in range(8):
                    linear2([take()], lambda k: Y2[:, k], DT)
                layer_norm()
                pe_mlp()
                layer_norm()
                begin_stage("act_evac")
                for _ in range(16):
                    linear2([take()], xk, DT)
                begin_stage("act_evac")
                with pe_loop(2, 8, act_evac=8):
                    for _ in range(8):
                        wt, b = take(), 2 * bank()
                        for j, (c, width) in enumerate(TOK2):
                            o = ps[0:META, b + 1, 0:P] if j == 0 else ps[:, b, P * (j - 1):P * j]
                            for k in range(DT):
                                ins = mm(o, X[:, k, c:c + width], wt[:, k], start=k == 0, stop=k == DT - 1)
                                if j == k == 0:
                                    begun(ins)
                        ins.then_inc(S["tile_done"], 1)
                begin_stage("act_evac")
                with pe_loop(2, 8, act_evac=8):
                    for _ in range(8):
                        linear2([take()], xk, DT)
                begin_stage("act_evac")
                pe_retention()
                begin_stage("dve_evac")
                with pe_loop(2, 8, dve_evac=4):
                    for _ in range(4):
                        linear2([take, take], lambda k: RG[:, k], DT)
                layer_norm()
                pe_mlp()
                layer_norm()

            def R2(t):
                return GELU[:, t]

            def linear2(chunks, rhs, kts):
                b = 2 * bank()
                for m, wt in enumerate(chunks):
                    if callable(wt):
                        wt = wt()
                    for k in range(kts):
                        for h in range(2):
                            ins = mm(ps[:, b + h, 0:HALF], wt[:, k], rhs(m * DT + k)[:, HALF * h:HALF * h + HALF],
                                     start=m == k == 0, stop=m == len(chunks) - 1 and k == kts - 1)
                            if k == h == 0:
                                begun(ins)
                ins.then_inc(S["tile_done"], 1)

            def layer_norm():
                begin_stage("dve_evac")
                for t in range(DT):
                    for h in range(2):
                        ins = mm(ps[:, 6 + h, 0:HALF], ONES, X[:, t, HALF * h:HALF * h + HALF], start=t == 0, stop=t == DT - 1)
                ins.then_inc(S["norm_sum"], 1)
                norm_sum(8, T2, 6, lambda t: X[:, t])
                pe.wait_ge(S["ln_out"], w.next("ln_out", 8))

            def pe_mlp():
                begin_stage("act_evac")
                with pe_loop(4, 8, act_evac=8):
                    for _ in range(8):
                        linear2([take()], lambda k: X[:, k], DT)
                begin_stage("dve_evac", 2)
                pe.wait_ge(S["hidden"], w.next("hidden", 32))
                with pe_loop(4, 8, dve_evac=2):
                    for _ in range(2):
                        linear2([take] * 4, lambda k: FFH[:, k], DT)

            def pe_mla():
                units = [(h, t) for h in range(2) for t in range(5)]
                flat = ps[:, :, :].rearrange("p b c -> p (b c)")
                with w.loop(PAIRS, staged=4, smax=10, diag=10, pt=10, o_evac=1):
                    def logits(u):
                        h, t = units[u]
                        c, width = TOK2[t]
                        keys = c + width
                        r = slice(HD * h, HD * h + HD)
                        if u >= 2:
                            pe.wait_ge(S["smax"], w.next("smax"))
                            if t == 0:
                                pe.nop(nofuse=True)
                        for lo, hi in ((0, min(keys, 512)), (512, keys)):
                            if hi <= lo:
                                continue
                            o = flat[0:width, 1024 * (u % 2) + lo:1024 * (u % 2) + hi]
                            mm(o, SQN[r, c:c + width], SKN[r, lo:hi], start=True, stop=False)
                            ins = mm(o, SQP[r, c:c + width], KPE[r, lo:hi], start=False, stop=True)
                        ins.then_inc(S["logits"], 1)

                    def transposed(u):
                        h, t = units[u]
                        width = TOK2[t][1]
                        pe.wait_ge(S["diag"], w.next("diag"))
                        if t == 0:
                            pe.nop(nofuse=True)
                        for j, (kc, kw) in enumerate(TOK2[:t + 1]):
                            o = ps[0:META, 5, 0:width] if j == 0 else ps[:, 4, P * (j - 1):P * j]
                            ins = mm(o, EX2[u % 2][0:width, kc:kc + kw], DG2[u % 2][0:width, 0:width], start=True, stop=True)
                        ins.then_inc(S["tr"], 1)

                    def values(u):
                        h, t = units[u]
                        c, width = TOK2[t]
                        pe.wait_ge(S["pt"], w.next("pt"))
                        r = slice(HD * h, HD * h + HD)
                        o = ps[r, 7, 0:META] if t == 0 else ps[r, 6, P * (t - 1):P * t]
                        for j, (kc, kw) in enumerate(TOK2[:t + 1]):
                            ins = mm(o, SV2[0:kw, j, HD * h:HD * h + HD], PT2[u % 2][0:kw, j, 0:width],
                                     start=j == 0, stop=j == t)
                        return ins

                    pe.wait_ge(S["staged"], w.next("staged", 4))
                    pe.nop(nofuse=True)
                    logits(0)
                    for u in range(10):
                        if u < 9:
                            logits(u + 1)
                        if u:
                            values(u - 1)
                        transposed(u)
                    pe.wait_ge(S["smax"], w.next("smax", 2))
                    values(9).then_inc(S["o_done"], 1)
                    pe.wait_ge(S["o_evac"], w.next("o_evac"))

            def pe_retention():
                flat = ps[:, :, :].rearrange("p b c -> p (b c)")
                with w.loop(RET_HEADS, staged=2, ret_s=5, ret_used=4, ret_y=1) as i:
                    pe.wait_ge(S["staged"], w.next("staged", 2))
                    for j, (c, kw) in enumerate(TOK2):
                        if j >= 2:
                            pe.wait_ge(S["ret_s"], w.next("ret_s"))
                        for lo, hi in ((0, min(T2 - c, 512)), (512, T2 - c)):
                            if hi <= lo:
                                continue
                            o = flat[0:kw, 1024 * (j % 2) + lo:1024 * (j % 2) + hi].rearrange("p (a c) -> p a c", a=1)
                            for k in range(2):
                                ins = mm(o, SRK[:, k, c:c + kw], HN[:, ds(i * 2 + k, 1), c + lo:c + hi], start=k == 0, stop=k == 1)
                        ins.then_inc(S["logits"], 1)
                    pe.wait_ge(S["ret_s"], w.next("ret_s", 2))
                    for v in range(4):
                        if v >= 2:
                            pe.wait_ge(S["ret_used"], w.next("ret_used"))
                        for h in range(2):
                            for j, (c, kw) in enumerate(TOK2):
                                lo, hi = max(c, HALF * h), HALF * (h + 1)
                                if lo >= hi:
                                    continue
                                ins = mm(ps[:, 4 + 2 * (v % 2) + h, lo - HALF * h:HALF], SRV[0:kw, j, P * v:P * v + P],
                                         RSC[0:kw, RSC_OFF[j] + lo - c:RSC_OFF[j] + hi - c],
                                         start=j == 0, stop=True, skip_group_check=True)
                        ins.then_inc(S["ret_o"], 1)
                    pe.wait_ge(S["ret_used"], w.next("ret_used", 2))
                    norm_sum(4, T2, 0, lambda t: RSQ[:, t], waited=True)
                    pe.wait_ge(S["ret_y"], w.next("ret_y"))

            def pe_dsa():
                units = [(h, t) for h in range(2) for t in range(QT)]
                with w.loop(PAIRS, staged=3, smax=8, diag=8, pt=8, o_evac=1):
                    def logits(u):
                        h, t = units[u]
                        r = slice(HD * h, HD * h + HD)
                        if u >= 2:
                            pe.wait_ge(S["smax"], w.next("smax"))
                        mm(ps[:, u % 2, 0:P * (t + 1)], ST1[r, P * t:P * t + P], ST2[r, 0:P * (t + 1)],
                           start=True, stop=True).then_inc(S["logits"], 1)

                    def transposed(u):
                        h, t = units[u]
                        pe.wait_ge(S["diag"], w.next("diag"))
                        for k in range(t + 1):
                            ins = mm(ps[:, 2 + u % 2, P * k:P * k + P], EX[u % 2][:, P * k:P * k + P], DG[u % 2],
                                     start=True, stop=True)
                        ins.then_inc(S["tr"], 1)

                    def values(u):
                        h, t = units[u]
                        pe.wait_ge(S["pt"], w.next("pt"))
                        for k in range(t + 1):
                            ins = mm(ps[HD * h:HD * h + HD, 4, P * t:P * t + P],
                                     KI[:, P * k + HD * h:P * k + HD * h + HD], PT[u % 2][:, k],
                                     start=k == 0, stop=k == t)
                        return ins

                    pe.wait_ge(S["staged"], w.next("staged", 3))
                    logits(0)
                    for u in range(8):
                        if u < 7:
                            logits(u + 1)
                        transposed(u)
                        if u:
                            values(u - 1)
                    pe.wait_ge(S["smax"], w.next("smax", 2))
                    values(7).then_inc(S["o_done"], 1)
                    pe.wait_ge(S["o_evac"], w.next("o_evac"))

            def pe_stick():
                units = [(h, t) for h in range(2) for t in reversed(range(QT))]
                with w.loop(PAIRS, staged=3, sp_masked=8, a_masked=8, a_raw=8, o_evac=1):
                    def width(t):
                        return SEQ - P * t

                    def z(u):
                        h, t = units[u]
                        r = slice(HD * h, HD * h + HD)
                        if u >= 6:
                            pe.wait_ge(S["a_raw"], w.next("a_raw"))
                        mm(ps[:, u % 6, 0:width(t)], ST2[r, P * t:P * t + P], ST1[r, P * t:SEQ],
                           start=True, stop=True).then_inc(S["z_done"], 1)

                    def after(u):
                        h, t = units[u]
                        pe.wait_ge(S["sp_masked"], w.next("sp_masked"))
                        for t2 in range(QT - 1, t - 1, -1):
                            o = SP_OFF[t2]
                            ins = mm(ps[:, u % 6, P * (t2 - t):width(t)], NTRI if t2 == t else NONES,
                                     SPP[h][:, o:o + width(t2)], start=False, stop=True, skip_group_check=True)
                        ins.then_inc(S["c_done"], 1)

                    def values(u):
                        h, t = units[u]
                        pe.wait_ge(S["a_masked"], w.next("a_masked"))
                        return mm(ps[HD * h:HD * h + HD, 6, P * t:SEQ], ST3[:, P * t + HD * h:P * t + HD * h + HD],
                                  SPA[u % 2][:, 0:width(t)], start=t == QT - 1, stop=True, skip_group_check=True)

                    pe.wait_ge(S["staged"], w.next("staged", 3))
                    for u in range(4):
                        z(u)
                    for u in range(8):
                        if u + 4 < 8:
                            z(u + 4)
                        after(u)
                        if u:
                            values(u - 1)
                    values(7).then_inc(S["o_done"], 1)
                    pe.wait_ge(S["a_raw"], w.next("a_raw", 6))
                    pe.wait_ge(S["o_evac"], w.next("o_evac"))

            def pe_moe():
                def gate_up(n):
                    pe.wait_ge(S["tokens_in"], w.next("tokens_in"))
                    for m in range(2):
                        for f in range(2):
                            wt = take()
                            for k in range(DT):
                                ins = mm(ps[:, 2 * m + n % 2, P * f:P * f + P], wt[:, k], XW[n % 2][:, k],
                                         start=k == 0, stop=k == DT - 1)
                                if k == 0:
                                    begun(ins)
                        ins.then_inc(S["gu_done"], 1)

                def down(n):
                    pe.wait_ge(S["hid"], w.next("hid"))
                    for h in range(2):
                        if n >= 2:
                            pe.wait_ge(S["dn_evac"], w.next("dn_evac"))
                        wt = take()
                        for j in range(4):
                            for k in range(2):
                                ins = mm(ps[:, 4 + 2 * (n % 2) + h, P * j:P * j + P], wt[:, 2 * j + k], HID[n % 2][:, k],
                                         start=k == 0, stop=k == 1)
                                if j == k == 0:
                                    begun(ins)
                        ins.then_inc(S["dn_done"], 1)

                gate_up(0)
                for n in (1, 2):
                    gate_up(n)
                    down(n - 1)
                with pe_loop((WINDOWS - 3) // 4, 24, tokens_in=4, hid=4, dn_evac=8):
                    for n in range(3, 7):
                        gate_up(n)
                        down(n - 1)
                down(WINDOWS - 1)

            body()

        @block.scalar
        def _(act):
            w = Counts(act)
            fn = nc.scalar.activation

            def step(ins):
                ins.then_inc(S["act_ops"], 1)
                act.wait_ge(S["act_ops"], w.next("act_ops"))

            def squares(n, src, dst):
                for t in range(n):
                    fn(dst(t), src(t), ACT.Square).then_inc(S["norm_sq"], 1)

            def deviation(v):
                act.wait_ge(S["norm_var"], w.next("norm_var"))
                fn(v, v, ACT.Sqrt).then_inc(S["norm_sd"], 1)

            def evac(out, in_, f=ACT.Copy, **kw):
                act.wait_ge(S["tile_done"], w.next("tile_done"))
                fn(out, in_, f, **kw).then_inc(S["act_evac"], 1)

            def bank(n, nb=4):
                return ps[:, n % nb]

            def body():
                R1 = R[:, 0:SEQ]
                act.wait_ge(S["x_in"], 16)
                act.wait_ge(S["consts"], 32)
                step(fn(LAM[:, 0:4], V[:, VEC_AT["lam"]:VEC_AT["lam"] + 4], ACT.Abs))
                fn(LAM[:, 0:4], LAM[:, 0:4], ACT.Exp, scale=-1.0).then_inc(S["lam_exp"], 1)
                squares(8, lambda t: XA[:, t], lambda t: HA[:, t])
                deviation(R1)
                for n, out in enumerate([CKV, KI] + [QI[:, j] for j in range(4)]):
                    evac(out, bank(n))
                if w.counted("tile_done"):
                    act.wait_ge(S["tile_done"], w.value("tile_done"))
                w.count("tile_done")
                squares(1, lambda t: CKV, lambda t: R1)
                deviation(R1)
                act.wait_ge(S["bias_vec"], w.next("bias_vec"))
                fn(BVEC[:, 0:BIAS_W // 2], ps[0:HEADS, 6, 0:BIAS_W // 2], ACT.Copy)
                fn(BVEC[:, BIAS_W // 2:], ps[0:HEADS, 5, 0:BIAS_W // 2], ACT.Copy).then_inc(S["bias_dram"], 1)
                for n, (t, h) in enumerate((t, h) for t in range(1, QT) for h in range(HEADS)):
                    act.wait_ge(S["rel_done"], w.next("rel_done"))
                    if n >= 2:
                        act.wait_ge(S["rel_used"], w.next("rel_used"))
                    fn(LG[n % 2][:, 0:P * (t + 1)], ps[:, 4 + n % 2, 0:P * (t + 1)], ACT.Relu).then_inc(S["rel_sb"], 1)
                w.count("rel_used", 2)
                for h in range(HEADS):
                    act.wait_ge(S["flip_done"], w.next("flip_done"))
                    fn(BIAS[:, h], ps[:, 4 + h % 2], ACT.Copy).then_inc(S["bias_flip"], 1)
                n = 0
                for j in range(4):
                    evac(QA[:, j], bank(n + j), scale=QK_SCALE)
                for j in range(4):
                    evac(QB[:, j], bank(n + 4 + j), scale=QK_SCALE)
                for j in range(4):
                    evac(KB[:, j], bank(n + 8 + j))
                for j in range(4):
                    evac(VB[:, :, P * j:P * j + P], bank(n + 12 + j).rearrange("p (t c) -> p t c", t=QT))
                with w.loop(2, tile_done=8) as i:
                    for j in range(8):
                        evac(GATES[:, ds(i * 8 + j, 1), :], ps[:, j % 4:j % 4 + 1], ACT.Sigmoid)
                for j in range(PAIRS):
                    evac(KA[:, j], bank(j))
                for t in range(QT):
                    evac(VA[:, t], bank(t))
                softmax_pairs(PAIRS, [t for _ in range(2) for t in range(QT)], [(P * (t + 1), P) for t in range(QT)],
                              LG, EX, 1.0, copy_first)
                act_stick()
                w.count("tile_done", 16)
                act.wait_ge(S["dve_evac"], w.next("dve_evac", 1 + 16))
                squares(8, lambda t: XA[:, t], lambda t: HA[:, t])
                deviation(R1)
                act.wait_ge(S["route_e"], w.next("route_e"))
                fn(SMALL[:, 176:192], SMALL[:, 176:192], ACT.Exp).then_inc(S["route_x"], 1)
                for n in range(2 * QT):
                    evac(HTOK[:, n // 2, 512 * (n % 2):512 * (n % 2) + 512], bank(n))
                act.wait_ge(S["route_e"], w.next("route_e"))
                fn(SMALL[:, 200:204], SMALL[:, 200:204], ACT.Exp).then_inc(S["route_x"], 1)
                for n in range(2 * DT):
                    evac(XS[:, n // 2, SEQ * (n % 2):SEQ * (n % 2) + SEQ], bank(n))
                for n in range(PAIR_T):
                    evac(WPAIR[:, n], bank(n))

                act.wait_ge(S["table"], w.next("table"))
                act.wait_ge(S["pad_in"], w.next("pad_in"))
                if w.counted("act_evac"):
                    act.wait_ge(S["act_evac"], w.value("act_evac"))

                def tokens(n, at):
                    first = act.value_load(WTAB[:, at], min_val=0, max_val=PAIRED)
                    if n >= 2:
                        act.wait_ge(S["gu_done"], w.next("gu_done"))
                    fn(XW[n % 2], XS[:, :, ds(first, P)], ACT.Copy).then_inc(S["tokens_in"], 1)

                def silu(n):
                    act.wait_ge(S["gu_done"], w.next("gu_done"))
                    if n >= 2:
                        act.wait_ge(S["hid"], w.next("hid"))
                    fn(SILU[n % 2], ps[:, n % 2, 0:2 * P].rearrange("p (f c) -> p f c", f=2), ACT.Silu).then_inc(S["sg"], 1)

                tokens(0, slice(TAB, TAB + 1))
                for n in range(2):
                    tokens(n + 1, slice(TAB + n + 1, TAB + n + 2))
                    silu(n)
                with w.loop((WINDOWS - 3) // 4, gu_done=8, hid=4) as i:
                    for n in range(2, 6):
                        tokens(n + 1, ds(i * 4 + (TAB + n + 1), 1))
                        silu(n)
                act.wait_ge(S["gu_done"], w.next("gu_done"))
                silu(WINDOWS - 1)
                w.count("gu_done")
                for n in range(2 * PAIR_T):
                    evac(YPAIR[:, n // 2, 512 * (n % 2):512 * (n % 2) + 512], bank(n))
                w.count("tile_done", DT)
                act.wait_ge(S["dve_evac"], w.next("dve_evac", DT))
                squares(8, lambda t: XA[:, t], lambda t: HA[:, t])
                deviation(R1)
                for n in range(8):
                    act.wait_ge(S["tile_done"], w.next("tile_done"))
                    fn(SG2[n % 2], ps[:, 4 + n % 4], ACT.Sigmoid).then_inc(S["sg"], 1)
                    if n >= 1:
                        act.wait_ge(S["dve_evac"], w.next("dve_evac"))
                act.wait_ge(S["dve_evac"], w.next("dve_evac"))
                squares(8, lambda t: XA[:, t], lambda t: HA[:, t])
                deviation(R1)
                ev = [PG[:, j] for j in range(4)] + [PREC[:, j, 3:] for j in range(4)] + [PQ[:, j] for j in range(2)] + [PKV, KPE, KPW]
                act.wait_ge(S["norm_out"], w.next("norm_out", 8 + 1 + 24))
                for n, out in enumerate(ev):
                    evac(two(out), halves(2 * (n % 4)))
                for n in range(8):
                    out, bias = (RA, "b_rg_a") if n < 4 else (RX, "b_rg_x")
                    evac(two(out[:, n % 4]), halves(2 * ((n + 13) % 4)), ACT.Sigmoid, bias=vec(bias, n % 4))
                act_lru()
                squares(2, lambda t: PQ[:, t], lambda t: GELU[:, t])
                deviation(R[:, :])
                act.wait_ge(S["norm_out"], w.next("norm_out", 2))
                squares(1, lambda t: PKV, lambda t: GELU[:, t])
                deviation(R[:, :])
                act.wait_ge(S["norm_out"], w.next("norm_out", 1))
                for n, out in enumerate([QN[:, j] for j in range(4)] + [QP[:, j] for j in range(4)] + [QW[:, j] for j in range(4)]
                                        + [KN[:, j] for j in range(4)]):
                    evac(two(out), halves(2 * (n % 3)))
                for j, (c, width) in enumerate(TOK2):
                    evac(V2[0:width, j], ps[0:width, 2 * ((16 + j) % 3)])
                softmax_pairs(PAIRS, [t for _ in range(2) for t in range(5)], [(c + width, width) for c, width in TOK2],
                              LG2, EX2, MLA_SCALE, copy_second)
                w.count("tile_done", 8)
                act.wait_ge(S["dve_evac"], w.next("dve_evac", 8))
                layer_norm("mix", 0)
                mlp(0)
                for n in range(8):
                    evac(two(HN[:, n]), halves(2 * (n % 4)))
                for n in range(8):
                    evac(two(RK[:, n]), halves(2 * (n % 4)), scale=1.0 / 16)
                with w.loop(2, tile_done=8) as i:
                    for n in range(8):
                        act.wait_ge(S["tile_done"], w.next("tile_done"))
                        b = 2 * (n % 4)
                        fn(RV[:, 1:5, ds(i * 1024 + P * n, P)], ps[:, b].rearrange("p (t c) -> p t c", t=4), ACT.Copy)
                        fn(RV[0:META, 0, ds(i * 1024 + P * n, P)], ps[0:META, b + 1, 0:P], ACT.Copy).then_inc(S["act_evac"], 1)
                with w.loop(2, tile_done=8) as i:
                    for n in range(8):
                        act.wait_ge(S["tile_done"], w.next("tile_done"))
                        b = 2 * (n % 4)
                        fn(RG[:, ds(i * 8 + n, 1), :].rearrange("p a (h c) -> p (a h) c", h=2), halves(b), ACT.Silu).then_inc(S["act_evac"], 1)
                with w.loop(RET_HEADS, ret_o=4, norm_var=1, ret_y=1):
                    for v in range(4):
                        act.wait_ge(S["ret_o"], w.next("ret_o"))
                        b = 4 + 2 * (v % 2)
                        fn(two(ROT[:, v]), halves(b), ACT.Copy)
                        fn(two(RSQ[:, v]), halves(b), ACT.Square).then_inc(S["ret_used"], 1)
                    deviation(R[:, :])
                    act.wait_ge(S["ret_y"], w.next("ret_y"))
                w.count("tile_done", 8)
                act.wait_ge(S["dve_evac"], w.next("dve_evac", 8))
                layer_norm("mix", 1)
                mlp(1)

            def copy_first(u, t):
                fn(PT[u % 2][:, 0:t + 1], ps[:, 2 + u % 2, 0:P * (t + 1)].rearrange("p (k c) -> p k c", k=t + 1),
                   ACT.Copy).then_inc(S["pt"], 1)

            def copy_second(u, t):
                width = TOK2[t][1]
                ins = fn(PT2[u % 2][0:META, 0, 0:width], ps[0:META, 5, 0:width], ACT.Copy)
                if t:
                    ins = fn(PT2[u % 2][:, 1:t + 1], ps[:, 4, 0:P * t].rearrange("p (k c) -> p k c", k=t), ACT.Copy)
                ins.then_inc(S["pt"], 1)

            def softmax_pairs(pairs, order, sizes, lg, ex, scale, copy):
                n = len(order)
                with w.loop(pairs, smax=n, tr=n, act_ops=n, o_done=1) as i:
                    def exponentials(u):
                        keys, rows = sizes[order[u]]
                        act.wait_ge(S["smax"], w.next("smax"))
                        st = SMALL[0:rows, 8 * (u % 2):8 * (u % 2) + 8]
                        step(nc.scalar.mul(st[:, 1:2], st[:, 0:1], -scale))
                        fn(ex[u % 2][0:rows, 0:keys], lg[u % 2][0:rows, 0:keys], ACT.Exp, bias=st[:, 1:2], scale=scale,
                           accum_out=st[:, 2:3]).then_inc(S["expd"], 1)

                    exponentials(0)
                    for u in range(n):
                        if u + 1 < n:
                            exponentials(u + 1)
                        act.wait_ge(S["tr"], w.next("tr"))
                        copy(u, order[u])
                    act.wait_ge(S["o_done"], w.next("o_done"))
                    if copy is copy_first:
                        fn(QA[:, ds(i, 1), :], ps[:, 4:5], ACT.Copy).then_inc(S["o_evac"], 1)
                    else:
                        fn(Y2[:, ds(i + 4, 1), META:], ps[:, 6:7], ACT.Copy)
                        fn(Y2[:, ds(i + 4, 1), 0:META], ps[:, 7:8, 0:META], ACT.Copy).then_inc(S["o_evac"], 1)

            def act_stick():
                units = [(h, t) for h in range(2) for t in reversed(range(QT))]
                nc.scalar.preload_act_table_set("natural_log_exp_and_others")
                with w.loop(PAIRS, z_done=8, act_ops=16, sp=8, c_done=8, o_done=1) as i:
                    def soft(u):
                        h, t = units[u]
                        m = SPT[u % 2][:, 0:SEQ - P * t]
                        act.wait_ge(S["z_done"], w.next("z_done"))
                        if u >= 2:
                            act.wait_ge(S["sp"], w.next("sp"))
                        step(fn(m, ps[:, u % 6, 0:SEQ - P * t], ACT.Abs))
                        step(fn(m, m, ACT.Exp, scale=-1.0))
                        fn(m, m, ACT.Ln, bias=1.0).then_inc(S["soft"], 1)

                    def weights(u):
                        h, t = units[u]
                        act.wait_ge(S["c_done"], w.next("c_done"))
                        fn(SPA[u % 2][:, 0:SEQ - P * t], ps[:, u % 6, 0:SEQ - P * t], ACT.Exp).then_inc(S["a_raw"], 1)

                    soft(0)
                    soft(1)
                    for u in range(8):
                        if u + 2 < 8:
                            soft(u + 2)
                        weights(u)
                    act.wait_ge(S["sp"], w.next("sp", 2))
                    act.wait_ge(S["o_done"], w.next("o_done"))
                    fn(QB[:, ds(i, 1), :], ps[:, 6:7], ACT.Copy).then_inc(S["o_evac"], 1)

            def act_lru():
                for j in range(4):
                    act.wait_ge(S["lru_r"], w.next("lru_r"))
                    fn(LRU_T[:, j], RA[:, j], ACT.Tanh)
                    fn(RA[:, j], RA[:, j], ACT.Exp, scale=-1.0).then_inc(S["lru_t"], 1)
                for j in range(4):
                    act.wait_ge(S["gelu_in"], w.next("gelu_in"))
                    fn(GELU[:, j], GELU[:, j], ACT.Tanh, scale=math.sqrt(2 / math.pi)).then_inc(S["gelu_th"], 1)
                for j in range(4):
                    act.wait_ge(S["lru_r"], w.next("lru_r"))
                    fn(LRU_T[:, j], LRU_T[:, j], ACT.Sqrt).then_inc(S["lru_t"], 1)
                act.wait_ge(S["lru_done"], w.next("lru_done", 4))

            def layer_norm(kind, l):
                for t in range(DT):
                    act.wait_ge(S["ln_cent"], w.next("ln_cent"))
                    fn(X[:, t], HN[:, t], ACT.Square).then_inc(S["norm_sq"], 1)
                deviation(R[:, :])
                for t in range(DT):
                    act.wait_ge(S["norm_out"], w.next("norm_out"))
                    fn(X[:, t], HN[:, t], ACT.Identity, bias=vec(f"ln_{kind}_b", 8 * l + t)).then_inc(S["ln_out"], 1)

            def mlp(l):
                with w.loop(4, tile_done=8) as i:
                    for n in range(8):
                        act.wait_ge(S["tile_done"], w.next("tile_done"))
                        fn(FFH[:, ds(i * 8 + n, 1), :].rearrange("p a (h c) -> p (a h) c", h=2), halves(2 * (n % 4)),
                           ACT.Relu).then_inc(S["act_evac"], 1)
                w.count("tile_done", 8)
                act.wait_ge(S["dve_evac"], w.next("dve_evac", 8))
                layer_norm("mlp", l)

            SG2 = [area(1024, 512), area(1536, 512)]
            body()

        @block.vector
        def _(dve):
            w = Counts(dve)
            v = nc.vector

            def step(ins):
                ins.then_inc(S["dve_ops"], 1)
                dve.wait_ge(S["dve_ops"], w.next("dve_ops"))

            def bc(x, *shape):
                return x.unsqueeze(2).to_broadcast([P, *shape])

            def inverse_deviation(T, dim, eps, b):
                pv, rv = (ps[:, 7], R[:, 0:SEQ]) if T == SEQ else (halves(6), two(R[:, :]))
                dve.wait_ge(S["norm_sum"], w.next("norm_sum"))
                v.tensor_scalar(rv, pv, 1.0 / dim, eps, ALU.mult, ALU.add).then_inc(S["norm_var"], 1)
                dve.wait_ge(S["norm_sd"], w.next("norm_sd"))
                step(v.reciprocal(R[:, 0:T], R[:, 0:T]))

            def rms(n, T, dim, eps, gain, src, dst):
                inverse_deviation(T, dim, eps, 7)
                for t in range(n):
                    v.scalar_tensor_tensor(out=dst(t), in0=src(t), scalar=vec(gain, t), in1=R[:, 0:T],
                                           op0=ALU.mult, op1=ALU.mult).then_inc(S["norm_out"], 1)

            def accumulate(out, in_, scale):
                if scale == 1.0:
                    ins = v.tensor_tensor(out, out, in_, ALU.add)
                else:
                    ins = v.scalar_tensor_tensor(out=out, in0=out, scalar=scale, in1=in_, op0=ALU.mult, op1=ALU.add)
                ins.then_inc(S["dve_evac"], 1)

            def layer_norm(kind, l):
                dve.wait_ge(S["norm_sum"], w.next("norm_sum"))
                step(v.tensor_scalar(two(R[:, :]), halves(6), 1.0 / D, None, ALU.mult))
                for t in range(DT):
                    v.tensor_tensor(HN[:, t], X[:, t], R[:, :], ALU.subtract).then_inc(S["ln_cent"], 1)
                inverse_deviation(T2, D, EPS2, 6)
                for t in range(DT):
                    v.scalar_tensor_tensor(out=HN[:, t], in0=HN[:, t], scalar=vec(f"ln_{kind}_g", 8 * l + t), in1=R[:, :],
                                           op0=ALU.mult, op1=ALU.mult).then_inc(S["norm_out"], 1)

            def body():
                dve.wait_ge(S["consts"], 32)
                rms(8, SEQ, D, EPS1, "attn_norm", lambda t: XA[:, t], lambda t: HA[:, t])
                w.count("tile_done", 6)
                dve.wait_ge(S["tile_done"], w.next("tile_done"))
                v.tensor_scalar(WI, ps[:, 2, 0:32], IDX_SCALE, None, ALU.mult).then_inc(S["dve_evac"], 1)
                dve.wait_ge(S["dve_evac"], w.next("dve_evac"))
                rms(1, SEQ, KV_RANK, EPS1, "kv_norm", lambda t: CKV, lambda t: CKV)
                for t in range(1, QT):
                    for h in range(HEADS):
                        dve.wait_ge(S["rel_sb"], w.next("rel_sb"))
                        rel, scalar = LG[((t - 1) * HEADS + h) % 2][:, 0:P * (t + 1)], WI[:, 8 * t + h:8 * t + h + 1]
                        if h == 0:
                            ins = v.tensor_scalar(SCORES[t], rel, scalar, None, ALU.mult)
                        else:
                            ins = v.scalar_tensor_tensor(out=SCORES[t], in0=rel, scalar=scalar, in1=SCORES[t],
                                                         op0=ALU.mult, op1=ALU.add)
                        ins.then_inc(S["rel_used"], 1)
                        dve.wait_ge(S["rel_used"], w.next("rel_used"))
                dve.wait_ge(S["bias_rows"], w.next("bias_rows", 16))
                top = SMALL[:, 16:24]
                for t in range(1, QT):
                    dve.wait_ge(S["score_cut"], w.next("score_cut"))
                    for _ in range(N_SEL // 8):
                        step(v.max(top, SCORES[t]))
                        step(v.match_replace(out=SCORES[t], in_to_replace=top, in_values=SCORES[t], imm_value=TAKEN))
                    step(v.tensor_scalar(MASKS[t], SCORES[t], TAKEN, NEG, ALU.not_equal, ALU.mult))
                dve.wait_ge(S["act_evac"], w.next("act_evac", 46))
                dve.wait_ge(S["score_mask"], w.next("score_mask"))
                dve.wait_ge(S["bias_flip"], w.next("bias_flip", 8))
                softmax_pairs(PAIRS, [t for _ in range(2) for t in range(QT)], stage_first, maximum_first,
                              DG, [P] * QT, 3, 2 * 8)
                dve_stick()
                w.count("tile_done", 46 - 6)
                dve.wait_ge(S["o_evac"], w.next("o_evac", 8))
                for n in range(DT):
                    dve.wait_ge(S["tile_done"], w.next("tile_done"))
                    b = 2 * (n % 4)
                    v.tensor_tensor(GATES[:, n], GATES[:, n], ps[:, b], ALU.mult)
                    v.tensor_tensor(GATES[:, DT + n], GATES[:, DT + n], ps[:, b + 1], ALU.mult).then_inc(S["dve_evac"], 1)
                for n in range(DT):
                    dve.wait_ge(S["tile_done"], w.next("tile_done"))
                    accumulate(XA[:, n], ps[:, n % 4], 1.0)
                dve.wait_ge(S["dve_evac"], w.next("dve_evac", 16))
                rms(8, SEQ, D, EPS1, "ffn_norm", lambda t: XA[:, t], lambda t: HA[:, t])
                router()
                dve_moe()
                rms(8, SEQ, D, EPS1, "ple_norm", lambda t: XA[:, t], lambda t: HA[:, t])
                for n in range(DT):
                    dve.wait_ge(S["tile_done"], w.next("tile_done"))
                    dve.wait_ge(S["sg"], w.next("sg"))
                    step(v.tensor_tensor(HT[n % 2], SG[n % 2], ps[:, n % 4], ALU.mult))
                    accumulate(XA[:, n], HT[n % 2], 1.0)
                dve.wait_ge(S["dve_evac"], w.next("dve_evac", 8))
                rms(8, SEQ, D, EPS1, "final_norm", lambda t: XA[:, t], lambda t: XA[:, t])
                dve_lru()
                rms(2, T2, 256, EPS2, "q_norm", lambda t: PQ[:, t], lambda t: PQ[:, t])
                rms(1, T2, 128, EPS2, "kv_norm2", lambda t: PKV, lambda t: PKV)
                dve.wait_ge(S["c2_in"], w.next("c2_in", 48))
                dve.wait_ge(S["act_evac"], w.next("act_evac", 4 + 8))
                for x, swapped in [(QP[:, j], QW[:, j]) for j in range(4)] + [(KPE, KPW)]:
                    v.tensor_tensor(x, x, ROPE_C, ALU.mult)
                    step(v.tensor_tensor(swapped, swapped, ROPE_S, ALU.mult))
                    step(v.tensor_tensor(x, x, swapped, ALU.add))
                dve.wait_ge(S["act_evac"], w.next("act_evac", 4 + 5))
                softmax_pairs(PAIRS, [t for _ in range(2) for t in range(5)], stage_second, maximum_second,
                              DG2, [width for _, width in TOK2], 4, 10)
                w.count("tile_done", 13 + 8 + 16 + 5)
                for n in range(DT):
                    dve.wait_ge(S["tile_done"], w.next("tile_done"))
                    accumulate(two(X[:, n]), halves(2 * (n % 4)), ALPHA)
                layer_norm("mix", 0)
                mlp(0)
                dve.wait_ge(S["c3_in"], w.next("c3_in", 48))
                for x in (HN, RK):
                    for h in range(RET_HEADS):
                        dve.wait_ge(S["act_evac"], w.next("act_evac", 2))
                        x1, x2, t1, t2 = x[:, 2 * h], x[:, 2 * h + 1], SRK[:, 0], SRK[:, 1]
                        v.tensor_tensor(t1, x1, SIN, ALU.mult)
                        step(v.tensor_tensor(t2, x2, SIN, ALU.mult))
                        v.tensor_tensor(x1, x1, COS, ALU.mult)
                        step(v.tensor_tensor(x2, x2, COS, ALU.mult))
                        v.tensor_tensor(x1, x1, t2, ALU.subtract)
                        step(v.tensor_tensor(x2, x2, t1, ALU.add))
                dve.wait_ge(S["act_evac"], w.next("act_evac", 32))
                flat = ps[:, :, :].rearrange("p b c -> p (b c)")
                if w.counted("staged"):
                    dve.wait_ge(S["staged"], w.value("staged"))
                with w.loop(RET_HEADS, logits=5, norm_sum=1, norm_sd=1, dve_ops=5, ret_y=1) as i:
                    v.tensor_copy(SRK, RK[:, ds(i * 2, 2), :]).then_inc(S["staged"], 1)
                    v.tensor_copy(SRV[:, 1:5], RV[:, 1:5, ds(i * 512, 512)])
                    v.tensor_copy(SRV[0:META, 0], RV[0:META, 0, ds(i * 512, 512)]).then_inc(S["staged"], 1)
                    for j, (c, kw) in enumerate(TOK2):
                        dve.wait_ge(S["logits"], w.next("logits"))
                        lo = 1024 * (j % 2)
                        v.tensor_tensor(RSC[0:kw, RSC_OFF[j]:RSC_OFF[j] + T2 - c].unsqueeze(1),
                                        flat[0:kw, lo:lo + T2 - c].unsqueeze(1),
                                        DECAY[0:kw, ds(i, 1), 0:T2 - c], ALU.mult).then_inc(S["ret_s"], 1)
                    dve.wait_ge(S["norm_sum"], w.next("norm_sum"))
                    v.tensor_scalar(two(R[:, :]), ps[:, 0:2, 0:HALF], 1.0 / 512, EPS2, ALU.mult, ALU.add).then_inc(S["norm_var"], 1)
                    dve.wait_ge(S["norm_sd"], w.next("norm_sd"))
                    step(v.reciprocal(R[:, :], R[:, :]))
                    for n in range(4):
                        step(v.tensor_tensor(ROT[:, n], ROT[:, n], R[:, :], ALU.mult))
                        g = RG[:, ds(i * 4 + n, 1), :]
                        ins = v.tensor_tensor(g, g, ROT[:, n:n + 1], ALU.mult)
                    ins.then_inc(S["ret_y"], 1)
                    dve.wait_ge(S["ret_y"], w.next("ret_y"))
                w.count("tile_done", 48)
                with w.loop(2, tile_done=4) as i:
                    for n in range(4):
                        dve.wait_ge(S["tile_done"], w.next("tile_done"))
                        accumulate(X[:, ds(i * 4 + n, 1), :].rearrange("p a (h c) -> p (a h) c", h=2), halves(2 * n), ALPHA)
                layer_norm("mix", 1)
                mlp(1)

            def mlp(l):
                with w.loop(4, act_evac=8) as i:
                    for n in range(8):
                        dve.wait_ge(S["act_evac"], w.next("act_evac"))
                        f = FFH[:, ds(i * 8 + n, 1), :]
                        v.tensor_tensor(f, f, f, ALU.mult).then_inc(S["hidden"], 1)
                w.count("tile_done", 32)
                with w.loop(4, tile_done=2) as i:
                    for n in range(2):
                        dve.wait_ge(S["tile_done"], w.next("tile_done"))
                        accumulate(X[:, ds(i * 2 + n, 1), :].rearrange("p a (h c) -> p (a h) c", h=2), halves(2 * n), ALPHA)
                layer_norm("mlp", l)

            def stage_first(i):
                for out, src in ((ST1, QA), (ST2, KA)):
                    v.tensor_copy(out.unsqueeze(1), src[:, ds(i, 1), :]).then_inc(S["staged"], 1)
                v.tensor_copy(KI.rearrange("p (t c) -> p t c", t=QT), VA[:, :, ds(i * P, P)]).then_inc(S["staged"], 1)

            def stage_second(i):
                for out, src in ((SQN, QN), (SQP, QP), (SKN, KN)):
                    v.tensor_copy(out.unsqueeze(1), src[:, ds(i, 1), :]).then_inc(S["staged"], 1)
                v.tensor_copy(SV2[0:META, 0], V2[0:META, 0, ds(i * P, P)])
                v.tensor_copy(SV2[:, 1:5], V2[:, 1:5, ds(i * P, P)]).then_inc(S["staged"], 1)

            def settle(ins=None):
                if ins is not None:
                    step(ins)
                v.nop(nofuse=True)

            def maximum_first(i, u, h, t):
                keys = P * (t + 1)
                lg = LG[u % 2][:, 0:keys]
                settle(v.tensor_tensor(lg.unsqueeze(1), ps[:, u % 2:u % 2 + 1, 0:keys],
                                     BIAS[:, ds(i * 2 + h, 1), SEQ - keys:SEQ], ALU.add))
                v.tensor_tensor_reduce(out=lg, in0=lg, in1=MASKS[t], scale=1.0, scalar=TAKEN, op0=ALU.add, op1=ALU.max,
                                       accum_out=SMALL[:, 8 * (u % 2):8 * (u % 2) + 1]).then_inc(S["smax"], 1)

            def maximum_second(i, u, h, t):
                c, rows = TOK2[t]
                keys = c + rows
                flat = ps[:, :, :].rearrange("p b c -> p (b c)")
                first = T2 - P if t == 0 else T2 - keys
                settle()
                v.tensor_tensor_reduce(out=LG2[u % 2][0:rows, 0:keys], in0=flat[0:rows, 1024 * (u % 2):1024 * (u % 2) + keys],
                                       in1=MASKW[0:rows, first:first + keys], scale=1.0, scalar=TAKEN, op0=ALU.add,
                                       op1=ALU.max, accum_out=SMALL[0:rows, 8 * (u % 2):8 * (u % 2) + 1]).then_inc(S["smax"], 1)

            def softmax_pairs(pairs, order, stage, maximum, dg, rows_of, n_staged, steps):
                n = len(order)
                with w.loop(pairs, logits=n, expd=n, dve_ops=steps, o_done=1) as i:
                    stage(i)
                    def largest(u):
                        dve.wait_ge(S["logits"], w.next("logits"))
                        maximum(i, u, u // (n // 2), order[u])

                    def scale(u):
                        rows = rows_of[order[u]]
                        st = SMALL[0:rows, 8 * (u % 2):8 * (u % 2) + 8]
                        dve.wait_ge(S["expd"], w.next("expd"))
                        step(v.reciprocal(st[:, 3:4], st[:, 2:3]))
                        v.tensor_scalar(dg[u % 2][0:rows, 0:rows], IDENT[0:rows, 0:rows], st[:, 3:4], None, ALU.mult)\
                            .then_inc(S["diag"], 1)

                    largest(0)
                    for u in range(n):
                        if u + 1 < n:
                            largest(u + 1)
                        scale(u)
                    dve.wait_ge(S["o_done"], w.next("o_done"))

            def dve_stick():
                units = [(h, t) for h in range(2) for t in reversed(range(QT))]
                with w.loop(PAIRS, soft=8, o_done=1) as i:
                    for out, src in ((ST1, QB), (ST2, KB)):
                        v.tensor_copy(out.unsqueeze(1), src[:, ds(i, 1), :]).then_inc(S["staged"], 1)
                    v.tensor_copy(ST3.rearrange("p (t c) -> p t c", t=QT), VB[:, :, ds(i * P, P)]).then_inc(S["staged"], 1)
                    for u, (h, t) in enumerate(units):
                        width = SEQ - P * t
                        dve.wait_ge(S["soft"], w.next("soft"))
                        v.scalar_tensor_tensor(out=SPP[h][:, SP_OFF[t]:SP_OFF[t] + width], in0=ps[:, u % 6, 0:width], scalar=0.0,
                                               in1=SPT[u % 2][:, 0:width], op0=ALU.max, op1=ALU.add).then_inc(S["sp"], 1)
                    dve.wait_ge(S["o_done"], w.next("o_done"))

            def first_of(eq, onehot, run):
                step(v.tensor_copy(run, eq[:, :, 0]))
                step(v.tensor_copy(onehot[:, :, 0], eq[:, :, 0]))
                for j in range(1, eq.shape[2]):
                    step(v.tensor_tensor(onehot[:, :, j], eq[:, :, j], run, ALU.is_gt))
                    step(v.tensor_tensor(run, run, eq[:, :, j], ALU.max))

            def small(off, *shape):
                n = int(np.prod(shape))
                x = SMALL[:, off:off + n]
                return x.rearrange("p (a b) -> p a b", a=shape[0]) if len(shape) == 2 else x

            def router():
                lt, gm, sh, eq = small(16, 4, 36), small(160, 4), small(176, 4, 4), small(204, 4, 4)
                run, oh, es = small(220, 4), small(224, 4, 4), small(240, 4, 8)
                prod = SMALL[:, 288:416].rearrange("p (t g e) -> p t g e", t=4, g=4)
                m1, m2, pg, diff = small(164, 4), small(168, 4), small(172, 4), small(200, 4)
                w1, w2 = small(272, 4), small(276, 4)
                dve.wait_ge(S["route_done"], w.next("route_done"))
                dve.wait_ge(S["wr_in"], w.next("wr_in", 32))
                step(v.tensor_tensor(lt, ps[:, 6, 0:144].rearrange("p (t c) -> p t c", t=4), BR, ALU.add))
                g = lt[:, :, 0:4]
                step(v.tensor_reduce(gm, g, AX, ALU.max))
                v.tensor_tensor(sh, g, bc(gm, 4, 4), ALU.subtract).then_inc(S["route_e"], 1)
                step(v.tensor_tensor(eq, g, bc(gm, 4, 4), ALU.is_equal))
                first_of(eq, oh, run)
                for n in range(GROUPS):
                    step(v.tensor_tensor(prod[:, :, n], lt[:, :, 4 + 8 * n:12 + 8 * n],
                                         oh[:, :, n].unsqueeze(2).to_broadcast([P, 4, 8]), ALU.mult))
                step(v.tensor_reduce(es, prod.rearrange("p t g e -> p t e g"), AX, ALU.add))
                eq8, oh1, oh2, es2 = small(16, 4, 8), small(48, 4, 8), small(80, 4, 8), small(112, 4, 8)
                step(v.tensor_reduce(m1, es, AX, ALU.max))
                step(v.tensor_tensor(eq8, es, bc(m1, 4, 8), ALU.is_equal))
                first_of(eq8, oh1, run)
                step(v.scalar_tensor_tensor(out=es2, in0=oh1, scalar=TAKEN, in1=es, op0=ALU.mult, op1=ALU.add))
                step(v.tensor_reduce(m2, es2, AX, ALU.max))
                v.tensor_tensor(diff, m2, m1, ALU.subtract).then_inc(S["route_e"], 1)
                step(v.tensor_tensor(eq8, es2, bc(m2, 4, 8), ALU.is_equal))
                first_of(eq8, oh2, run)
                for pick, inner in ((PICK1, oh1), (PICK2, oh2)):
                    for n in range(GROUPS):
                        step(v.tensor_tensor(pick[:, :, 8 * n:8 * n + 8], inner,
                                             oh[:, :, n].unsqueeze(2).to_broadcast([P, 4, 8]), ALU.mult))
                v.tensor_tensor(PICKED, PICK1, PICK2, ALU.add).then_inc(S["route_ev"], 1)
                dve.wait_ge(S["route_x"], w.next("route_x", 2))
                step(v.tensor_reduce(pg, sh, AX, ALU.add))
                step(v.reciprocal(pg, pg))
                step(v.tensor_scalar(w1, diff, 1.0, None, ALU.add))
                step(v.reciprocal(w1, w1))
                step(v.tensor_tensor(w1, w1, pg, ALU.mult))
                step(v.tensor_tensor(w2, w1, diff, ALU.mult))
                cnt, end, start, many, wend, wfirst, one, t1, t2, off = (TABLE[:, j] for j in range(10))
                dve.wait_ge(S["rank_done"], w.next("rank_done"))
                step(v.tensor_copy(cnt, ps[:, 6, 128:160]))
                step(v.tensor_scalar(one, cnt, 0.0, 1.0, ALU.mult, ALU.add))
                step(v.tensor_tensor_scan(end, one, cnt, 0.0, ALU.mult, ALU.add))
                step(v.tensor_tensor(start, end, cnt, ALU.subtract))
                step(v.tensor_tensor(PICKED, ps[:, 6, 0:128].rearrange("p (t e) -> p t e", t=QT),
                                     start.unsqueeze(1).to_broadcast([P, QT, EXPERTS]), ALU.add))
                for j, pick in enumerate((PICK1, PICK2)):
                    step(v.tensor_tensor(PRODUCT, PICKED, pick, ALU.mult))
                    step(v.tensor_reduce(SLOT[:, j], PRODUCT, AX, ALU.add))
                step(v.tensor_scalar(many, cnt, 0.0, None, ALU.is_gt))
                for j in range(1, QT):
                    step(v.scalar_tensor_tensor(out=many, in0=cnt, scalar=float(P * j), in1=many, op0=ALU.is_gt, op1=ALU.add))
                step(v.tensor_tensor_scan(wend, one, many, 0.0, ALU.mult, ALU.add))
                step(v.tensor_tensor(wfirst, wend, many, ALU.subtract))
                row = vec("row")
                step(v.tensor_scalar(t1, wfirst, row, None, ALU.is_gt))
                step(v.scalar_tensor_tensor(out=t1, in0=wend, scalar=row, in1=t1, op0=ALU.is_gt, op1=ALU.subtract))
                dve.wait_ge(S["iota_in"], w.next("iota_in", 16))
                step(v.tensor_scalar(t2, IOTA[:, 0:EXPERTS], 6.0, None, ALU.mult))
                step(v.tensor_tensor(t2, t2, t1, ALU.mult))
                step(v.tensor_reduce(COLUMN[:, 0:1], t2, AX, ALU.add))
                step(v.tensor_scalar(COLUMN[:, 0:1], COLUMN[:, 0:1], float(MOE_AT), None, ALU.add))
                step(v.tensor_scalar(off, wfirst, row, -float(P), ALU.subtract, ALU.mult))
                step(v.scalar_tensor_tensor(out=off, in0=start, scalar=-float(PAIRED), in1=off, op0=ALU.add, op1=ALU.add))
                step(v.tensor_tensor(off, off, t1, ALU.mult))
                step(v.tensor_reduce(COLUMN[:, 1:2], off, AX, ALU.add))
                step(v.tensor_scalar(COLUMN[:, 1:2], COLUMN[:, 1:2], float(PAIRED), None, ALU.add))
                for j in range(2):
                    ins = v.tensor_scalar(DIAGS[:, j], IDENT, COLUMN[:, j:j + 1], None, ALU.mult)
                ins.then_inc(S["table_in"], 1)
                dve.wait_ge(S["merged"], w.next("merged", DT))
                for t in range(QT):
                    step(v.tensor_scalar(PICK[:, t], IOTA, SLOT[:, 0, t:t + 1], None, ALU.is_equal))
                    v.scalar_tensor_tensor(out=PICK[:, t], in0=IOTA, scalar=SLOT[:, 1, t:t + 1], in1=PICK[:, t],
                                           op0=ALU.is_equal, op1=ALU.add).then_inc(S["pick_in"], 1)
                    if t == 0:
                        dve.wait_ge(S["table_rows"], w.next("table_rows"))
                        v.tensor_copy(WTAB.rearrange("p (a n) -> p a n", a=2),
                                      ps[0:1, 6, 0:2 * P].rearrange("p (a n) -> p a n", a=2)[:, :, 0:TAB]).then_inc(S["table"], 1)
                for t in range(QT):
                    step(v.tensor_scalar(WEIGH[:, t], IOTA, SLOT[:, 0, t:t + 1], w1[:, t:t + 1], ALU.is_equal, ALU.mult))
                    step(v.tensor_scalar(PAIR_TMP, IOTA, SLOT[:, 1, t:t + 1], w2[:, t:t + 1], ALU.is_equal, ALU.mult))
                    v.tensor_tensor(WEIGH[:, t], WEIGH[:, t], PAIR_TMP, ALU.add).then_inc(S["weigh_in"], 1)
                dve.wait_ge(S["weigh_in"], w.next("weigh_in", QT))

            def dve_moe():
                w.count("tile_done", 2 * QT + 2 * DT + PAIR_T)
                dve.wait_ge(S["act_evac"], w.next("act_evac", 2 * QT + 2 * DT + PAIR_T))
                dve.wait_ge(S["table"], w.next("table"))

                def hidden(n):
                    dve.wait_ge(S["sg"], w.next("sg"))
                    dve.wait_ge(S["gu_done"], w.next("gu_done", 2))
                    v.tensor_tensor(HID[n % 2], SILU[n % 2], ps[:, 2 + n % 2, 0:2 * P].rearrange("p (f c) -> p f c", f=2),
                                    ALU.mult).then_inc(S["hid"], 1)

                def down(n, at):
                    first = dve.value_load(WTAB[:, at], min_val=0, max_val=PAIRED)
                    if n:
                        dve.wait_ge(S["dn_evac"], w.next("dn_evac", 2))
                    for h in range(2):
                        dve.wait_ge(S["dn_done"], w.next("dn_done"))
                        v.tensor_copy(YS[:, 4 * h:4 * h + 4, ds(first, P)],
                                      ps[:, 4 + 2 * (n % 2) + h].rearrange("p (j c) -> p j c", j=4)).then_inc(S["dn_evac"], 1)

                hidden(0)
                for n in (1, 2):
                    hidden(n)
                    down(n - 1, slice(TAB + n - 1, TAB + n))
                with w.loop((WINDOWS - 3) // 4, sg=4, gu_done=8, dn_done=8, dn_evac=8) as i:
                    for n in range(3, 7):
                        hidden(n)
                        down(n - 1, ds(i * 4 + (TAB + n - 1), 1))
                down(WINDOWS - 1, slice(TAB + WINDOWS - 1, TAB + WINDOWS))
                w.count("tile_done", 2 * PAIR_T)
                w.count("act_evac", 2 * PAIR_T)
                for k in range(DT):
                    dve.wait_ge(S["tile_done"], w.next("tile_done"))
                    accumulate(XA[:, k], ps[:, k % 4], 1.0)
                dve.wait_ge(S["dve_evac"], w.next("dve_evac", DT))

            def dve_lru():
                e, s, s2, acc, sp8 = (LAM[:, 4 * j:4 * j + 4] for j in range(5))
                lam = V[:, VEC_AT["lam"]:VEC_AT["lam"] + 4]
                dve.wait_ge(S["lam_exp"], w.next("lam_exp"))
                step(v.tensor_scalar(s, e, 2.0, None, ALU.add))
                step(v.reciprocal(s, s))
                step(v.tensor_tensor(s, s, e, ALU.mult))
                step(v.tensor_tensor(s2, s, s, ALU.mult))
                step(v.tensor_scalar(acc, s2, 1.0 / 15, 1.0 / 13, ALU.mult, ALU.add))
                for k in (11, 9, 7, 5, 3, 1):
                    step(v.tensor_tensor(acc, acc, s2, ALU.mult))
                    step(v.tensor_scalar(acc, acc, 1.0 / k, None, ALU.add))
                step(v.tensor_tensor(acc, acc, s, ALU.mult))
                step(v.tensor_scalar(sp8, lam, -1.0, 0.0, ALU.mult, ALU.max))
                step(v.scalar_tensor_tensor(out=sp8, in0=acc, scalar=2.0, in1=sp8, op0=ALU.mult, op1=ALU.add))
                step(v.tensor_scalar(sp8, sp8, LRU_C, None, ALU.mult))
                dve.wait_ge(S["pad_zero"], w.next("pad_zero"))
                dve.wait_ge(S["act_evac"], w.next("act_evac", 4))
                for j in range(4):
                    dve.wait_ge(S["act_evac"], w.next("act_evac"))
                    step(v.tensor_scalar(XC[:, j], PREC[:, j, 3:3 + N2], vec("conv_w", 12 + j), vec("conv_b", j), ALU.mult, ALU.add))
                    for k in (2, 1, 0):
                        ins = v.scalar_tensor_tensor(out=XC[:, j], in0=PREC[:, j, k:k + N2], scalar=vec("conv_w", 4 * k + j),
                                                     in1=XC[:, j], op0=ALU.mult, op1=ALU.add)
                        if k:
                            step(ins)
                    ins.then_inc(S["lru_x"], 1)
                dve.wait_ge(S["act_evac"], w.next("act_evac", 5))
                for j in range(4):
                    dve.wait_ge(S["act_evac"], w.next("act_evac"))
                    v.tensor_scalar(RA[:, j], RA[:, j], sp8[:, j:j + 1], None, ALU.mult).then_inc(S["lru_r"], 1)
                dve.wait_ge(S["act_evac"], w.next("act_evac", 4))
                for j in range(4):
                    dve.wait_ge(S["lru_t"], w.next("lru_t"))
                    step(v.tensor_tensor(RX[:, j], RX[:, j], XC[:, j], ALU.mult))
                    step(v.tensor_scalar(XC[:, j], LRU_T[:, j], 1.0, None, ALU.add))
                    step(v.reciprocal(XC[:, j], XC[:, j]))
                    step(v.scalar_tensor_tensor(out=LRU_T[:, j], in0=LRU_T[:, j], scalar=2.0, in1=XC[:, j], op0=ALU.mult, op1=ALU.mult))
                    v.tensor_scalar(LRU_T[:, j], LRU_T[:, j], 2.0 ** -116, None, ALU.max).then_inc(S["lru_r"], 1)
                for j in range(4):
                    dve.wait_ge(S["lru_t"], w.next("lru_t"))
                    step(v.scalar_tensor_tensor(out=RX[:, j], in0=LRU_T[:, j], scalar=-2.0 ** -58, in1=RX[:, j],
                                                op0=ALU.add, op1=ALU.mult))
                    step(v.tensor_tensor_scan(Y2[:, j], RA[:, j], RX[:, j], 0.0, ALU.mult, ALU.add))
                    dve.wait_ge(S["gelu_done"], w.next("gelu_done"))
                    v.tensor_tensor(Y2[:, j], Y2[:, j], PG[:, j], ALU.mult).then_inc(S["lru_done"], 1)

            WI = SMALL[:, 416:448]
            body()

        @block.gpsimd
        def _(pool):
            w = Counts(pool)
            g = nc.gpsimd

            def step(ins):
                ins.then_inc(S["pool_ops"], 1)
                pool.wait_ge(S["pool_ops"], w.next("pool_ops"))

            def keep(out, compare, fill):
                return g.affine_select(out=out, in_=out, **compare, fill=fill)

            CAUSAL = dict(compare_op=ALU.is_ge, base=0, pattern=[[-1, P]], channel_multiplier=1)
            BEFORE = dict(compare_op=ALU.is_gt, base=0, pattern=[[1, P]], channel_multiplier=-1)

            def body():
                pool.dma_start(HOT, a["onehot"]).then_inc(S["hot_in"], 16)
                pool.dma_start(RELB, a["rel_bias"]).then_inc(S["hot_in"], 16)
                pool.dma_start(WIDX, a["w_idx"]).then_inc(S["small_in"], 16)
                pool.wait_ge(S["bias_dram"], w.next("bias_dram"))
                pool.dma_start(bias_scratch.ap(), BVEC).then_inc(S["bvec_out"], 16)
                pool.wait_ge(S["bvec_out"], w.next("bvec_out", 16))
                rows = bass.AP(bias_scratch, 0, [[1, P], [BIAS_W, HEADS], [1, SEQ]])
                pool.dma_start(BIAS_FLIPPED, rows).then_inc(S["bias_rows"], 16)
                pool.wait_ge(S["bias_rows"], w.next("bias_rows", 16))
                step(g.memset(MASKS[0], 0.0))
                keep(MASKS[0], CAUSAL, NEG).then_inc(S["score_mask"], 1)
                for t in range(1, QT):
                    pool.wait_ge(S["rel_used"], w.next("rel_used", HEADS))
                    keep(SCORES[t][:, P * t:P * t + P], CAUSAL, LOW).then_inc(S["score_cut"], 1)
                pool.wait_ge(S["staged"], w.next("staged", 3))
                pool.dma_start(WROUT, a["w_router"]).then_inc(S["wr_in"], 16)
                pool.dma_start(BR, a["b_router"]).then_inc(S["wr_in"], 16)
                units = [(h, t) for h in range(2) for t in reversed(range(QT))]
                with w.loop(PAIRS, sp=8, a_raw=8):
                    def mask_p(u):
                        h, t = units[u]
                        pool.wait_ge(S["sp"], w.next("sp"))
                        g.nop(nofuse=True)
                        keep(SPP[h][:, SP_OFF[t]:SP_OFF[t] + P], BEFORE, 0.0).then_inc(S["sp_masked"], 1)

                    def mask_a(u):
                        pool.wait_ge(S["a_raw"], w.next("a_raw"))
                        g.nop(nofuse=True)
                        keep(SPA[u % 2][:, 0:P], BEFORE, 0.0).then_inc(S["a_masked"], 1)

                    mask_p(0)
                    mask_p(1)
                    for u in range(8):
                        if u + 2 < 8:
                            mask_p(u + 2)
                        mask_a(u)
                w.count("dve_evac")
                for n in range(DT):
                    pool.wait_ge(S["dve_evac"], w.next("dve_evac"))
                    g.tensor_tensor(MERGED[:, n], GATES[:, n], GATES[:, DT + n], ALU.add).then_inc(S["merged"], 1)
                pool.wait_ge(S["merged"], w.next("merged", DT))
                g.memset(XS[:, :, PAIRED:], 0.0).then_inc(S["pad_in"], 1)
                pool.dma_start(IOTA, a["iota"]).then_inc(S["iota_in"], 16)
                pool.dma_start(PX, a["p"]).then_inc(S["p_in"], 16)
                pool.wait_ge(S["norm_out"], w.next("norm_out", 33))
                pool.dma_start(MASKW, a["causal"]).then_inc(S["c2_in"], 16)
                pool.dma_start(ROPE_C, a["mla_cos"]).then_inc(S["c2_in"], 16)
                pool.dma_start(ROPE_S, a["mla_sin"]).then_inc(S["c2_in"], 16)
                g.memset(PREC[:, :, 0:3], 0.0).then_inc(S["pad_zero"], 1)
                w.count("act_evac", 46 + 2 * QT + 2 * DT + PAIR_T + 2 * PAIR_T)
                for j in range(4):
                    pool.wait_ge(S["act_evac"], w.next("act_evac"))
                    step(g.tensor_tensor(GELU[:, j], PG[:, j], PG[:, j], ALU.mult))
                    step(g.tensor_scalar(GELU[:, j], GELU[:, j], 0.044715, 1.0, ALU.mult, ALU.add))
                    g.tensor_tensor(GELU[:, j], GELU[:, j], PG[:, j], ALU.mult).then_inc(S["gelu_in"], 1)
                for j in range(4):
                    pool.wait_ge(S["gelu_th"], w.next("gelu_th"))
                    step(g.tensor_scalar(GELU[:, j], GELU[:, j], 0.5, 0.5, ALU.mult, ALU.add))
                    g.tensor_tensor(PG[:, j], PG[:, j], GELU[:, j], ALU.mult).then_inc(S["gelu_done"], 1)
                pool.wait_ge(S["dve_evac"], w.next("dve_evac", 8 + 8 + 8 + 8))
                pool.dma_start(DECAY, a["decay"]).then_inc(S["c3_in"], 16)
                pool.dma_start(COS, a["cos"]).then_inc(S["c3_in"], 16)
                pool.dma_start(SIN, a["sin"]).then_inc(S["c3_in"], 16)

            body()


def bucket(dist):
    dist = np.maximum(dist, 0)
    exact = N_BUCKETS // 2
    d = np.maximum(dist, 1).astype(np.float32)
    large = exact + (np.log(d / exact) / math.log(128 / exact) * (N_BUCKETS - exact)).astype(np.int32)
    return np.where(dist < exact, dist, np.minimum(large, N_BUCKETS - 1))


def constants():
    f = np.float32
    i = np.arange(P)
    mats = np.stack([np.eye(P), np.ones((P, P)), np.eye(P)[::-1], -(i[:, None] >= i[None, :]).astype(f), -np.ones((P, P))], 1)
    hot = np.zeros((N_BUCKETS, BIAS_W), f)
    hot[bucket(SEQ - 1 - np.arange(BIAS_W)), np.arange(BIAS_W)] = 1
    causal = np.where(np.arange(T2)[None, :] - (T2 - P) > i[:, None], NEG, 0.0)
    pos = np.arange(T2, dtype=f)

    def angles(half):
        inv = (f(10000.0) ** (-np.arange(half, dtype=f) / half)).astype(f)
        ang = (pos[None, :] * inv[:, None]).astype(f)
        return np.cos(ang), np.sin(ang)

    c, s = angles(16)
    rope = np.zeros((2, P, T2), f)
    for at in (0, HD):
        rope[0, at:at + 32] = np.concatenate([c, c])
        rope[1, at:at + 32] = np.concatenate([-s, s])
    cos, sin = angles(P)
    log_gamma = np.log(f(1.0) - f(2.0) ** (f(-5.0) - np.arange(RET_HEADS, dtype=f)))
    diff = np.arange(T2)[None, :] - i[:, None]
    decay = np.where(diff[:, None] >= 0, np.exp(log_gamma[None, :, None] * np.maximum(diff, 0)[:, None]), 0)
    out = dict(mats=mats, iota=np.broadcast_to(np.arange(PAIRED), (P, PAIRED)), onehot=hot, causal=causal, mla_cos=rope[0], mla_sin=rope[1], cos=cos, sin=sin, decay=decay)
    return {k: np.ascontiguousarray(v, dtype=f) for k, v in out.items()}


def blocks(w):
    k, n = w.shape
    return w.reshape(k // P, P, n // P, P).transpose(2, 1, 0, 3)


def layout(i):
    f = np.float32
    cut = np.cumsum([0, 512, 128, 512, 64, 8, 1536, 1024, 1024])
    w_in = i["w_in"][0]
    qa, ckv, qidx, kidx, widx, qkv, ga, gb = (w_in[:, a:b] for a, b in zip(cut[:-1], cut[1:]))
    chunks = [blocks(x) for x in (ckv, np.concatenate([kidx, kidx], 1), qidx, qa, qkv, ga, gb)]
    uk = np.moveaxis(i["w_uk"][0], 0, 1).reshape(P, 512)
    uv = np.moveaxis(i["w_uv"][0], 0, 1).reshape(P, 512)
    chunks.append(np.concatenate([uk, uv], 1).reshape(1, P, 8, P))
    chunks.append(np.concatenate([blocks(i["w_branch_a"][0]), blocks(i["w_branch_b"][0])], 2))
    chunks.append(blocks(i["w_out"][0]))
    gate = [blocks(i["w_gate"][0, e]) for e in range(EXPERTS)]
    up = [blocks(i["w_up"][0, e]) for e in range(EXPERTS)]
    down = [blocks(i["w_down"][0, e]).transpose(1, 0, 2, 3).reshape(P, 2, 8, P).transpose(1, 0, 2, 3) for e in range(EXPERTS)]
    for e in range(EXPERTS):
        chunks += [gate[e], up[e], down[e]]
    ple = blocks(i["w_ple"][0]).transpose(1, 0, 2, 3).reshape(P, 2, 8, P).transpose(1, 0, 2, 3)
    pleg = blocks(i["w_ple_gate"][0])
    chunks += [ple[:1], pleg[:4], ple[1:], pleg[4:]]
    ev = i["ev_w_in_2"][0]
    kpe = ev[:, 1408:1440]
    swap = lambda x: np.concatenate([x[..., 16:], x[..., :16]], -1)
    zero = np.zeros((D, 32), f)
    chunks.append(blocks(np.concatenate([ev[:, :1408], kpe, zero, kpe, zero, swap(kpe), zero, swap(kpe), zero], 1)))
    rg = np.concatenate([i["ev_w_rg_a_2"][0], i["ev_w_rg_x_2"][0]], 0)
    chunks.append(rg.transpose(1, 0, 2)[None])
    uq = i["ev_w_uq_2"][0].reshape(256, HEADS, 96)
    z = np.zeros((256, HEADS, 32), f)
    nope = uq[:, :, :64].reshape(256, 512)
    pe = np.concatenate([uq[:, :, 64:], z], 2).reshape(256, 512)
    pw = np.concatenate([swap(uq[:, :, 64:]), z], 2).reshape(256, 512)
    chunks += [blocks(x).transpose(1, 0, 2, 3).reshape(1, P, 8, P) for x in (nope, pe, pw)]
    ukv = i["ev_w_ukv_2"][0].reshape(P, HEADS, 2, 64)
    chunks.append(np.concatenate([ukv[:, :, 0].reshape(P, 512), ukv[:, :, 1].reshape(P, 512)], 1).reshape(1, P, 8, P))
    chunks.append(blocks(i["ev_w_out_2"][0]))

    def deep(w):
        b = blocks(w)
        return b.reshape(b.shape[0], P, -1, 8, P).transpose(0, 2, 1, 3, 4).reshape(-1, P, 8, P)

    for l in range(2):
        if l:
            chunks += [blocks(i["od_w_in_2"][0]), deep(i["od_w_out_2"][0])]
        chunks += [blocks(i["mlp_w1_2"][l]), deep(i["mlp_w2_2"][l])]
    weights = np.concatenate([np.asarray(c, f).reshape(-1, P, D) for c in chunks], 0)
    assert weights.shape[0] == N_CHUNKS, (weights.shape, N_CHUNKS)

    col = lambda x: np.asarray(x, f).reshape(-1, P).T
    vecs = [i["attn_norm"], i["kv_norm"], i["ffn_norm"], i["ple_norm"], i["final_norm"], i["ev_conv_w_2"], i["ev_conv_b_2"],
            i["ev_b_rg_a_2"], i["ev_b_rg_x_2"], i["ev_lru_lambda_2"], i["ev_q_norm_g_2"], i["ev_kv_norm_g_2"],
            i["ln_mix_g_2"], i["ln_mix_b_2"], i["ln_mlp_g_2"], i["ln_mlp_b_2"], np.arange(P)]
    tiles = lambda x: np.asarray(x, f).T.reshape(-1, P, x.shape[0]).transpose(1, 0, 2)
    rows = lambda x: np.asarray(x, f).reshape(DT, P, -1).transpose(1, 0, 2)
    router = np.concatenate([i["w_r1"][0], np.moveaxis(i["w_r2"][0], 0, 1).reshape(D, EXPERTS)], 1)
    b_router = np.concatenate([i["b_r1"][0], i["b_r2"][0].reshape(-1)])
    out = dict(x=tiles(i["x"][0]), meta=tiles(i["meta_tokens_2"]), p=tiles(i["p"][0, 0]), weights=weights,
               vecs=np.concatenate([col(v) for v in vecs], 1), w_idx=rows(widx), w_router=rows(router),
               b_router=np.broadcast_to(b_router, (P, QT, 36)), rel_bias=i["rel_bias"])
    return {k: np.ascontiguousarray(v, dtype=f) for k, v in (out | constants()).items()}


def kernel(**inputs):
    import concourse.bacc as bacc
    from concourse.bass_utils import run_bass_kernel_spmd

    arrays = layout({k: np.asarray(v) for k, v in inputs.items()})
    nc = bacc.Bacc("TRN2", target_bir_lowering=False, num_devices=1)
    aps = {k: nc.dram_tensor(f"in_{k}", v.shape, F32, kind="ExternalInput").ap() for k, v in arrays.items()}
    aps["out"] = nc.dram_tensor("out_tiles", (P, DT, SEQ), F32, kind="ExternalOutput").ap()
    build(nc, aps)
    r = run_bass_kernel_spmd(nc, [{f"in_{k}": v for k, v in arrays.items()}], core_ids=[0])
    out = r.results[0]["out_tiles"]
    return np.ascontiguousarray(out.transpose(2, 1, 0).reshape(1, SEQ, D))
```

```python
import math
from contextlib import ExitStack, contextmanager

import numpy as np
import concourse.bass as bass
from concourse import mybir

F32 = mybir.dt.float32
F32R = mybir.dt.float32r
ALU = mybir.AluOpType
ACT = mybir.ActivationFunctionType
AX = mybir.AxisListType.X
ds = bass.ds

P = 128
D = 1024
DT = D // P
SEQ = 512
META = 16
T2 = SEQ + META
HALF = T2 // 2
QT = SEQ // P
HEADS = 8
HD = 64
PAIRS = HEADS // 2
KV_RANK = 128
N_SEL = min(256, SEQ // 4)
IDX_SCALE = (8 ** -0.5) * (64 ** -0.5)
QK_SCALE = HD ** -0.5
N_BUCKETS = 32
GROUPS, PER_GROUP = 4, 8
EXPERTS = GROUPS * PER_GROUP
EPS1, EPS2 = 1e-6, 1e-5
ALPHA = 4.0 ** 0.25
MLA_SCALE = 96 ** -0.5
RET_HEADS = 4
LRU_C = 8.0
FF = 4 * D
NEG = -1.0e30
LOW = -1.0e38
TAKEN = -3.0e38

CHUNKS = [("kv", 2), ("qidx", 4), ("qa", 4), ("qb", 4), ("kb", 4), ("vb", 4), ("ukuv", 1), ("gates", 16),
          ("merge", 8), ("wout", 8), ("moe", 6 * EXPERTS), ("ple", 10),
          ("evin", 13), ("rg", 1), ("uq", 3), ("ukv", 1), ("evout", 8), ("up0", 32), ("down0", 32),
          ("odqk", 16), ("odg", 16), ("odv", 16), ("odout", 16), ("up1", 32), ("down1", 32)]
N_CHUNKS = sum(n for _, n in CHUNKS)
MOE_AT = sum(n for _, n in CHUNKS[:[name for name, _ in CHUNKS].index("moe")])
TOP_K = 2
PAIRED = TOP_K * SEQ
PAIR_T = PAIRED // P
WINDOWS = (PAIRED - EXPERTS) // P + EXPERTS
WIDE = PAIRED + P
TAB = WINDOWS + 1
MOE_USES = 6 * WINDOWS
N_USES = N_CHUNKS + MOE_USES - 6 * EXPERTS
SLOTS = 8


def use_of(name):
    names = [n for n, _ in CHUNKS]
    return sum(MOE_USES if n == "moe" else k for n, k in CHUNKS[:names.index(name)])


VECS = [("attn_norm", 8), ("kv_norm", 1), ("ffn_norm", 8), ("ple_norm", 8), ("final_norm", 8),
        ("conv_w", 16), ("conv_b", 4), ("b_rg_a", 4), ("b_rg_x", 4), ("lam", 4), ("q_norm", 2), ("kv_norm2", 1),
        ("ln_mix_g", 16), ("ln_mix_b", 16), ("ln_mlp_g", 16), ("ln_mlp_b", 16), ("row", 1), ("eps1", 1), ("eps2", 1)]
VEC_AT, _n = {}, 0
for _name, _w in VECS:
    VEC_AT[_name] = _n
    _n += _w
N_VEC = _n

TOK2 = [(0, META)] + [(META + P * i, P) for i in range(QT)]
BIAS_W = SEQ + P


class Counts:

    def __init__(self, eng):
        self.eng = eng
        self.base, self.local, self.per, self.i = {}, {}, {}, None

    def value(self, name, back=0):
        at = self.base.get(name, 0) + self.local.get(name, 0) - back
        return at if self.i is None or not self.per.get(name) else self.i * self.per[name] + at

    def count(self, name, k=1):
        assert self.i is None or name in self.per, name
        self.local[name] = self.local.get(name, 0) + k

    def next(self, name, k=1):
        self.count(name, k)
        return self.value(name)

    def counted(self, name, back=0):
        return self.base.get(name, 0) + self.local.get(name, 0) > back

    @contextmanager
    def loop(self, times, **per):
        for n, k in self.local.items():
            self.base[n] = self.base.get(n, 0) + k
        self.local, self.per = {}, per
        with self.eng.Fori(0, times) as i:
            self.i = i
            yield i
        self.i = None
        assert {n: k for n, k in self.local.items() if k} == {n: k for n, k in per.items() if k}, (self.local, per)
        for n, k in per.items():
            self.base[n] = self.base.get(n, 0) + k * times
        self.local, self.per = {}, {}


def build(nc, a):
    ctx = ExitStack()
    with ctx:
        def sb(name, shape):
            return ctx.enter_context(nc.sbuf_tensor(name, shape, F32))

        with nc.sbuf_tensor("area", [P, 34688], F32) as AREA:
            pass
        PARTS = ctx.enter_context(nc.sbuf_tensor("parts", [P, 34688], F32R))
        X = sb("residual", [P, DT, T2])
        HN = sb("normed", [P, DT, T2])
        RING = sb("weights", [P, SLOTS, D])
        V = sb("vectors", [P, N_VEC])
        CM = sb("matrices", [P, 5, P])
        R = sb("rstd", [P, T2])
        ps = ctx.enter_context(nc.psum_tensor("ps", [P, 8, 512], F32))
        IDENT, ONES, FLIP, NTRI, NONES = (CM[:, j] for j in range(5))

        def area(off, *shape):
            n = int(np.prod(shape))
            assert off + n <= 34688, (off, n)
            v = AREA[:, off:off + n]
            if len(shape) == 2:
                v = v.rearrange("p (a b) -> p a b", a=shape[0])
            if len(shape) == 3:
                v = v.rearrange("p (a b c) -> p a b c", a=shape[0], b=shape[1])
            return v

        CKV, KI = area(0, SEQ), area(512, SEQ)
        QA, QI = area(1024, PAIRS, SEQ), area(3072, PAIRS, SEQ)
        QB, KB = area(5120, PAIRS, SEQ), area(7168, PAIRS, SEQ)
        VB = area(9216, QT, SEQ)
        GATES = area(11264, 16, SEQ)
        KA, VA = area(19456, PAIRS, SEQ), area(21504, QT, SEQ)
        BIAS = area(23552, HEADS, SEQ)
        SCORE_OFF = [27648 + o for o in (0, 128, 384, 768)]
        SCORES = [area(o, P * (t + 1)) for t, o in enumerate(SCORE_OFF)]
        MASKS = [area(o + 1280, P * (t + 1)) for t, o in enumerate(SCORE_OFF)]
        TMP = 30208
        LG = [area(TMP, 512), area(TMP + 512, 512)]
        EX = [area(TMP + 1024, 512), area(TMP + 1536, 512)]
        PT = [area(TMP + 2048, 4, P), area(TMP + 2560, 4, P)]
        DG = [area(33280, P), area(33408, P)]
        ST1, ST2 = area(33536, 512), area(34048, 512)
        MERGED = area(7168, DT, SEQ)
        BIAS_FLIPPED = area(11264, HEADS, SEQ)
        SPT = [area(27648, 512), area(28160, 512)]
        SPP = [area(28672, 1280), area(29952, 1280)]
        SPA = [area(31232, 512), area(31744, 512)]
        ST3 = area(32256, 512)
        SMALL = sb("small", [P, 448])
        WIDX = area(19456, DT, 8)
        WROUT = area(0, DT, 36)
        SP_OFF = [0, 512, 896, 1152]
        HOT, RELB = area(27648, BIAS_W)[0:N_BUCKETS], area(28288, HEADS)[0:N_BUCKETS]
        BVEC = area(28928, BIAS_W)[0:HEADS]
        BR = area(288, QT, 36)
        LAM = sb("lambda", [P, 24])
        SG = [area(1024, 512), area(1536, 512)]
        HT = [area(2048, 512), area(2560, 512)]
        PICK1, PICK2, PICKED, PRODUCT = (area(512 + 128 * j, QT, EXPERTS) for j in range(4))
        TABLE = area(1024, 12, EXPERTS)
        SLOT, COLUMN = area(1408, 2, QT), area(1416, 2)
        DIAGS = area(1424, 2, P)
        HID = [area(3072, 2, P), area(3328, 2, P)]
        SILU = [area(3584, 2, P), area(3840, 2, P)]
        XW = [area(4096, DT, P), area(5120, DT, P)]
        HTOK, PICK = area(6144, QT, D), area(10240, QT, PAIRED)
        YS = area(6144, DT, WIDE)
        WEIGH = area(15360, QT, PAIRED)
        XS = area(19456, DT, WIDE)
        YPAIR = area(19456, PAIR_T, D)
        PX = area(28672, 2, SEQ)
        WPAIR = area(29696, PAIR_T, SEQ)
        IOTA = area(33664, PAIRED)
        PAIR_TMP = area(2048, PAIRED)
        WTAB = ctx.enter_context(nc.sbuf_tensor("windows", [P, 2 * TAB], mybir.dt.int32))[0:1]

        N2 = T2
        PG, PREC = area(0, 4, N2), area(2112, 4, N2 + 3)
        PQ, PKV, KPE, KPW = area(4236, 2, N2), area(5292, N2), area(5820, N2), area(6348, N2)
        XC, RA, RX = area(6876, 4, N2), area(8988, 4, N2), area(11100, 4, N2)
        QN, QP, QW, KN = area(13212, 4, N2), area(15324, 4, N2), area(17436, 4, N2), area(19548, 4, N2)
        V2 = area(21660, 5, 512)
        Y2 = area(24220, 8, N2)
        GELU = area(26332, 4, N2)
        LRU_T = area(2112, 4, N2)
        MASKW, ROPE_C, ROPE_S = area(28444, N2), area(28972, N2), area(29500, N2)
        LG2 = [area(30028, N2), area(30556, N2)]
        EX2 = [area(31084, N2), area(31612, N2)]
        PT2 = [area(32140, 5, P), area(32780, 5, P)]
        DG2 = [area(33420, P), area(33548, P)]
        SQN, SQP, SKN, SV2 = area(6876, N2), area(7404, N2), area(7932, N2), area(4236, 5, P)
        def part(off, *shape):
            v = PARTS[:, off:off + int(np.prod(shape))]
            return v.rearrange("p (a b) -> p a b", a=shape[0]) if len(shape) == 2 else v

        FH, FL = part(0, 16, N2), part(8448, 16, N2)
        XH, XL = part(16896, DT, N2), part(21120, DT, N2)
        IN_MLP, IN_ODD = ([[part(off + D * j, D) for j in range(2)], [part(off + D * (2 + j), D) for j in range(2)]]
                          for off in (25344, 22912))
        XHO, XLO = part(4224, DT, N2), part(8448, DT, N2)
        RK, RV, RG = area(0, 8, N2), area(4224, 5, 2048), area(14464, 16, N2)
        SRK, SRV, RSC = area(22912, 2, N2), area(23968, 5, 512), area(26528, 1808)
        ROPED = area(27008, 2, N2)
        RSC_OFF = [0, 528, 1040, 1424, 1680]
        DECAY, COS, SIN = area(28336, 4, N2), area(30448, N2), area(30976, N2)
        ROT, RSQ = area(30448, 4, N2), area(32560, 4, N2)

        names = """x_in consts norm_sq norm_sum norm_sd norm_out act_ops dve_ops pool_ops
            tile_done act_evac dve_evac chunk_begun rel_done rel_sb rel_used score_cut score_mask
            bias_vec bias_dram bias_rows bias_flip small_in logits smax expd diag tr pt o_done o_evac staged
            z_done soft sp sp_masked c_done a_raw a_masked merged flip_done
            route_done route_ev route_e rank_done table_in table_rows table iota_in pad_in pick_in weigh_in
            tokens_in gate_on sg gu_done hid dn_done dn_evac
            p_in meta_in out_done ln_cent ln_out c2_in c3_in hot_in bvec_out wr_in route_x lam_exp gelu_in gelu_th
            gelu_done xq w_hi w_lo x_hi x_lo lru_t pad_zero lru_x lru_r lru_done ret_s ret_v ret_used ret_o ret_y""".split()
        S = {n: ctx.enter_context(nc.semaphore(n)) for n in names}
        chunk_full = [ctx.enter_context(nc.semaphore(f"chunk_full{s}")) for s in range(SLOTS)]
        bias_scratch = nc.dram_tensor("bias_scratch", (HEADS, BIAS_W), F32, kind="Internal")

        B1 = slice(META, T2)
        XA, HA = X[:, :, B1], HN[:, :, B1]

        def vec(name, j=0):
            return V[:, VEC_AT[name] + j:VEC_AT[name] + j + 1]

        def halves(bank):
            return ps[:, bank:bank + 2, 0:HALF]

        def two(v):
            return v.rearrange("p (h c) -> p h c", h=2)

        block = ctx.enter_context(nc.Block())

        @block.sync
        def _(sp):
            w = Counts(sp)
            sp.dma_start(XA, a["x"]).then_inc(S["x_in"], 16)
            sp.dma_start(V[:], a["vecs"]).then_inc(S["consts"], 16)
            sp.dma_start(CM[:], a["mats"]).then_inc(S["consts"], 16)
            sp.dma_start(X[:, :, 0:META], a["meta"]).then_inc(S["meta_in"], 16)

            def load(slot, chunk):
                sp.dma_start(RING[:, slot:slot + 1, :],
                             a["weights"][chunk].rearrange("a p n -> p a n")).then_inc(chunk_full[slot], 16)

            for c in range(SLOTS):
                load(c, slice(c, c + 1))

            def refill(use, chunk, back=0):
                sp.wait_ge(S["chunk_begun"], back + use - SLOTS + 2)
                load(use % SLOTS, chunk)

            def stream(first, last, shift):
                times = (last - first) // SLOTS
                with sp.Fori(0, times) as i:
                    for s in range(SLOTS):
                        refill(first + s, ds(i * SLOTS + (first + s - shift), 1), i * SLOTS)
                for u in range(first + SLOTS * times, last):
                    refill(u, slice(u - shift, u - shift + 1))

            stream(SLOTS, MOE_AT, 0)
            sp.wait_ge(S["table"], w.next("table"))

            def window(use, at, back=0):
                gate_up = sp.value_load(WTAB[:, at(0)], min_val=MOE_AT, max_val=MOE_AT + 6 * (EXPERTS - 1))
                for j in range(4):
                    refill(use + j, ds(gate_up + j, 1), back)
                down(use + 4, at(-1), back)

            def down(use, at, back=0):
                first = sp.value_load(WTAB[:, at], min_val=MOE_AT, max_val=MOE_AT + 6 * (EXPERTS - 1))
                for j in range(2):
                    refill(use + j, ds(first + (4 + j), 1), back)

            first = sp.value_load(WTAB[:, 0:1], min_val=MOE_AT, max_val=MOE_AT + 6 * (EXPERTS - 1))
            for j in range(4):
                refill(MOE_AT + j, ds(first + j, 1))
            for n in (1, 2):
                window(MOE_AT + 6 * n - 2, lambda b: slice(n + b, n + b + 1))
            with sp.Fori(0, (WINDOWS - 3) // 4) as i:
                for n in range(4):
                    window(MOE_AT + 6 * (n + 3) - 2, lambda b: ds(i * 4 + (n + 3 + b), 1), i * 24)
            down(MOE_AT + MOE_USES - 2, slice(WINDOWS - 1, WINDOWS))
            stream(MOE_AT + MOE_USES, N_USES, MOE_USES - 6 * EXPERTS)
            for t in range(0, DT, 2):
                sp.wait_ge(S["ln_out"], 3 * DT + t + 2)
                sp.dma_start(a["out"][:, t:t + 2], X[:, t:t + 2, B1]).then_inc(S["out_done"], 16)
            sp.wait_ge(S["out_done"], 16 * (DT // 2))

        @block.tensor
        def _(pe):
            w = Counts(pe)
            mm = nc.tensor.matmul
            chunk = {"base": 0, "local": 0, "i": None, "per": 0}

            @contextmanager
            def pe_loop(times, chunks, **per):
                assert chunks % SLOTS == 0
                chunk["base"] += chunk["local"]
                chunk["local"], chunk["per"] = 0, chunks
                with w.loop(times, **per) as i:
                    chunk["i"] = i
                    yield i
                assert chunk["local"] == chunks
                chunk["i"], chunk["local"] = None, 0
                chunk["base"] += chunks * times

            def take():
                n = chunk["base"] + chunk["local"]
                chunk["local"] += 1
                fill = n // SLOTS + 1
                if chunk["i"] is not None:
                    fill = chunk["i"] * (chunk["per"] // SLOTS) + fill
                pe.wait_ge(chunk_full[n % SLOTS], fill * 16)
                return RING[:, n % SLOTS, :].rearrange("p (k c) -> p k c", k=DT)

            def take_parts(place):
                n = chunk["base"] + chunk["local"]
                chunk["local"] += 1
                pe.wait_ge(S["w_lo"], w.next("w_lo"))
                return [x[n % 2].rearrange("p (k c) -> p k c", k=DT) for x in place]

            def begun(ins):
                ins.then_inc(S["chunk_begun"], 1)

            stage = {"n": 0, "evac": "act_evac", "nb": 4}

            def begin_stage(evac, nb=4):
                if w.counted("act_evac"):
                    pe.wait_ge(S["act_evac"], w.value("act_evac"))
                if w.counted("dve_evac"):
                    pe.wait_ge(S["dve_evac"], w.value("dve_evac"))
                stage.update(n=0, evac=evac, nb=nb)

            def bank():
                n = stage["n"]
                stage["n"] += 1
                if n >= stage["nb"] or w.i is not None:
                    if w.counted(stage["evac"], stage["nb"] - 1):
                        pe.wait_ge(S[stage["evac"]], w.value(stage["evac"], stage["nb"] - 1))
                w.count(stage["evac"])
                return n % stage["nb"]

            def linear(rhs, wt, fresh=False):
                b = bank()
                for k in range(DT):
                    if fresh:
                        pe.wait_ge(S["norm_out"], w.next("norm_out"))
                    ins = mm(ps[:, b], wt[:, k], rhs(k), start=k == 0, stop=k == DT - 1)
                    if k == 0:
                        begun(ins)
                ins.then_inc(S["tile_done"], 1)

            def norm_sum(n, T, b, src, at=META):
                for t in range(n):
                    pe.wait_ge(S["norm_sq"], w.next("norm_sq"))
                    parts = [(0, at, SEQ)] if T == SEQ else [(0, 0, HALF), (1, HALF, HALF)]
                    for h, c, width in parts:
                        ins = mm(ps[:, b + h, 0:width], ONES, src(t)[:, c:c + width], start=t == 0, stop=t == n - 1)
                ins.then_inc(S["norm_sum"], 1)

            def body():
                pe.wait_ge(S["consts"], 32)
                norm_sum(8, SEQ, 7, lambda t: HN[:, t])
                hn = lambda k: HA[:, k]
                begin_stage("act_evac")
                for n in range(6):
                    linear(hn, take(), fresh=n == 0)
                pe.wait_ge(S["small_in"], w.next("small_in", 16))
                w.count("dve_evac", 2)
                b = 2
                if w.counted("act_evac", 3):
                    pe.wait_ge(S["act_evac"], w.value("act_evac", 3))
                for t in range(QT):
                    for k in range(DT):
                        ins = mm(ps[:, b, 8 * t:8 * t + 8], HA[:, k, P * t:P * t + P], WIDX[:, k],
                                 start=k == 0, stop=k == DT - 1)
                ins.then_inc(S["tile_done"], 1)
                pe.wait_ge(S["norm_sq"], w.next("norm_sq"))
                mm(ps[:, 7], ONES, R[:, 0:SEQ], start=True, stop=True).then_inc(S["norm_sum"], 1)
                pe.wait_ge(S["hot_in"], w.next("hot_in", 32))
                for j in range(2):
                    ins = mm(ps[0:HEADS, 6, 0:BIAS_W // 2] if j == 0 else ps[0:HEADS, 5, 0:BIAS_W // 2],
                             RELB, HOT[:, j * (BIAS_W // 2):(j + 1) * (BIAS_W // 2)], start=True, stop=True)
                ins.then_inc(S["bias_vec"], 1)
                if w.counted("act_evac"):
                    pe.wait_ge(S["act_evac"], w.value("act_evac"))
                for n, (t, h) in enumerate((t, h) for t in range(1, QT) for h in range(HEADS)):
                    if n == 0:
                        pe.wait_ge(S["bias_dram"], w.next("bias_dram", 1))
                    if n >= 2:
                        pe.wait_ge(S["rel_sb"], w.next("rel_sb"))
                    r = slice(HD * (h % 2), HD * (h % 2) + HD)
                    mm(ps[:, 4 + n % 2, 0:P * (t + 1)], QI[r, h // 2, P * t:P * t + P], KI[r, 0:P * (t + 1)],
                       start=True, stop=True).then_inc(S["rel_done"], 1)
                pe.wait_ge(S["rel_sb"], w.next("rel_sb", 2))
                pe.wait_ge(S["bias_rows"], w.next("bias_rows", 16))
                for h in range(HEADS):
                    if h >= 2:
                        pe.wait_ge(S["bias_flip"], w.next("bias_flip"))
                    mm(ps[:, 4 + h % 2], FLIP, BIAS_FLIPPED[:, h], start=True, stop=True).then_inc(S["flip_done"], 1)
                pe.wait_ge(S["bias_flip"], w.next("bias_flip", 2))
                begin_stage("act_evac")
                for _ in range(12):
                    linear(hn, take())
                for _ in range(4):
                    wt, b = take(), bank()
                    for t in range(QT):
                        for k in range(DT):
                            ins = mm(ps[:, b, P * t:P * t + P], HA[:, k, P * t:P * t + P], wt[:, k],
                                     start=k == 0, stop=k == DT - 1)
                            if t == k == 0:
                                begun(ins)
                    ins.then_inc(S["tile_done"], 1)
                stage["n"] = 0
                if w.counted("act_evac"):
                    pe.wait_ge(S["act_evac"], w.value("act_evac"))
                pe.wait_ge(S["norm_out"], w.next("norm_out"))
                wt = take()
                for n in range(PAIRS):
                    ins = mm(ps[:, bank()], wt[:, n], CKV, start=True, stop=True)
                    ins.then_inc(S["tile_done"], 1)
                wv = wt[:, PAIRS:].rearrange("p k c -> p (k c)")
                for t in range(QT):
                    b = bank()
                    if t == 0:
                        begun(mm(ps[:, b, 0:256], CKV[:, 0:P], wv[:, 0:256], start=True, stop=True))
                        ins = mm(ps[:, b, 256:512], CKV[:, 0:P], wv[:, 256:512], start=True, stop=True)
                    else:
                        ins = mm(ps[:, b], CKV[:, P * t:P * t + P], wv, start=True, stop=True)
                    ins.then_inc(S["tile_done"], 1)
                if w.counted("act_evac"):
                    pe.wait_ge(S["act_evac"], w.value("act_evac"))
                pe_dsa()
                pe_stick()
                if w.counted("o_evac"):
                    pe.wait_ge(S["o_evac"], w.value("o_evac"))
                begin_stage("dve_evac", 4)
                for n in range(DT):
                    wt, b = take(), 2 * bank()
                    for k in range(PAIRS):
                        ins = mm(ps[:, b], wt[:, k], QA[:, k], start=k == 0, stop=k == PAIRS - 1)
                        if k == 0:
                            begun(ins)
                    for k in range(PAIRS):
                        ins = mm(ps[:, b + 1], wt[:, PAIRS + k], QB[:, k], start=k == 0, stop=k == PAIRS - 1)
                    ins.then_inc(S["tile_done"], 1)
                pe.wait_ge(S["merged"], w.next("merged", DT))
                begin_stage("dve_evac")
                for _ in range(DT):
                    linear(lambda k: MERGED[:, k], take())
                begin_stage("dve_evac")
                norm_sum(8, SEQ, 7, lambda t: HN[:, t])
                pe.wait_ge(S["wr_in"], w.next("wr_in", 32))
                for t in range(QT):
                    for k in range(DT):
                        if t == 0:
                            pe.wait_ge(S["norm_out"], w.next("norm_out"))
                        ins = mm(ps[:, 6, 36 * t:36 * t + 36], HA[:, k, P * t:P * t + P], WROUT[:, k],
                                 start=k == 0, stop=k == DT - 1)
                ins.then_inc(S["route_done"], 1)
                begin_stage("act_evac")
                for t in range(QT):
                    for j in range(2):
                        b = bank()
                        for k in range(4):
                            ins = mm(ps[:, b, P * k:P * k + P], HA[:, 4 * j + k, P * t:P * t + P], IDENT,
                                     is_transpose=True, start=True, stop=True)
                        ins.then_inc(S["tile_done"], 1)
                pe.wait_ge(S["route_ev"], w.next("route_ev"))
                for t in range(QT + 1):
                    o = ps[:, 6, EXPERTS * t:EXPERTS * t + EXPERTS]
                    for t2 in range(min(t + 1, QT)):
                        ins = mm(o, ONES, PICKED[:, t2], start=t2 == 0, stop=t == QT and t2 == QT - 1)
                    if t < QT:
                        ins = mm(o, NTRI, PICKED[:, t], start=False, stop=True)
                ins.then_inc(S["rank_done"], 1)
                if w.counted("act_evac"):
                    pe.wait_ge(S["act_evac"], w.value("act_evac"))
                pe.wait_ge(S["pick_in"], w.next("pick_in", QT))
                begin_stage("act_evac")
                for k in range(DT):
                    for h in range(2):
                        b = bank()
                        for t in range(QT):
                            ins = mm(ps[:, b], HTOK[:, t, P * k:P * k + P], PICK[:, t, SEQ * h:SEQ * h + SEQ],
                                     start=t == 0, stop=t == QT - 1)
                        ins.then_inc(S["tile_done"], 1)
                pe.wait_ge(S["table_in"], w.next("table_in"))
                for j in range(2):
                    ins = mm(ps[:, 6, P * j:P * j + P], ONES, DIAGS[:, j], start=True, stop=True)
                ins.then_inc(S["table_rows"], 1)
                pe.wait_ge(S["weigh_in"], w.next("weigh_in", QT))
                for n in range(PAIR_T):
                    b = bank()
                    for t in range(QT):
                        ins = mm(ps[:, b, P * t:P * t + P], WEIGH[:, t, P * n:P * n + P], IDENT,
                                 is_transpose=True, start=True, stop=True)
                    ins.then_inc(S["tile_done"], 1)
                if w.counted("act_evac"):
                    pe.wait_ge(S["act_evac"], w.value("act_evac"))
                pe_moe()
                begin_stage("act_evac")
                pe.wait_ge(S["dn_evac"], w.next("dn_evac", 4))
                for n in range(PAIR_T):
                    for j in range(2):
                        b = bank()
                        for k in range(4):
                            ins = mm(ps[:, b, P * k:P * k + P], YS[:, 4 * j + k, P * n:P * n + P], IDENT,
                                     is_transpose=True, start=True, stop=True)
                        ins.then_inc(S["tile_done"], 1)
                begin_stage("dve_evac")
                for k in range(DT):
                    b = bank()
                    for n in range(PAIR_T):
                        ins = mm(ps[:, b], YPAIR[:, n, P * k:P * k + P], WPAIR[:, n], start=n == 0, stop=n == PAIR_T - 1)
                    ins.then_inc(S["tile_done"], 1)
                norm_sum(8, SEQ, 7, lambda t: HN[:, t])
                pe.wait_ge(S["p_in"], w.next("p_in", 16))
                begin_stage("dve_evac", 4)
                for g in range(2):
                    wp = take()
                    for n in range(4):
                        b = bank()
                        for k in range(2):
                            ins = mm(ps[:, b], wp[:, 2 * n + k], PX[:, k], start=k == 0, stop=k == 1)
                            if n == k == 0:
                                begun(ins)
                    for n in range(4):
                        wt = take()
                        for k in range(DT):
                            if g == n == 0:
                                pe.wait_ge(S["norm_out"], w.next("norm_out"))
                            ins = mm(ps[:, 4 + n], wt[:, k], HA[:, k], start=k == 0, stop=k == DT - 1)
                            if k == 0:
                                begun(ins)
                        ins.then_inc(S["tile_done"], 1)
                begin_stage("dve_evac")
                norm_sum(8, SEQ, 7, lambda t: MERGED[:, t], at=0)
                pe.wait_ge(S["meta_in"], w.next("meta_in", 16))
                begin_stage("act_evac")
                xk = lambda k: X[:, k]
                for n in range(13):
                    linear2([take()], xk, DT, fresh="norm_out" if n == 0 else None)
                begin_stage("act_evac", 3)
                norm_sum(2, T2, 6, lambda t: R2(t))
                norm_sum(1, T2, 6, lambda t: R2(t))
                wt = take()
                for n in range(8):
                    if n < 4:
                        pe.wait_ge(S["lru_x"], w.next("lru_x"))
                    b = 2 * bank()
                    for h in range(2):
                        ins = mm(ps[:, b + h, 0:HALF], wt[:, n], XC[:, n % 4, HALF * h:HALF * h + HALF], start=True, stop=True)
                        if n == h == 0:
                            begun(ins)
                    ins.then_inc(S["tile_done"], 1)
                pe.wait_ge(S["norm_out"], w.next("norm_out", 3))
                for c in range(3):
                    wt = take()
                    for n in range(4):
                        b = 2 * bank()
                        for k in range(2):
                            for h in range(2):
                                ins = mm(ps[:, b + h, 0:HALF], wt[:, 2 * n + k], PQ[:, k, HALF * h:HALF * h + HALF],
                                         start=k == 0, stop=k == 1)
                                if n == k == h == 0:
                                    begun(ins)
                        ins.then_inc(S["tile_done"], 1)
                wt = take()
                for n in range(4):
                    b = 2 * bank()
                    for h in range(2):
                        ins = mm(ps[:, b + h, 0:HALF], wt[:, n], PKV[:, HALF * h:HALF * h + HALF], start=True, stop=True)
                        if n == h == 0:
                            begun(ins)
                    ins.then_inc(S["tile_done"], 1)
                wv = wt[:, 4:].rearrange("p k c -> p (k c)")
                for c, width in TOK2:
                    ins = mm(ps[0:width, 2 * bank()], PKV[:, c:c + width], wv, start=True, stop=True)
                    ins.then_inc(S["tile_done"], 1)
                begin_stage("act_evac")
                pe_mla()
                pe.wait_ge(S["lru_done"], w.next("lru_done", 4))
                begin_stage("dve_evac")
                for _ in range(8):
                    linear2([take()], lambda k: Y2[:, k], DT)
                layer_norm()
                pe_mlp()
                layer_norm()
                begin_stage("act_evac")
                w.count("ln_out", 8)
                for n in range(16):
                    linear2_parts(1, XHO, XLO, IN_ODD, fresh=n == 0)
                begin_stage("act_evac")
                with pe_loop(2, 8, act_evac=8, w_lo=8):
                    for _ in range(8):
                        linear2_parts(1, XHO, XLO, IN_ODD)
                begin_stage("act_evac")
                with pe_loop(2, 8, act_evac=8):
                    for _ in range(8):
                        wt, b = take(), 2 * bank()
                        for j, (c, width) in enumerate(TOK2):
                            o = ps[0:META, b + 1, 0:P] if j == 0 else ps[:, b, P * (j - 1):P * j]
                            for k in range(DT):
                                ins = mm(o, X[:, k, c:c + width], wt[:, k], start=k == 0, stop=k == DT - 1)
                                if j == k == 0:
                                    begun(ins)
                        ins.then_inc(S["tile_done"], 1)
                begin_stage("act_evac")
                pe_retention()
                begin_stage("dve_evac")
                with pe_loop(2, 8, dve_evac=4):
                    for _ in range(4):
                        linear2([take, take], lambda k: RG[:, k], DT)
                layer_norm()
                pe_mlp()
                layer_norm()

            def R2(t):
                return QN[:, t]

            def linear2(chunks, rhs, kts, fresh=None):
                b = 2 * bank()
                for m, wt in enumerate(chunks):
                    if callable(wt):
                        wt = wt()
                    for k in range(kts):
                        if fresh:
                            pe.wait_ge(S[fresh], w.next(fresh))
                        for h in range(2):
                            ins = mm(ps[:, b + h, 0:HALF], wt[:, k], rhs(m * DT + k)[:, HALF * h:HALF * h + HALF],
                                     start=m == k == 0, stop=m == len(chunks) - 1 and k == kts - 1)
                            if k == h == 0:
                                begun(ins)
                ins.then_inc(S["tile_done"], 1)

            def linear2_parts(chunks, high, low, place=IN_MLP, fresh=False):
                b = 2 * bank()
                for m in range(chunks):
                    wh, wl = take_parts(place)
                    for k in range(DT):
                        if fresh:
                            pe.wait_ge(S["x_lo"], w.next("x_lo"))
                        for h in range(2):
                            for j, (wt, x) in enumerate(((wh, high), (wl, high), (wh, low))):
                                ins = mm(ps[:, b + h, 0:HALF], wt[:, k], x[:, m * DT + k, HALF * h:HALF * h + HALF],
                                         start=m == k == j == 0, stop=m == chunks - 1 and k == DT - 1 and j == 2)
                                if k == h == j == 0:
                                    begun(ins)
                ins.then_inc(S["tile_done"], 1)

            def layer_norm():
                if w.counted("act_evac"):
                    pe.wait_ge(S["act_evac"], w.value("act_evac"))
                if w.counted("dve_evac", 1):
                    pe.wait_ge(S["dve_evac"], w.value("dve_evac", 1))
                for t in range(DT):
                    if t == DT - 1:
                        if w.counted("dve_evac"):
                            pe.wait_ge(S["dve_evac"], w.value("dve_evac"))
                    for h in range(2):
                        ins = mm(ps[:, h, 0:HALF], ONES, X[:, t, HALF * h:HALF * h + HALF], start=t == 0, stop=t == DT - 1)
                ins.then_inc(S["norm_sum"], 1)
                norm_sum(8, T2, 6, lambda t: X[:, t])

            def pe_mlp():
                w.count("ln_out", 8)
                for half in range(2):
                    begin_stage("act_evac")
                    w.count("dve_evac", 16)
                    if half == 0:
                        for n in range(16):
                            linear2_parts(1, XH, XL, fresh=n == 0)
                    else:
                        with pe_loop(2, 8, act_evac=8, w_lo=8):
                            for _ in range(8):
                                linear2_parts(1, XH, XL)
                    begin_stage("dve_evac")
                    with pe_loop(2, 8, dve_evac=4, w_lo=8):
                        for _ in range(4):
                            linear2_parts(2, FH, FL)

            def pe_mla():
                units = [(h, t) for h in range(2) for t in range(5)]
                flat = ps[:, :, :].rearrange("p b c -> p (b c)")
                with w.loop(PAIRS, staged=4, smax=10, diag=10, pt=10, o_evac=1):
                    def logits(u):
                        h, t = units[u]
                        c, width = TOK2[t]
                        keys = c + width
                        r = slice(HD * h, HD * h + HD)
                        if u >= 2:
                            pe.wait_ge(S["smax"], w.next("smax"))
                            if t == 0:
                                pe.nop(nofuse=True)
                        for lo, hi in ((0, min(keys, 512)), (512, keys)):
                            if hi <= lo:
                                continue
                            o = flat[0:width, 1024 * (u % 2) + lo:1024 * (u % 2) + hi]
                            mm(o, SQN[r, c:c + width], SKN[r, lo:hi], start=True, stop=False)
                            ins = mm(o, SQP[r, c:c + width], KPE[r, lo:hi], start=False, stop=True)
                        ins.then_inc(S["logits"], 1)

                    def transposed(u):
                        h, t = units[u]
                        width = TOK2[t][1]
                        pe.wait_ge(S["diag"], w.next("diag"))
                        if t == 0:
                            pe.nop(nofuse=True)
                        for j, (kc, kw) in enumerate(TOK2[:t + 1]):
                            o = ps[0:META, 5, 0:width] if j == 0 else ps[:, 4, P * (j - 1):P * j]
                            ins = mm(o, EX2[u % 2][0:width, kc:kc + kw], DG2[u % 2][0:width, 0:width], start=True, stop=True)
                        ins.then_inc(S["tr"], 1)

                    def values(u):
                        h, t = units[u]
                        c, width = TOK2[t]
                        pe.wait_ge(S["pt"], w.next("pt"))
                        r = slice(HD * h, HD * h + HD)
                        o = ps[r, 7, 0:META] if t == 0 else ps[r, 6, P * (t - 1):P * t]
                        for j, (kc, kw) in enumerate(TOK2[:t + 1]):
                            ins = mm(o, SV2[0:kw, j, HD * h:HD * h + HD], PT2[u % 2][0:kw, j, 0:width],
                                     start=j == 0, stop=j == t)
                        return ins

                    pe.wait_ge(S["staged"], w.next("staged", 4))
                    pe.nop(nofuse=True)
                    logits(0)
                    for u in range(10):
                        if u < 9:
                            logits(u + 1)
                        if u:
                            values(u - 1)
                        transposed(u)
                    pe.wait_ge(S["smax"], w.next("smax", 2))
                    values(9).then_inc(S["o_done"], 1)
                    pe.wait_ge(S["o_evac"], w.next("o_evac"))

            def pe_retention():
                flat = ps[:, :, :].rearrange("p b c -> p (b c)")
                w.count("norm_sd", 5 + 2 + 2)
                with w.loop(RET_HEADS, staged=1, ret_s=5, ret_v=1, ret_used=4, norm_sd=1) as i:
                    pe.wait_ge(S["staged"], w.next("staged"))
                    for j, (c, kw) in enumerate(TOK2):
                        if j >= 2:
                            pe.wait_ge(S["ret_s"], w.next("ret_s"))
                        for lo, hi in ((0, min(T2 - c, 512)), (512, T2 - c)):
                            if hi <= lo:
                                continue
                            o = flat[0:kw, 1024 * (j % 2) + lo:1024 * (j % 2) + hi].rearrange("p (a c) -> p a c", a=1)
                            for k in range(2):
                                ins = mm(o, SRK[:, k, c:c + kw], HN[:, ds(i * 2 + k, 1), c + lo:c + hi], start=k == 0, stop=k == 1)
                        ins.then_inc(S["logits"], 1)
                    pe.wait_ge(S["ret_s"], w.next("ret_s", 2))
                    pe.wait_ge(S["ret_v"], w.next("ret_v"))
                    for v in range(4):
                        if v >= 2:
                            pe.wait_ge(S["ret_used"], w.next("ret_used"))
                        for h in range(2):
                            for j, (c, kw) in enumerate(TOK2):
                                lo, hi = max(c, HALF * h), HALF * (h + 1)
                                if lo >= hi:
                                    continue
                                ins = mm(ps[:, 4 + 2 * (v % 2) + h, lo - HALF * h:HALF], SRV[0:kw, j, P * v:P * v + P],
                                         RSC[0:kw, RSC_OFF[j] + lo - c:RSC_OFF[j] + hi - c],
                                         start=j == 0, stop=True, skip_group_check=True)
                        ins.then_inc(S["ret_o"], 1)
                    for v in range(4):
                        if v >= 2:
                            pe.wait_ge(S["ret_used"], w.next("ret_used"))
                        for h in range(2):
                            ins = mm(ps[:, h, 0:HALF], ONES, RSQ[:, v, HALF * h:HALF * h + HALF], start=v == 0, stop=v == 3)
                    ins.then_inc(S["norm_sum"], 1)
                    pe.wait_ge(S["norm_sd"], w.next("norm_sd"))
                pe.wait_ge(S["ret_y"], w.next("ret_y", RET_HEADS))

            def pe_dsa():
                units = [(h, t) for h in range(2) for t in range(QT)]
                with pe_loop(PAIRS // 2, 8, staged=6, smax=16, diag=16, pt=16, o_evac=2, dve_evac=8):
                    def logits(u):
                        h, t = units[u]
                        r = slice(HD * h, HD * h + HD)
                        if u >= 2:
                            pe.wait_ge(S["smax"], w.next("smax"))
                        mm(ps[:, u % 2, 0:P * (t + 1)], ST1[r, P * t:P * t + P], ST2[r, 0:P * (t + 1)],
                           start=True, stop=True).then_inc(S["logits"], 1)

                    def gate(u):
                        if u % 2 == 0:
                            if w.counted("dve_evac", 1):
                                pe.wait_ge(S["dve_evac"], w.value("dve_evac", 1))
                            w.count("dve_evac")
                            gate.wt = take()
                        for k in range(4 * (u % 2), 4 * (u % 2) + 4):
                            ins = mm(ps[:, 5 + (u // 2) % 2], gate.wt[:, k], HA[:, k], start=k == 0, stop=k == DT - 1)
                            if k == 0:
                                begun(ins)
                        if u % 2:
                            ins.then_inc(S["tile_done"], 1)

                    def transposed(u):
                        h, t = units[u]
                        pe.wait_ge(S["diag"], w.next("diag"))
                        for k in range(t + 1):
                            ins = mm(ps[:, 2 + u % 2, P * k:P * k + P], EX[u % 2][:, P * k:P * k + P], DG[u % 2],
                                     start=True, stop=True)
                        ins.then_inc(S["tr"], 1)

                    def values(u):
                        h, t = units[u]
                        pe.wait_ge(S["pt"], w.next("pt"))
                        for k in range(t + 1):
                            ins = mm(ps[HD * h:HD * h + HD, 4, P * t:P * t + P],
                                     KI[:, P * k + HD * h:P * k + HD * h + HD], PT[u % 2][:, k],
                                     start=k == 0, stop=k == t)
                        return ins

                    for _ in range(2):
                        pe.wait_ge(S["staged"], w.next("staged", 3))
                        logits(0)
                        for u in range(8):
                            if u < 7:
                                logits(u + 1)
                            gate(u)
                            transposed(u)
                            if u:
                                values(u - 1)
                        pe.wait_ge(S["smax"], w.next("smax", 2))
                        values(7).then_inc(S["o_done"], 1)
                        pe.wait_ge(S["o_evac"], w.next("o_evac"))

            def pe_stick():
                units = [(h, t) for h in range(2) for t in reversed(range(QT))]
                with w.loop(PAIRS, staged=3, sp_masked=8, a_masked=8, a_raw=8, o_evac=1):
                    def width(t):
                        return SEQ - P * t

                    def z(u):
                        h, t = units[u]
                        r = slice(HD * h, HD * h + HD)
                        if u >= 6:
                            pe.wait_ge(S["a_raw"], w.next("a_raw"))
                        mm(ps[:, u % 6, 0:width(t)], ST2[r, P * t:P * t + P], ST1[r, P * t:SEQ],
                           start=True, stop=True).then_inc(S["z_done"], 1)

                    def after(u):
                        h, t = units[u]
                        pe.wait_ge(S["sp_masked"], w.next("sp_masked"))
                        for t2 in range(QT - 1, t - 1, -1):
                            o = SP_OFF[t2]
                            ins = mm(ps[:, u % 6, P * (t2 - t):width(t)], NTRI if t2 == t else NONES,
                                     SPP[h][:, o:o + width(t2)], start=False, stop=True, skip_group_check=True)
                        ins.then_inc(S["c_done"], 1)

                    def values(u):
                        h, t = units[u]
                        pe.wait_ge(S["a_masked"], w.next("a_masked"))
                        return mm(ps[HD * h:HD * h + HD, 6, P * t:SEQ], ST3[:, P * t + HD * h:P * t + HD * h + HD],
                                  SPA[u % 2][:, 0:width(t)], start=t == QT - 1, stop=True, skip_group_check=True)

                    pe.wait_ge(S["staged"], w.next("staged", 3))
                    for u in range(4):
                        z(u)
                    for u in range(8):
                        if u + 4 < 8:
                            z(u + 4)
                        after(u)
                        if u:
                            values(u - 1)
                    values(7).then_inc(S["o_done"], 1)
                    pe.wait_ge(S["a_raw"], w.next("a_raw", 6))
                    pe.wait_ge(S["o_evac"], w.next("o_evac"))

            def pe_moe():
                def gate_up(n):
                    pe.wait_ge(S["tokens_in"], w.next("tokens_in"))
                    for m in range(2):
                        for f in range(2):
                            wt = take()
                            for k in range(DT):
                                ins = mm(ps[:, 2 * m + n % 2, P * f:P * f + P], wt[:, k], XW[n % 2][:, k],
                                         start=k == 0, stop=k == DT - 1)
                                if k == 0:
                                    begun(ins)
                        ins.then_inc(S["gu_done"], 1)

                def down(n):
                    pe.wait_ge(S["hid"], w.next("hid"))
                    for h in range(2):
                        if n >= 2:
                            pe.wait_ge(S["dn_evac"], w.next("dn_evac"))
                        wt = take()
                        for j in range(4):
                            for k in range(2):
                                ins = mm(ps[:, 4 + 2 * (n % 2) + h, P * j:P * j + P], wt[:, 2 * j + k], HID[n % 2][:, k],
                                         start=k == 0, stop=k == 1)
                                if j == k == 0:
                                    begun(ins)
                        ins.then_inc(S["dn_done"], 1)

                gate_up(0)
                for n in (1, 2):
                    gate_up(n)
                    down(n - 1)
                with pe_loop((WINDOWS - 3) // 4, 24, tokens_in=4, hid=4, dn_evac=8):
                    for n in range(3, 7):
                        gate_up(n)
                        down(n - 1)
                down(WINDOWS - 1)

            body()

        @block.scalar
        def _(act):
            w = Counts(act)
            fn = nc.scalar.activation

            def step(ins):
                ins.then_inc(S["act_ops"], 1)
                act.wait_ge(S["act_ops"], w.next("act_ops"))

            def squares(n, src, dst, fresh=False):
                nc.scalar.preload_act_table_set("natural_log_exp_and_others")
                for t in range(n):
                    if fresh:
                        act.wait_ge(S["dve_evac"], w.next("dve_evac"))
                    fn(dst(t), src(t), ACT.Square).then_inc(S["norm_sq"], 1)

            def inverse_deviation(T, dim, eps):
                pv, rv = (ps[:, 7], R[:, 0:SEQ]) if T == SEQ else (halves(6), two(R[:, :]))
                act.wait_ge(S["norm_sum"], w.next("norm_sum"))
                step(fn(rv, pv, ACT.Ln, scale=1.0 / dim, bias=vec(eps)))
                fn(rv, rv, ACT.Exp, scale=-0.5).then_inc(S["norm_sd"], 1)

            def evac(out, in_, f=ACT.Copy, **kw):
                act.wait_ge(S["tile_done"], w.next("tile_done"))
                fn(out, in_, f, **kw).then_inc(S["act_evac"], 1)

            def bank(n, nb=4):
                return ps[:, n % nb]

            def body():
                R1 = R[:, 0:SEQ]
                act.wait_ge(S["x_in"], 16)
                act.wait_ge(S["consts"], 32)
                step(fn(LAM[:, 0:4], V[:, VEC_AT["lam"]:VEC_AT["lam"] + 4], ACT.Abs))
                fn(LAM[:, 0:4], LAM[:, 0:4], ACT.Exp, scale=-1.0).then_inc(S["lam_exp"], 1)
                squares(8, lambda t: XA[:, t], lambda t: HA[:, t])
                inverse_deviation(SEQ, D, "eps1")
                for n, out in enumerate([CKV, KI] + [QI[:, j] for j in range(4)]):
                    evac(out, bank(n))
                if w.counted("tile_done"):
                    act.wait_ge(S["tile_done"], w.value("tile_done"))
                w.count("tile_done")
                squares(1, lambda t: CKV, lambda t: R1)
                inverse_deviation(SEQ, KV_RANK, "eps1")
                act.wait_ge(S["bias_vec"], w.next("bias_vec"))
                fn(BVEC[:, 0:BIAS_W // 2], ps[0:HEADS, 6, 0:BIAS_W // 2], ACT.Copy)
                fn(BVEC[:, BIAS_W // 2:], ps[0:HEADS, 5, 0:BIAS_W // 2], ACT.Copy).then_inc(S["bias_dram"], 1)
                for n, (t, h) in enumerate((t, h) for t in range(1, QT) for h in range(HEADS)):
                    act.wait_ge(S["rel_done"], w.next("rel_done"))
                    if n >= 2:
                        act.wait_ge(S["rel_used"], w.next("rel_used"))
                    fn(LG[n % 2][:, 0:P * (t + 1)], ps[:, 4 + n % 2, 0:P * (t + 1)], ACT.Relu).then_inc(S["rel_sb"], 1)
                w.count("rel_used", 2)
                for h in range(HEADS):
                    act.wait_ge(S["flip_done"], w.next("flip_done"))
                    fn(BIAS[:, h], ps[:, 4 + h % 2], ACT.Copy).then_inc(S["bias_flip"], 1)
                n = 0
                for j in range(4):
                    evac(QA[:, j], bank(n + j), scale=QK_SCALE)
                for j in range(4):
                    evac(QB[:, j], bank(n + 4 + j), scale=QK_SCALE)
                for j in range(4):
                    evac(KB[:, j], bank(n + 8 + j))
                for j in range(4):
                    evac(VB[:, :, P * j:P * j + P], bank(n + 12 + j).rearrange("p (t c) -> p t c", t=QT))
                for j in range(PAIRS):
                    evac(KA[:, j], bank(j))
                for t in range(QT):
                    evac(VA[:, t], bank(t))
                softmax_pairs(PAIRS, [t for _ in range(2) for t in range(QT)], [(P * (t + 1), P) for t in range(QT)],
                              LG, EX, 1.0, copy_first)
                act_stick()
                w.count("tile_done", 16 + 16)
                act.wait_ge(S["dve_evac"], w.next("dve_evac", 2 + 16))
                for n in range(DT):
                    for x in (GATES[:, n], GATES[:, DT + n]):
                        ins = fn(x, x, ACT.Sigmoid)
                    ins.then_inc(S["gate_on"], 1)
                act.wait_ge(S["dve_evac"], w.next("dve_evac", 8))
                squares(8, lambda t: XA[:, t], lambda t: HA[:, t], fresh=True)
                inverse_deviation(SEQ, D, "eps1")
                act.wait_ge(S["route_e"], w.next("route_e"))
                fn(SMALL[:, 176:192], SMALL[:, 176:192], ACT.Exp).then_inc(S["route_x"], 1)
                for n in range(2 * QT):
                    evac(HTOK[:, n // 2, 512 * (n % 2):512 * (n % 2) + 512], bank(n))
                act.wait_ge(S["route_e"], w.next("route_e"))
                fn(SMALL[:, 200:204], SMALL[:, 200:204], ACT.Exp).then_inc(S["route_x"], 1)
                for n in range(2 * DT):
                    evac(XS[:, n // 2, SEQ * (n % 2):SEQ * (n % 2) + SEQ], bank(n))
                for n in range(PAIR_T):
                    evac(WPAIR[:, n], bank(n))

                act.wait_ge(S["table"], w.next("table"))
                act.wait_ge(S["pad_in"], w.next("pad_in"))

                def tokens(n, at):
                    first = act.value_load(WTAB[:, at], min_val=0, max_val=PAIRED)
                    if n >= 2:
                        act.wait_ge(S["gu_done"], w.next("gu_done"))
                    fn(XW[n % 2], XS[:, :, ds(first, P)], ACT.Copy).then_inc(S["tokens_in"], 1)

                def silu(n):
                    act.wait_ge(S["gu_done"], w.next("gu_done"))
                    if n >= 2:
                        act.wait_ge(S["hid"], w.next("hid"))
                    fn(SILU[n % 2], ps[:, n % 2, 0:2 * P].rearrange("p (f c) -> p f c", f=2), ACT.Silu).then_inc(S["sg"], 1)

                tokens(0, slice(TAB, TAB + 1))
                for n in range(2):
                    tokens(n + 1, slice(TAB + n + 1, TAB + n + 2))
                    silu(n)
                with w.loop((WINDOWS - 3) // 4, gu_done=8, hid=4) as i:
                    for n in range(2, 6):
                        tokens(n + 1, ds(i * 4 + (TAB + n + 1), 1))
                        silu(n)
                act.wait_ge(S["gu_done"], w.next("gu_done"))
                silu(WINDOWS - 1)
                w.count("gu_done")
                for n in range(2 * PAIR_T):
                    evac(YPAIR[:, n // 2, 512 * (n % 2):512 * (n % 2) + 512], bank(n))
                w.count("tile_done", DT)
                squares(8, lambda t: XA[:, t], lambda t: HA[:, t], fresh=True)
                inverse_deviation(SEQ, D, "eps1")
                for n in range(8):
                    act.wait_ge(S["tile_done"], w.next("tile_done"))
                    fn(SG2[n % 2], ps[:, 4 + n % 4], ACT.Sigmoid).then_inc(S["sg"], 1)
                    if n >= 1:
                        act.wait_ge(S["dve_evac"], w.next("dve_evac"))
                        fn(MERGED[:, n - 1], XA[:, n - 1], ACT.Square).then_inc(S["norm_sq"], 1)
                nc.scalar.preload_act_table_set("natural_log_exp_and_others")
                act.wait_ge(S["dve_evac"], w.next("dve_evac"))
                fn(MERGED[:, 7], XA[:, 7], ACT.Square).then_inc(S["norm_sq"], 1)
                inverse_deviation(SEQ, D, "eps1")
                ev = [PG[:, j] for j in range(4)] + [PREC[:, j, 3:] for j in range(4)] + [PQ[:, j] for j in range(2)] + [PKV, KPE, KPW]
                act.wait_ge(S["norm_out"], w.next("norm_out", 8 + 1 + 24))
                for n, out in enumerate(ev):
                    evac(two(out), halves(2 * (n % 4)))
                act.wait_ge(S["act_evac"], w.next("act_evac", 30 + 2 * QT + 2 * DT + 3 * PAIR_T + 13))
                squares(2, lambda t: PQ[:, t], lambda t: QN[:, t])
                inverse_deviation(T2, 256, "eps2")
                act.wait_ge(S["norm_out"], w.next("norm_out", 2))
                squares(1, lambda t: PKV, lambda t: QN[:, t])
                inverse_deviation(T2, 128, "eps2")
                for n in range(8):
                    out, bias = (RA, "b_rg_a") if n < 4 else (RX, "b_rg_x")
                    evac(two(out[:, n % 4]), halves(2 * (n % 3)), ACT.Sigmoid, bias=vec(bias, n % 4))
                for j in range(4):
                    act.wait_ge(S["lru_r"], w.next("lru_r"))
                    fn(LRU_T[:, j], RA[:, j], ACT.Tanh)
                    fn(RA[:, j], RA[:, j], ACT.Exp, scale=-1.0).then_inc(S["lru_t"], 1)
                act.wait_ge(S["norm_out"], w.next("norm_out", 1))
                for n, out in enumerate([QN[:, j] for j in range(4)] + [QP[:, j] for j in range(4)] + [QW[:, j] for j in range(4)]
                                        + [KN[:, j] for j in range(4)]):
                    evac(two(out), halves(2 * ((n + 8) % 3)))
                for j, (c, width) in enumerate(TOK2):
                    evac(V2[0:width, j], ps[0:width, 2 * ((24 + j) % 3)])
                act_lru()
                softmax_pairs(PAIRS, [t for _ in range(2) for t in range(5)], [(c + width, width) for c, width in TOK2],
                              LG2, EX2, MLA_SCALE, copy_second)
                w.count("tile_done", 8)
                act.wait_ge(S["dve_evac"], w.next("dve_evac", 8))
                layer_norm("mix", 0)
                mlp(0)
                use = use_of("odqk") + 1
                for n in range(8):
                    high(use + n, place=IN_ODD)
                    evac(two(HN[:, n]), halves(2 * (n % 4)))
                for n in range(8):
                    high(use + 8 + n, place=IN_ODD)
                    evac(two(RK[:, n]), halves(2 * (n % 4)), scale=1.0 / 16)
                with w.loop(2, tile_done=8) as i:
                    for n in range(8):
                        high(use + 16 + n, i, IN_ODD)
                        act.wait_ge(S["tile_done"], w.next("tile_done"))
                        b = 2 * (n % 4)
                        fn(RG[:, ds(i * 8 + n, 1), :].rearrange("p a (h c) -> p (a h) c", h=2), halves(b), ACT.Silu).then_inc(S["act_evac"], 1)
                with w.loop(2, tile_done=8) as i:
                    for n in range(8):
                        act.wait_ge(S["tile_done"], w.next("tile_done"))
                        b = 2 * (n % 4)
                        fn(RV[:, 1:5, ds(i * 1024 + P * n, P)], ps[:, b].rearrange("p (t c) -> p t c", t=4), ACT.Copy)
                        fn(RV[0:META, 0, ds(i * 1024 + P * n, P)], ps[0:META, b + 1, 0:P], ACT.Copy).then_inc(S["act_evac"], 1)
                nc.scalar.preload_act_table_set("natural_log_exp_and_others")
                with w.loop(RET_HEADS, ret_o=4, norm_sum=1, act_ops=1, ret_y=1) as i:
                    fn(SRV[:, 1:5], RV[:, 1:5, ds(i * 512, 512)], ACT.Copy)
                    fn(SRV[0:META, 0], RV[0:META, 0, ds(i * 512, 512)], ACT.Copy).then_inc(S["ret_v"], 1)
                    for v in range(4):
                        act.wait_ge(S["ret_o"], w.next("ret_o"))
                        b = 4 + 2 * (v % 2)
                        fn(two(ROT[:, v]), halves(b), ACT.Copy)
                        fn(two(RSQ[:, v]), halves(b), ACT.Square).then_inc(S["ret_used"], 1)
                    act.wait_ge(S["norm_sum"], w.next("norm_sum"))
                    step(fn(two(R[:, :]), ps[:, 0:2, 0:HALF], ACT.Ln, scale=1.0 / 512, bias=vec("eps2")))
                    fn(R[:, :], R[:, :], ACT.Exp, scale=-0.5).then_inc(S["norm_sd"], 1)
                    act.wait_ge(S["ret_y"], w.next("ret_y"))
                w.count("tile_done", 8)
                act.wait_ge(S["dve_evac"], w.next("dve_evac", 8))
                layer_norm("mix", 1)
                mlp(1)

            def copy_first(u, t):
                fn(PT[u % 2][:, 0:t + 1], ps[:, 2 + u % 2, 0:P * (t + 1)].rearrange("p (k c) -> p k c", k=t + 1),
                   ACT.Copy).then_inc(S["pt"], 1)

            def copy_second(u, t):
                width = TOK2[t][1]
                ins = fn(PT2[u % 2][0:META, 0, 0:width], ps[0:META, 5, 0:width], ACT.Copy)
                if t:
                    ins = fn(PT2[u % 2][:, 1:t + 1], ps[:, 4, 0:P * t].rearrange("p (k c) -> p k c", k=t), ACT.Copy)
                ins.then_inc(S["pt"], 1)

            def softmax_pairs(pairs, order, sizes, lg, ex, scale, copy):
                n = len(order)
                with w.loop(pairs, smax=n, tr=n, act_ops=n, o_done=1) as i:
                    def exponentials(u):
                        keys, rows = sizes[order[u]]
                        act.wait_ge(S["smax"], w.next("smax"))
                        st = SMALL[0:rows, 8 * (u % 2):8 * (u % 2) + 8]
                        step(nc.scalar.mul(st[:, 1:2], st[:, 0:1], -scale))
                        fn(ex[u % 2][0:rows, 0:keys], lg[u % 2][0:rows, 0:keys], ACT.Exp, bias=st[:, 1:2], scale=scale,
                           accum_out=st[:, 2:3]).then_inc(S["expd"], 1)

                    exponentials(0)
                    for u in range(n):
                        if u + 1 < n:
                            exponentials(u + 1)
                        act.wait_ge(S["tr"], w.next("tr"))
                        copy(u, order[u])
                    act.wait_ge(S["o_done"], w.next("o_done"))
                    if copy is copy_first:
                        fn(QA[:, ds(i, 1), :], ps[:, 4:5], ACT.Copy).then_inc(S["o_evac"], 1)
                    else:
                        fn(Y2[:, ds(i + 4, 1), META:], ps[:, 6:7], ACT.Copy)
                        fn(Y2[:, ds(i + 4, 1), 0:META], ps[:, 7:8, 0:META], ACT.Copy).then_inc(S["o_evac"], 1)

            def act_stick():
                units = [(h, t) for h in range(2) for t in reversed(range(QT))]
                nc.scalar.preload_act_table_set("natural_log_exp_and_others")
                with w.loop(PAIRS, z_done=8, act_ops=16, sp=8, c_done=8, o_done=1) as i:
                    def soft(u):
                        h, t = units[u]
                        m = SPT[u % 2][:, 0:SEQ - P * t]
                        act.wait_ge(S["z_done"], w.next("z_done"))
                        if u >= 2:
                            act.wait_ge(S["sp"], w.next("sp"))
                        step(fn(m, ps[:, u % 6, 0:SEQ - P * t], ACT.Abs))
                        step(fn(m, m, ACT.Exp, scale=-1.0))
                        fn(m, m, ACT.Ln, bias=1.0).then_inc(S["soft"], 1)

                    def weights(u):
                        h, t = units[u]
                        act.wait_ge(S["c_done"], w.next("c_done"))
                        fn(SPA[u % 2][:, 0:SEQ - P * t], ps[:, u % 6, 0:SEQ - P * t], ACT.Exp).then_inc(S["a_raw"], 1)

                    soft(0)
                    soft(1)
                    for u in range(8):
                        if u + 2 < 8:
                            soft(u + 2)
                        weights(u)
                    act.wait_ge(S["sp"], w.next("sp", 2))
                    act.wait_ge(S["o_done"], w.next("o_done"))
                    fn(QB[:, ds(i, 1), :], ps[:, 6:7], ACT.Copy).then_inc(S["o_evac"], 1)

            def act_lru():
                for j in range(4):
                    act.wait_ge(S["gelu_in"], w.next("gelu_in"))
                    fn(GELU[:, j], GELU[:, j], ACT.Tanh, scale=math.sqrt(2 / math.pi)).then_inc(S["gelu_th"], 1)
                for j in range(4):
                    act.wait_ge(S["lru_r"], w.next("lru_r"))
                    fn(LRU_T[:, j], LRU_T[:, j], ACT.Sqrt).then_inc(S["lru_t"], 1)

            def layer_norm(kind, l):
                nc.scalar.preload_act_table_set("natural_log_exp_and_others")
                w.count("norm_sum")
                for t in range(DT):
                    act.wait_ge(S["ln_cent"], w.next("ln_cent"))
                    fn(X[:, t], HN[:, t], ACT.Square).then_inc(S["norm_sq"], 1)
                inverse_deviation(T2, D, "eps2")
                if kind == "mix":
                    high(use_of(f"up{l}"))
                elif l == 0:
                    high(use_of("odqk"), place=IN_ODD)
                for t in range(DT):
                    act.wait_ge(S["norm_out"], w.next("norm_out"))
                    fn(X[:, t], HN[:, t], ACT.Identity, bias=vec(f"ln_{kind}_b", 8 * l + t)).then_inc(S["ln_out"], 1)
                    if kind == "mix" or l == 0:
                        fn((XH if kind == "mix" else XHO)[:, t], HN[:, t], ACT.Identity, bias=vec(f"ln_{kind}_b", 8 * l + t)).then_inc(S["x_hi"], 1)

            def high(n, i=None, place=IN_MLP):
                turn = n // SLOTS + 1
                act.wait_ge(chunk_full[n % SLOTS], (turn if i is None else i + turn) * 16)
                act.wait_ge(S["chunk_begun"], n if i is None else i * SLOTS + n)
                fn(place[0][n % 2], RING[:, n % SLOTS], ACT.Copy).then_inc(S["w_hi"], 1)

            def mlp(l):
                n = use_of(f"up{l}") + 1
                if w.counted("dve_evac"):
                    act.wait_ge(S["dve_evac"], w.value("dve_evac"))
                for half in range(2):
                    with w.loop(2, tile_done=8, dve_evac=8) as i:
                        for j in range(8):
                            high(n + j, i)
                            if w.counted("dve_evac", 7):
                                act.wait_ge(S["dve_evac"], w.value("dve_evac", 7))
                            act.wait_ge(S["tile_done"], w.next("tile_done"))
                            fn(two(HN[:, j]), halves(2 * (j % 4)), ACT.Relu).then_inc(S["act_evac"], 1)
                            w.count("dve_evac")
                    n += 16
                    with w.loop(2 - half) as i:
                        for j in range(8):
                            high(n + j, i)
                    n += 16
                    w.count("tile_done", 8)
                    w.count("dve_evac", 8)
                for j in range(7):
                    high(n - 8 + j)
                if w.counted("dve_evac"):
                    act.wait_ge(S["dve_evac"], w.value("dve_evac"))
                layer_norm("mlp", l)

            SG2 = [area(1024, 512), area(1536, 512)]
            body()

        @block.vector
        def _(dve):
            w = Counts(dve)
            v = nc.vector

            def step(ins, k=1):
                ins.then_inc(S["dve_ops"], 1)
                dve.wait_ge(S["dve_ops"], w.next("dve_ops", k))

            def bc(x, *shape):
                return x.unsqueeze(2).to_broadcast([P, *shape])

            def rms(n, T, gain, src, dst):
                w.count("norm_sum")
                dve.wait_ge(S["norm_sd"], w.next("norm_sd"))
                for t in range(n):
                    v.scalar_tensor_tensor(out=dst(t), in0=src(t), scalar=vec(gain, t), in1=R[:, 0:T],
                                           op0=ALU.mult, op1=ALU.mult).then_inc(S["norm_out"], 1)

            def accumulate(out, in_, scale):
                if scale == 1.0:
                    ins = v.tensor_tensor(out, out, in_, ALU.add)
                else:
                    ins = v.scalar_tensor_tensor(out=out, in0=out, scalar=scale, in1=in_, op0=ALU.mult, op1=ALU.add)
                ins.then_inc(S["dve_evac"], 1)

            def layer_norm(kind, l):
                dve.wait_ge(S["norm_sum"], w.next("norm_sum"))
                step(v.tensor_scalar(two(R[:, :]), halves(0), 1.0 / D, None, ALU.mult))
                for t in range(DT):
                    v.tensor_tensor(HN[:, t], X[:, t], R[:, :], ALU.subtract).then_inc(S["ln_cent"], 1)
                w.count("norm_sum")
                dve.wait_ge(S["norm_sd"], w.next("norm_sd"))
                parts = (XH, XL) if kind == "mix" else (XHO, XLO) if l == 0 else None
                for t in range(DT + 2):
                    if t < DT:
                        v.scalar_tensor_tensor(out=HN[:, t], in0=HN[:, t], scalar=vec(f"ln_{kind}_g", 8 * l + t), in1=R[:, :],
                                               op0=ALU.mult, op1=ALU.mult).then_inc(S["norm_out"], 1)
                    if t >= 2 and parts:
                        high, low = parts[0][:, t - 2], parts[1][:, t - 2]
                        dve.wait_ge(S["x_hi"], w.next("x_hi"))
                        v.tensor_tensor(low, X[:, t - 2], high, ALU.subtract).then_inc(S["x_lo"], 1)

            def body():
                dve.wait_ge(S["consts"], 32)
                rms(8, SEQ, "attn_norm", lambda t: XA[:, t], lambda t: HA[:, t])
                w.count("tile_done", 6)
                dve.wait_ge(S["tile_done"], w.next("tile_done"))
                for j in range(2):
                    v.tensor_scalar(WI[:, 16 * j:16 * j + 16], ps[:, 2, 16 * j:16 * j + 16], IDX_SCALE, None, ALU.mult)\
                        .then_inc(S["dve_evac"], 1)
                dve.wait_ge(S["dve_evac"], w.next("dve_evac", 2))
                rms(1, SEQ, "kv_norm", lambda t: CKV, lambda t: CKV)
                for t in range(1, QT):
                    for h in range(HEADS):
                        dve.wait_ge(S["rel_sb"], w.next("rel_sb"))
                        rel, scalar = LG[((t - 1) * HEADS + h) % 2][:, 0:P * (t + 1)], WI[:, 8 * t + h:8 * t + h + 1]
                        if h == 0:
                            ins = v.tensor_scalar(SCORES[t], rel, scalar, None, ALU.mult)
                        else:
                            ins = v.scalar_tensor_tensor(out=SCORES[t], in0=rel, scalar=scalar, in1=SCORES[t],
                                                         op0=ALU.mult, op1=ALU.add)
                        ins.then_inc(S["rel_used"], 1)
                        dve.wait_ge(S["rel_used"], w.next("rel_used"))
                dve.wait_ge(S["bias_rows"], w.next("bias_rows", 16))
                top = SMALL[:, 16:24]
                for t in range(1, QT):
                    dve.wait_ge(S["score_cut"], w.next("score_cut"))
                    for _ in range(N_SEL // 8):
                        step(v.max(top, SCORES[t]))
                        step(v.match_replace(out=SCORES[t], in_to_replace=top, in_values=SCORES[t], imm_value=TAKEN))
                    step(v.tensor_scalar(MASKS[t], SCORES[t], TAKEN, NEG, ALU.not_equal, ALU.mult))
                dve.wait_ge(S["act_evac"], w.next("act_evac", 30))
                w.count("tile_done", 30 - 6)
                dve.wait_ge(S["score_mask"], w.next("score_mask"))
                dve.wait_ge(S["bias_flip"], w.next("bias_flip", 8))
                softmax_pairs(PAIRS, [t for _ in range(2) for t in range(QT)], stage_first, maximum_first,
                              DG, [P] * QT, 3, 2 * 8, gate_out)
                dve_stick()
                dve.wait_ge(S["o_evac"], w.next("o_evac", 8))
                for n in range(DT):
                    dve.wait_ge(S["tile_done"], w.next("tile_done"))
                    dve.wait_ge(S["gate_on"], w.next("gate_on"))
                    b = 2 * (n % 4)
                    v.tensor_tensor(GATES[:, n], GATES[:, n], ps[:, b], ALU.mult)
                    v.tensor_tensor(GATES[:, DT + n], GATES[:, DT + n], ps[:, b + 1], ALU.mult).then_inc(S["dve_evac"], 1)
                for n in range(DT):
                    dve.wait_ge(S["tile_done"], w.next("tile_done"))
                    accumulate(XA[:, n], ps[:, n % 4], 1.0)
                dve.wait_ge(S["dve_evac"], w.next("dve_evac", 16 + 16))
                rms(8, SEQ, "ffn_norm", lambda t: XA[:, t], lambda t: HA[:, t])
                router()
                dve_moe()
                rms(8, SEQ, "ple_norm", lambda t: XA[:, t], lambda t: HA[:, t])
                for n in range(DT):
                    dve.wait_ge(S["tile_done"], w.next("tile_done"))
                    dve.wait_ge(S["sg"], w.next("sg"))
                    step(v.tensor_tensor(HT[n % 2], SG[n % 2], ps[:, n % 4], ALU.mult))
                    accumulate(XA[:, n], HT[n % 2], 1.0)
                dve.wait_ge(S["dve_evac"], w.next("dve_evac", 8))
                rms(8, SEQ, "final_norm", lambda t: XA[:, t], lambda t: XA[:, t])
                dve_lru()
                dve.wait_ge(S["c2_in"], w.next("c2_in", 48))
                dve.wait_ge(S["act_evac"], w.next("act_evac", 4 + 8))
                for x, swapped in [(QP[:, j], QW[:, j]) for j in range(4)] + [(KPE, KPW)]:
                    v.tensor_tensor(x, x, ROPE_C, ALU.mult)
                    step(v.tensor_tensor(swapped, swapped, ROPE_S, ALU.mult))
                    step(v.tensor_tensor(x, x, swapped, ALU.add))
                dve.wait_ge(S["act_evac"], w.next("act_evac", 4 + 5))
                softmax_pairs(PAIRS, [t for _ in range(2) for t in range(5)], stage_second, maximum_second,
                              DG2, [width for _, width in TOK2], 4, 12, recurrence)
                w.count("tile_done", 13 + 8 + 16 + 5)
                for n in range(DT):
                    dve.wait_ge(S["tile_done"], w.next("tile_done"))
                    accumulate(two(X[:, n]), halves(2 * (n % 4)), ALPHA)
                layer_norm("mix", 0)
                mlp(0)
                dve.wait_ge(S["c3_in"], w.next("c3_in", 48))
                for x in (HN, RK):
                    for h in range(RET_HEADS):
                        dve.wait_ge(S["act_evac"], w.next("act_evac", 2))
                        x1, x2, t1, t2 = x[:, 2 * h], x[:, 2 * h + 1], ROPED[:, 0], ROPED[:, 1]
                        v.tensor_tensor(t1, x1, SIN, ALU.mult)
                        step(v.tensor_tensor(t2, x2, SIN, ALU.mult))
                        v.tensor_tensor(x1, x1, COS, ALU.mult)
                        step(v.tensor_tensor(x2, x2, COS, ALU.mult))
                        v.tensor_tensor(x1, x1, t2, ALU.subtract)
                        step(v.tensor_tensor(x2, x2, t1, ALU.add))
                dve.wait_ge(S["act_evac"], w.next("act_evac", 32))
                flat = ps[:, :, :].rearrange("p b c -> p (b c)")
                v.tensor_copy(SRK, RK[:, 0:2]).then_inc(S["staged"], 1)

                def head(i, last=False):
                    for j, (c, kw) in enumerate(TOK2):
                        dve.wait_ge(S["logits"], w.next("logits"))
                        lo = 1024 * (j % 2)
                        v.tensor_tensor(RSC[0:kw, RSC_OFF[j]:RSC_OFF[j] + T2 - c].unsqueeze(1),
                                        flat[0:kw, lo:lo + T2 - c].unsqueeze(1),
                                        DECAY[0:kw, ds(i, 1), 0:T2 - c], ALU.mult).then_inc(S["ret_s"], 1)
                    for n in range(4):
                        dve.wait_ge(S["ret_used"], w.next("ret_used"))
                        ins = v.tensor_tensor(ROT[:, n:n + 1], ROT[:, n:n + 1], RG[:, ds(i * 4 + n, 1), :], ALU.mult)
                    step(ins)
                    w.count("norm_sum")
                    dve.wait_ge(S["norm_sd"], w.next("norm_sd"))
                    if not last:
                        v.tensor_copy(SRK, RK[:, ds(i * 2 + 2, 2), :]).then_inc(S["staged"], 1)
                    for n in range(4):
                        ins = v.tensor_tensor(RG[:, ds(i * 4 + n, 1), :], ROT[:, n:n + 1], R[:, :].unsqueeze(1), ALU.mult)
                    ins.then_inc(S["ret_y"], 1)

                with w.loop(RET_HEADS - 1, logits=5, norm_sum=1, norm_sd=1, ret_used=4, dve_ops=1) as i:
                    head(i)
                head(RET_HEADS - 1, last=True)
                w.count("tile_done", 48)
                with w.loop(2, tile_done=4) as i:
                    for n in range(4):
                        dve.wait_ge(S["tile_done"], w.next("tile_done"))
                        accumulate(X[:, ds(i * 4 + n, 1), :].rearrange("p a (h c) -> p (a h) c", h=2), halves(2 * n), ALPHA)
                layer_norm("mix", 1)
                mlp(1)

            def mlp(l):
                for half in range(2):
                    with w.loop(2, act_evac=8, dve_ops=16) as i:
                        for n in range(8):
                            dve.wait_ge(S["act_evac"], w.next("act_evac"))
                            f, at = HN[:, n:n + 1], ds(i * 8 + n, 1)
                            v.tensor_tensor(FH[:, at, :], f, f, ALU.mult).then_inc(S["dve_ops"], 1)
                            step(v.tensor_tensor(f, f, f, ALU.mult), 2)
                            v.tensor_tensor(FL[:, at, :], f, FH[:, at, :], ALU.subtract).then_inc(S["dve_evac"], 1)
                    w.count("tile_done", 16)
                    with w.loop(2, tile_done=4) as i:
                        for n in range(4):
                            dve.wait_ge(S["tile_done"], w.next("tile_done"))
                            accumulate(X[:, ds(i * 4 + n, 1), :].rearrange("p a (h c) -> p (a h) c", h=2), halves(2 * n),
                                       1.0 if half else ALPHA)
                layer_norm("mlp", l)

            def stage_first(i):
                for out, src in ((ST1, QA), (ST2, KA)):
                    v.tensor_copy(out.unsqueeze(1), src[:, ds(i, 1), :]).then_inc(S["staged"], 1)
                v.tensor_copy(KI.rearrange("p (t c) -> p t c", t=QT), VA[:, :, ds(i * P, P)]).then_inc(S["staged"], 1)

            def stage_second(i):
                for out, src in ((SQN, QN), (SQP, QP), (SKN, KN)):
                    v.tensor_copy(out.unsqueeze(1), src[:, ds(i, 1), :]).then_inc(S["staged"], 1)
                v.tensor_copy(SV2[0:META, 0], V2[0:META, 0, ds(i * P, P)])
                v.tensor_copy(SV2[:, 1:5], V2[:, 1:5, ds(i * P, P)]).then_inc(S["staged"], 1)

            def settle(ins=None):
                if ins is not None:
                    step(ins)
                v.nop(nofuse=True)

            def maximum_first(i, u, h, t):
                keys = P * (t + 1)
                lg = LG[u % 2][:, 0:keys]
                settle(v.tensor_tensor(lg.unsqueeze(1), ps[:, u % 2:u % 2 + 1, 0:keys],
                                     BIAS[:, ds(i * 2 + h, 1), SEQ - keys:SEQ], ALU.add))
                v.tensor_tensor_reduce(out=lg, in0=lg, in1=MASKS[t], scale=1.0, scalar=TAKEN, op0=ALU.add, op1=ALU.max,
                                       accum_out=SMALL[:, 8 * (u % 2):8 * (u % 2) + 1]).then_inc(S["smax"], 1)

            def maximum_second(i, u, h, t):
                c, rows = TOK2[t]
                keys = c + rows
                flat = ps[:, :, :].rearrange("p b c -> p (b c)")
                first = T2 - P if t == 0 else T2 - keys
                settle()
                v.tensor_tensor_reduce(out=LG2[u % 2][0:rows, 0:keys], in0=flat[0:rows, 1024 * (u % 2):1024 * (u % 2) + keys],
                                       in1=MASKW[0:rows, first:first + keys], scale=1.0, scalar=TAKEN, op0=ALU.add,
                                       op1=ALU.max, accum_out=SMALL[0:rows, 8 * (u % 2):8 * (u % 2) + 1]).then_inc(S["smax"], 1)

            def recurrence(i, u):
                if u != 2:
                    return
                root, keep, state, gate, out = (AREA[:, ds(i * N2 + off, N2)] for off in (2112, 8988, 11100, 0, 24220))
                dve.wait_ge(S["lru_t"], w.next("lru_t"))
                step(v.scalar_tensor_tensor(out=state, in0=root, scalar=-2.0 ** -58, in1=state, op0=ALU.add, op1=ALU.mult))
                step(v.tensor_tensor_scan(out, keep, state, 0.0, ALU.mult, ALU.add))
                dve.wait_ge(S["gelu_done"], w.next("gelu_done"))
                v.tensor_tensor(out, out, gate, ALU.mult).then_inc(S["lru_done"], 1)

            def gate_out(i, u):
                if u % 2:
                    dve.wait_ge(S["tile_done"], w.next("tile_done"))
                    v.tensor_copy(GATES[:, ds(i * 4 + u // 2, 1), :], ps[:, 5 + (u // 2) % 2].unsqueeze(1))\
                        .then_inc(S["dve_evac"], 1)

            def softmax_pairs(pairs, order, stage, maximum, dg, rows_of, n_staged, steps, between=None):
                n = len(order)
                tiles = {gate_out: dict(tile_done=4), recurrence: dict(lru_t=1, gelu_done=1)}.get(between, {})
                with w.loop(pairs, logits=n, expd=n, dve_ops=steps, o_done=1, **tiles) as i:
                    stage(i)
                    def largest(u):
                        dve.wait_ge(S["logits"], w.next("logits"))
                        maximum(i, u, u // (n // 2), order[u])

                    def scale(u):
                        rows = rows_of[order[u]]
                        st = SMALL[0:rows, 8 * (u % 2):8 * (u % 2) + 8]
                        dve.wait_ge(S["expd"], w.next("expd"))
                        step(v.reciprocal(st[:, 3:4], st[:, 2:3]))
                        v.tensor_scalar(dg[u % 2][0:rows, 0:rows], IDENT[0:rows, 0:rows], st[:, 3:4], None, ALU.mult)\
                            .then_inc(S["diag"], 1)

                    largest(0)
                    for u in range(n):
                        if u + 1 < n:
                            largest(u + 1)
                        scale(u)
                        if between:
                            between(i, u)
                    dve.wait_ge(S["o_done"], w.next("o_done"))

            def dve_stick():
                units = [(h, t) for h in range(2) for t in reversed(range(QT))]
                with w.loop(PAIRS, soft=8, o_done=1) as i:
                    for out, src in ((ST1, QB), (ST2, KB)):
                        v.tensor_copy(out.unsqueeze(1), src[:, ds(i, 1), :]).then_inc(S["staged"], 1)
                    v.tensor_copy(ST3.rearrange("p (t c) -> p t c", t=QT), VB[:, :, ds(i * P, P)]).then_inc(S["staged"], 1)
                    for u, (h, t) in enumerate(units):
                        width = SEQ - P * t
                        dve.wait_ge(S["soft"], w.next("soft"))
                        v.scalar_tensor_tensor(out=SPP[h][:, SP_OFF[t]:SP_OFF[t] + width], in0=ps[:, u % 6, 0:width], scalar=0.0,
                                               in1=SPT[u % 2][:, 0:width], op0=ALU.max, op1=ALU.add).then_inc(S["sp"], 1)
                    dve.wait_ge(S["o_done"], w.next("o_done"))

            def first_of(eq, onehot, run):
                n = eq.shape[2]
                step(v.tensor_tensor(eq, eq, FALLING[:, 0:n].unsqueeze(1).to_broadcast([P, QT, n]), ALU.mult))
                step(v.tensor_reduce(run, eq, AX, ALU.max))
                step(v.tensor_tensor(onehot, eq, bc(run, QT, n), ALU.is_equal))

            def small(off, *shape):
                n = int(np.prod(shape))
                x = SMALL[:, off:off + n]
                return x.rearrange("p (a b) -> p a b", a=shape[0]) if len(shape) == 2 else x

            def router():
                lt, gm, sh, eq = small(16, 4, 36), small(160, 4), small(176, 4, 4), small(204, 4, 4)
                run, oh, es = small(220, 4), small(224, 4, 4), small(240, 4, 8)
                prod = SMALL[:, 288:416].rearrange("p (t g e) -> p t g e", t=4, g=4)
                m1, m2, pg, diff = small(164, 4), small(168, 4), small(172, 4), small(200, 4)
                w1, w2 = small(272, 4), small(276, 4)
                dve.wait_ge(S["iota_in"], w.next("iota_in", 16))
                step(v.tensor_scalar(FALLING, IOTA[:, 0:8], -1.0, 8.0, ALU.mult, ALU.add))
                dve.wait_ge(S["route_done"], w.next("route_done"))
                dve.wait_ge(S["wr_in"], w.next("wr_in", 32))
                step(v.tensor_tensor(lt, ps[:, 6, 0:144].rearrange("p (t c) -> p t c", t=4), BR, ALU.add))
                g = lt[:, :, 0:4]
                step(v.tensor_reduce(gm, g, AX, ALU.max))
                v.tensor_tensor(sh, g, bc(gm, 4, 4), ALU.subtract).then_inc(S["route_e"], 1)
                step(v.tensor_tensor(eq, g, bc(gm, 4, 4), ALU.is_equal))
                first_of(eq, oh, run)
                chosen = oh.unsqueeze(3).to_broadcast([P, QT, GROUPS, PER_GROUP])
                step(v.tensor_tensor(prod, lt[:, :, 4:36].rearrange("p t (g e) -> p t g e", g=GROUPS), chosen, ALU.mult))
                step(v.tensor_reduce(es, prod.rearrange("p t g e -> p t e g"), AX, ALU.add))
                eq8, oh1, oh2, es2 = small(16, 4, 8), small(48, 4, 8), small(80, 4, 8), small(112, 4, 8)
                step(v.tensor_reduce(m1, es, AX, ALU.max))
                step(v.tensor_tensor(eq8, es, bc(m1, 4, 8), ALU.is_equal))
                first_of(eq8, oh1, run)
                step(v.scalar_tensor_tensor(out=es2, in0=oh1, scalar=TAKEN, in1=es, op0=ALU.mult, op1=ALU.add))
                step(v.tensor_reduce(m2, es2, AX, ALU.max))
                v.tensor_tensor(diff, m2, m1, ALU.subtract).then_inc(S["route_e"], 1)
                step(v.tensor_tensor(eq8, es2, bc(m2, 4, 8), ALU.is_equal))
                first_of(eq8, oh2, run)
                for pick, inner in ((PICK1, oh1), (PICK2, oh2)):
                    step(v.tensor_tensor(pick.rearrange("p t (g e) -> p t g e", g=GROUPS),
                                         inner.unsqueeze(2).to_broadcast([P, QT, GROUPS, PER_GROUP]), chosen, ALU.mult))
                v.tensor_tensor(PICKED, PICK1, PICK2, ALU.add).then_inc(S["route_ev"], 1)
                dve.wait_ge(S["route_x"], w.next("route_x", 2))
                step(v.tensor_reduce(pg, sh, AX, ALU.add))
                step(v.reciprocal(pg, pg))
                step(v.tensor_scalar(w1, diff, 1.0, None, ALU.add))
                step(v.reciprocal(w1, w1))
                step(v.tensor_tensor(w1, w1, pg, ALU.mult))
                step(v.tensor_tensor(w2, w1, diff, ALU.mult))
                cnt, end, start, many, wend, wfirst, one, t1, t2, off = (TABLE[:, j] for j in range(10))
                dve.wait_ge(S["rank_done"], w.next("rank_done"))
                step(v.tensor_copy(cnt, ps[:, 6, 128:160]))
                step(v.tensor_scalar(one, cnt, 0.0, 1.0, ALU.mult, ALU.add))
                step(v.tensor_tensor_scan(end, one, cnt, 0.0, ALU.mult, ALU.add))
                step(v.tensor_tensor(start, end, cnt, ALU.subtract))
                step(v.tensor_tensor(PICKED, ps[:, 6, 0:128].rearrange("p (t e) -> p t e", t=QT),
                                     start.unsqueeze(1).to_broadcast([P, QT, EXPERTS]), ALU.add))
                for j, pick in enumerate((PICK1, PICK2)):
                    step(v.tensor_tensor(PRODUCT, PICKED, pick, ALU.mult))
                    step(v.tensor_reduce(SLOT[:, j], PRODUCT, AX, ALU.add))
                dve.wait_ge(S["merged"], w.next("merged", DT))
                for t in range(QT):
                    step(v.tensor_scalar(PICK[:, t], IOTA, SLOT[:, 0, t:t + 1], None, ALU.is_equal))
                    v.scalar_tensor_tensor(out=PICK[:, t], in0=IOTA, scalar=SLOT[:, 1, t:t + 1], in1=PICK[:, t],
                                           op0=ALU.is_equal, op1=ALU.add).then_inc(S["pick_in"], 1)
                step(v.tensor_scalar(many, cnt, 0.0, None, ALU.is_gt))
                for j in range(1, QT):
                    step(v.scalar_tensor_tensor(out=many, in0=cnt, scalar=float(P * j), in1=many, op0=ALU.is_gt, op1=ALU.add))
                step(v.tensor_tensor_scan(wend, one, many, 0.0, ALU.mult, ALU.add))
                step(v.tensor_tensor(wfirst, wend, many, ALU.subtract))
                row = vec("row")
                step(v.tensor_scalar(t1, wfirst, row, None, ALU.is_gt))
                step(v.scalar_tensor_tensor(out=t1, in0=wend, scalar=row, in1=t1, op0=ALU.is_gt, op1=ALU.subtract))
                step(v.tensor_scalar(t2, IOTA[:, 0:EXPERTS], 6.0, None, ALU.mult))
                step(v.tensor_tensor(t2, t2, t1, ALU.mult))
                step(v.tensor_reduce(COLUMN[:, 0:1], t2, AX, ALU.add))
                step(v.tensor_scalar(COLUMN[:, 0:1], COLUMN[:, 0:1], float(MOE_AT), None, ALU.add))
                step(v.tensor_scalar(off, wfirst, row, -float(P), ALU.subtract, ALU.mult))
                step(v.scalar_tensor_tensor(out=off, in0=start, scalar=-float(PAIRED), in1=off, op0=ALU.add, op1=ALU.add))
                step(v.tensor_tensor(off, off, t1, ALU.mult))
                step(v.tensor_reduce(COLUMN[:, 1:2], off, AX, ALU.add))
                step(v.tensor_scalar(COLUMN[:, 1:2], COLUMN[:, 1:2], float(PAIRED), None, ALU.add))
                for j in range(2):
                    ins = v.tensor_scalar(DIAGS[:, j], IDENT, COLUMN[:, j:j + 1], None, ALU.mult)
                ins.then_inc(S["table_in"], 1)
                for t in range(QT):
                    step(v.tensor_scalar(WEIGH[:, t], IOTA, SLOT[:, 0, t:t + 1], w1[:, t:t + 1], ALU.is_equal, ALU.mult))
                    step(v.tensor_scalar(PAIR_TMP, IOTA, SLOT[:, 1, t:t + 1], w2[:, t:t + 1], ALU.is_equal, ALU.mult))
                    v.tensor_tensor(WEIGH[:, t], WEIGH[:, t], PAIR_TMP, ALU.add).then_inc(S["weigh_in"], 1)
                dve.wait_ge(S["weigh_in"], w.next("weigh_in", QT))
                dve.wait_ge(S["table_rows"], w.next("table_rows"))
                v.tensor_copy(WTAB.rearrange("p (a n) -> p a n", a=2),
                              ps[0:1, 6, 0:2 * P].rearrange("p (a n) -> p a n", a=2)[:, :, 0:TAB]).then_inc(S["table"], 1)

            def dve_moe():
                w.count("tile_done", 2 * QT + 2 * DT + PAIR_T)
                dve.wait_ge(S["act_evac"], w.next("act_evac", 2 * QT + 2 * DT + PAIR_T))
                dve.wait_ge(S["table"], w.next("table"))

                def hidden(n):
                    dve.wait_ge(S["sg"], w.next("sg"))
                    dve.wait_ge(S["gu_done"], w.next("gu_done", 2))
                    v.tensor_tensor(HID[n % 2], SILU[n % 2], ps[:, 2 + n % 2, 0:2 * P].rearrange("p (f c) -> p f c", f=2),
                                    ALU.mult).then_inc(S["hid"], 1)

                def down(n, at):
                    first = dve.value_load(WTAB[:, at], min_val=0, max_val=PAIRED)
                    if n:
                        dve.wait_ge(S["dn_evac"], w.next("dn_evac", 2))
                    for h in range(2):
                        dve.wait_ge(S["dn_done"], w.next("dn_done"))
                        v.tensor_copy(YS[:, 4 * h:4 * h + 4, ds(first, P)],
                                      ps[:, 4 + 2 * (n % 2) + h].rearrange("p (j c) -> p j c", j=4)).then_inc(S["dn_evac"], 1)

                hidden(0)
                for n in (1, 2):
                    hidden(n)
                    down(n - 1, slice(TAB + n - 1, TAB + n))
                with w.loop((WINDOWS - 3) // 4, sg=4, gu_done=8, dn_done=8, dn_evac=8) as i:
                    for n in range(3, 7):
                        hidden(n)
                        down(n - 1, ds(i * 4 + (TAB + n - 1), 1))
                down(WINDOWS - 1, slice(TAB + WINDOWS - 1, TAB + WINDOWS))
                w.count("tile_done", 2 * PAIR_T)
                w.count("act_evac", 2 * PAIR_T)
                for k in range(DT):
                    dve.wait_ge(S["tile_done"], w.next("tile_done"))
                    accumulate(XA[:, k], ps[:, k % 4], 1.0)
                dve.wait_ge(S["dve_evac"], w.next("dve_evac", DT))

            def dve_lru():
                e, s, s2, acc, sp8 = (LAM[:, 4 * j:4 * j + 4] for j in range(5))
                lam = V[:, VEC_AT["lam"]:VEC_AT["lam"] + 4]
                dve.wait_ge(S["lam_exp"], w.next("lam_exp"))
                step(v.tensor_scalar(s, e, 2.0, None, ALU.add))
                step(v.reciprocal(s, s))
                step(v.tensor_tensor(s, s, e, ALU.mult))
                step(v.tensor_tensor(s2, s, s, ALU.mult))
                step(v.tensor_scalar(acc, s2, 1.0 / 15, 1.0 / 13, ALU.mult, ALU.add))
                for k in (11, 9, 7, 5, 3, 1):
                    step(v.tensor_tensor(acc, acc, s2, ALU.mult))
                    step(v.tensor_scalar(acc, acc, 1.0 / k, None, ALU.add))
                step(v.tensor_tensor(acc, acc, s, ALU.mult))
                step(v.tensor_scalar(sp8, lam, -1.0, 0.0, ALU.mult, ALU.max))
                step(v.scalar_tensor_tensor(out=sp8, in0=acc, scalar=2.0, in1=sp8, op0=ALU.mult, op1=ALU.add))
                step(v.tensor_scalar(sp8, sp8, LRU_C, None, ALU.mult))
                dve.wait_ge(S["pad_zero"], w.next("pad_zero"))
                dve.wait_ge(S["act_evac"], w.next("act_evac", 4))
                for j in range(4):
                    dve.wait_ge(S["act_evac"], w.next("act_evac"))
                    step(v.tensor_scalar(XC[:, j], PREC[:, j, 3:3 + N2], vec("conv_w", 12 + j), vec("conv_b", j), ALU.mult, ALU.add))
                    for k in (2, 1, 0):
                        ins = v.scalar_tensor_tensor(out=XC[:, j], in0=PREC[:, j, k:k + N2], scalar=vec("conv_w", 4 * k + j),
                                                     in1=XC[:, j], op0=ALU.mult, op1=ALU.add)
                        if k:
                            step(ins)
                    ins.then_inc(S["lru_x"], 1)
                dve.wait_ge(S["act_evac"], w.next("act_evac", 5))
                rms(2, T2, "q_norm", lambda t: PQ[:, t], lambda t: PQ[:, t])
                rms(1, T2, "kv_norm2", lambda t: PKV, lambda t: PKV)
                for j in range(4):
                    dve.wait_ge(S["act_evac"], w.next("act_evac"))
                    v.tensor_scalar(RA[:, j], RA[:, j], sp8[:, j:j + 1], None, ALU.mult).then_inc(S["lru_r"], 1)
                dve.wait_ge(S["act_evac"], w.next("act_evac", 4))
                for j in range(4):
                    dve.wait_ge(S["lru_t"], w.next("lru_t"))
                    step(v.tensor_tensor(RX[:, j], RX[:, j], XC[:, j], ALU.mult))
                    step(v.tensor_scalar(XC[:, j], LRU_T[:, j], 1.0, None, ALU.add))
                    step(v.reciprocal(XC[:, j], XC[:, j]))
                    step(v.scalar_tensor_tensor(out=LRU_T[:, j], in0=LRU_T[:, j], scalar=2.0, in1=XC[:, j], op0=ALU.mult, op1=ALU.mult))
                    v.tensor_scalar(LRU_T[:, j], LRU_T[:, j], 2.0 ** -116, None, ALU.max).then_inc(S["lru_r"], 1)

            WI = SMALL[:, 416:448]
            FALLING = SMALL[:, 280:288]
            body()

        @block.gpsimd
        def _(pool):
            w = Counts(pool)
            g = nc.gpsimd

            def step(ins):
                ins.then_inc(S["pool_ops"], 1)
                pool.wait_ge(S["pool_ops"], w.next("pool_ops"))

            def keep(out, compare, fill):
                return g.affine_select(out=out, in_=out, **compare, fill=fill)

            CAUSAL = dict(compare_op=ALU.is_ge, base=0, pattern=[[-1, P]], channel_multiplier=1)
            BEFORE = dict(compare_op=ALU.is_gt, base=0, pattern=[[1, P]], channel_multiplier=-1)

            def body():
                pool.dma_start(HOT, a["onehot"]).then_inc(S["hot_in"], 16)
                pool.dma_start(RELB, a["rel_bias"]).then_inc(S["hot_in"], 16)
                pool.dma_start(WIDX, a["w_idx"]).then_inc(S["small_in"], 16)
                pool.wait_ge(S["bias_dram"], w.next("bias_dram"))
                pool.dma_start(bias_scratch.ap(), BVEC).then_inc(S["bvec_out"], 16)
                pool.wait_ge(S["bvec_out"], w.next("bvec_out", 16))
                rows = bass.AP(bias_scratch, 0, [[1, P], [BIAS_W, HEADS], [1, SEQ]])
                pool.dma_start(BIAS_FLIPPED, rows).then_inc(S["bias_rows"], 16)
                pool.wait_ge(S["bias_rows"], w.next("bias_rows", 16))
                step(g.memset(MASKS[0], 0.0))
                keep(MASKS[0], CAUSAL, NEG).then_inc(S["score_mask"], 1)
                for t in range(1, QT):
                    pool.wait_ge(S["rel_used"], w.next("rel_used", HEADS))
                    keep(SCORES[t][:, P * t:P * t + P], CAUSAL, LOW).then_inc(S["score_cut"], 1)
                pool.wait_ge(S["staged"], w.next("staged", 3))
                pool.dma_start(WROUT, a["w_router"]).then_inc(S["wr_in"], 16)
                pool.dma_start(BR, a["b_router"]).then_inc(S["wr_in"], 16)
                units = [(h, t) for h in range(2) for t in reversed(range(QT))]
                with w.loop(PAIRS, sp=8, a_raw=8):
                    def mask_p(u):
                        h, t = units[u]
                        pool.wait_ge(S["sp"], w.next("sp"))
                        g.nop(nofuse=True)
                        keep(SPP[h][:, SP_OFF[t]:SP_OFF[t] + P], BEFORE, 0.0).then_inc(S["sp_masked"], 1)

                    def mask_a(u):
                        pool.wait_ge(S["a_raw"], w.next("a_raw"))
                        g.nop(nofuse=True)
                        keep(SPA[u % 2][:, 0:P], BEFORE, 0.0).then_inc(S["a_masked"], 1)

                    mask_p(0)
                    mask_p(1)
                    for u in range(8):
                        if u + 2 < 8:
                            mask_p(u + 2)
                        mask_a(u)
                w.count("dve_evac", 2 + 16)
                for n in range(DT):
                    pool.wait_ge(S["dve_evac"], w.next("dve_evac"))
                    g.tensor_tensor(MERGED[:, n], GATES[:, n], GATES[:, DT + n], ALU.add).then_inc(S["merged"], 1)
                pool.wait_ge(S["merged"], w.next("merged", DT))
                g.memset(XS[:, :, PAIRED:], 0.0).then_inc(S["pad_in"], 1)
                pool.dma_start(IOTA, a["iota"]).then_inc(S["iota_in"], 16)
                pool.dma_start(PX, a["p"]).then_inc(S["p_in"], 16)
                pool.wait_ge(S["norm_out"], w.next("norm_out", 33))
                pool.dma_start(MASKW, a["causal"]).then_inc(S["c2_in"], 16)
                pool.dma_start(ROPE_C, a["mla_cos"]).then_inc(S["c2_in"], 16)
                pool.dma_start(ROPE_S, a["mla_sin"]).then_inc(S["c2_in"], 16)
                g.memset(PREC[:, :, 0:3], 0.0).then_inc(S["pad_zero"], 1)
                w.count("act_evac", 30 + 2 * QT + 2 * DT + PAIR_T + 2 * PAIR_T)
                for j in range(4):
                    pool.wait_ge(S["act_evac"], w.next("act_evac"))
                    step(g.tensor_tensor(GELU[:, j], PG[:, j], PG[:, j], ALU.mult))
                    step(g.tensor_scalar(GELU[:, j], GELU[:, j], 0.044715, 1.0, ALU.mult, ALU.add))
                    g.tensor_tensor(GELU[:, j], GELU[:, j], PG[:, j], ALU.mult).then_inc(S["gelu_in"], 1)
                for j in range(4):
                    pool.wait_ge(S["gelu_th"], w.next("gelu_th"))
                    step(g.tensor_scalar(GELU[:, j], GELU[:, j], 0.5, 0.5, ALU.mult, ALU.add))
                    g.tensor_tensor(PG[:, j], PG[:, j], GELU[:, j], ALU.mult).then_inc(S["gelu_done"], 1)
                low_parts(use_of("up0"), 64)
                pool.wait_ge(S["norm_sum"], w.next("norm_sum", 5 + 2 + 2 + 1))
                pool.dma_start(DECAY, a["decay"]).then_inc(S["c3_in"], 16)
                pool.dma_start(COS, a["cos"]).then_inc(S["c3_in"], 16)
                pool.dma_start(SIN, a["sin"]).then_inc(S["c3_in"], 16)
                low_parts(use_of("odqk"), 32, IN_ODD)
                w.count("w_hi")
                low_parts(use_of("up1"), 64)

            def low_parts(first, chunks, place=IN_MLP):
                with w.loop(chunks // 8, w_hi=8):
                    for n in range(first, first + 8):
                        pool.wait_ge(S["w_hi"], w.next("w_hi"))
                        g.tensor_tensor(place[1][n % 2], RING[:, n % SLOTS], place[0][n % 2], ALU.subtract).then_inc(S["w_lo"], 1)

            body()


def bucket(dist):
    dist = np.maximum(dist, 0)
    exact = N_BUCKETS // 2
    d = np.maximum(dist, 1).astype(np.float32)
    large = exact + (np.log(d / exact) / math.log(128 / exact) * (N_BUCKETS - exact)).astype(np.int32)
    return np.where(dist < exact, dist, np.minimum(large, N_BUCKETS - 1))


def constants():
    f = np.float32
    i = np.arange(P)
    mats = np.stack([np.eye(P), np.ones((P, P)), np.eye(P)[::-1], -(i[:, None] >= i[None, :]).astype(f), -np.ones((P, P))], 1)
    hot = np.zeros((N_BUCKETS, BIAS_W), f)
    hot[bucket(SEQ - 1 - np.arange(BIAS_W)), np.arange(BIAS_W)] = 1
    causal = np.where(np.arange(T2)[None, :] - (T2 - P) > i[:, None], NEG, 0.0)
    pos = np.arange(T2, dtype=f)

    def angles(half):
        inv = (f(10000.0) ** (-np.arange(half, dtype=f) / half)).astype(f)
        ang = (pos[None, :] * inv[:, None]).astype(f)
        return np.cos(ang), np.sin(ang)

    c, s = angles(16)
    rope = np.zeros((2, P, T2), f)
    for at in (0, HD):
        rope[0, at:at + 32] = np.concatenate([c, c])
        rope[1, at:at + 32] = np.concatenate([-s, s])
    cos, sin = angles(P)
    log_gamma = np.log(f(1.0) - f(2.0) ** (f(-5.0) - np.arange(RET_HEADS, dtype=f)))
    diff = np.arange(T2)[None, :] - i[:, None]
    decay = np.where(diff[:, None] >= 0, np.exp(log_gamma[None, :, None] * np.maximum(diff, 0)[:, None]), 0)
    out = dict(mats=mats, iota=np.broadcast_to(np.arange(PAIRED), (P, PAIRED)), onehot=hot, causal=causal, mla_cos=rope[0], mla_sin=rope[1], cos=cos, sin=sin, decay=decay)
    return {k: np.ascontiguousarray(v, dtype=f) for k, v in out.items()}


def blocks(w):
    k, n = w.shape
    return w.reshape(k // P, P, n // P, P).transpose(2, 1, 0, 3)


def layout(i):
    f = np.float32
    cut = np.cumsum([0, 512, 128, 512, 64, 8, 1536, 1024, 1024])
    w_in = i["w_in"][0]
    qa, ckv, qidx, kidx, widx, qkv, ga, gb = (w_in[:, a:b] for a, b in zip(cut[:-1], cut[1:]))
    chunks = [blocks(x) for x in (ckv, np.concatenate([kidx, kidx], 1), qidx, qa, qkv)]
    uk = np.moveaxis(i["w_uk"][0], 0, 1).reshape(P, 512)
    uv = np.moveaxis(i["w_uv"][0], 0, 1).reshape(P, 512)
    chunks.append(np.concatenate([uk, uv], 1).reshape(1, P, 8, P))
    chunks += [blocks(ga), blocks(gb)]
    chunks.append(np.concatenate([blocks(i["w_branch_a"][0]), blocks(i["w_branch_b"][0])], 2))
    chunks.append(blocks(i["w_out"][0]))
    gate = [blocks(i["w_gate"][0, e]) for e in range(EXPERTS)]
    up = [blocks(i["w_up"][0, e]) for e in range(EXPERTS)]
    down = [blocks(i["w_down"][0, e]).transpose(1, 0, 2, 3).reshape(P, 2, 8, P).transpose(1, 0, 2, 3) for e in range(EXPERTS)]
    for e in range(EXPERTS):
        chunks += [gate[e], up[e], down[e]]
    ple = blocks(i["w_ple"][0]).transpose(1, 0, 2, 3).reshape(P, 2, 8, P).transpose(1, 0, 2, 3)
    pleg = blocks(i["w_ple_gate"][0])
    chunks += [ple[:1], pleg[:4], ple[1:], pleg[4:]]
    ev = i["ev_w_in_2"][0]
    kpe = ev[:, 1408:1440]
    swap = lambda x: np.concatenate([x[..., 16:], x[..., :16]], -1)
    zero = np.zeros((D, 32), f)
    chunks.append(blocks(np.concatenate([ev[:, :1408], kpe, zero, kpe, zero, swap(kpe), zero, swap(kpe), zero], 1)))
    rg = np.concatenate([i["ev_w_rg_a_2"][0], i["ev_w_rg_x_2"][0]], 0)
    chunks.append(rg.transpose(1, 0, 2)[None])
    uq = i["ev_w_uq_2"][0].reshape(256, HEADS, 96)
    z = np.zeros((256, HEADS, 32), f)
    nope = uq[:, :, :64].reshape(256, 512)
    pe = np.concatenate([uq[:, :, 64:], z], 2).reshape(256, 512)
    pw = np.concatenate([swap(uq[:, :, 64:]), z], 2).reshape(256, 512)
    chunks += [blocks(x).transpose(1, 0, 2, 3).reshape(1, P, 8, P) for x in (nope, pe, pw)]
    ukv = i["ev_w_ukv_2"][0].reshape(P, HEADS, 2, 64)
    chunks.append(np.concatenate([ukv[:, :, 0].reshape(P, 512), ukv[:, :, 1].reshape(P, 512)], 1).reshape(1, P, 8, P))
    chunks.append(blocks(i["ev_w_out_2"][0]))

    def deep(w):
        b = blocks(w)
        return b.reshape(b.shape[0], P, -1, 8, P).transpose(0, 2, 1, 3, 4).reshape(-1, P, 8, P)

    for l in range(2):
        if l:
            odd = blocks(i["od_w_in_2"][0])
            chunks += [odd[:16], odd[32:], odd[16:32], deep(i["od_w_out_2"][0])]
        up, down = blocks(i["mlp_w1_2"][l]), deep(i["mlp_w2_2"][l]).reshape(8, 4, P, 8, P)
        for half in range(2):
            chunks += [up[16 * half:16 * half + 16], down[:, 2 * half:2 * half + 2].reshape(16, P, 8, P)]
    weights = np.concatenate([np.asarray(c, f).reshape(-1, P, D) for c in chunks], 0)
    assert weights.shape[0] == N_CHUNKS, (weights.shape, N_CHUNKS)

    col = lambda x: np.asarray(x, f).reshape(-1, P).T
    vecs = [i["attn_norm"], i["kv_norm"], i["ffn_norm"], i["ple_norm"], i["final_norm"], i["ev_conv_w_2"], i["ev_conv_b_2"],
            i["ev_b_rg_a_2"], i["ev_b_rg_x_2"], i["ev_lru_lambda_2"], i["ev_q_norm_g_2"], i["ev_kv_norm_g_2"],
            i["ln_mix_g_2"], i["ln_mix_b_2"], i["ln_mlp_g_2"], i["ln_mlp_b_2"], np.arange(P), np.full(P, EPS1), np.full(P, EPS2)]
    tiles = lambda x: np.asarray(x, f).T.reshape(-1, P, x.shape[0]).transpose(1, 0, 2)
    rows = lambda x: np.asarray(x, f).reshape(DT, P, -1).transpose(1, 0, 2)
    router = np.concatenate([i["w_r1"][0], np.moveaxis(i["w_r2"][0], 0, 1).reshape(D, EXPERTS)], 1)
    b_router = np.concatenate([i["b_r1"][0], i["b_r2"][0].reshape(-1)])
    out = dict(x=tiles(i["x"][0]), meta=tiles(i["meta_tokens_2"]), p=tiles(i["p"][0, 0]), weights=weights,
               vecs=np.concatenate([col(v) for v in vecs], 1), w_idx=rows(widx), w_router=rows(router),
               b_router=np.broadcast_to(b_router, (P, QT, 36)), rel_bias=i["rel_bias"])
    return {k: np.ascontiguousarray(v, dtype=f) for k, v in (out | constants()).items()}


def kernel(**inputs):
    import concourse.bacc as bacc
    from concourse.bass_utils import run_bass_kernel_spmd

    arrays = layout({k: np.asarray(v) for k, v in inputs.items()})
    nc = bacc.Bacc("TRN2", target_bir_lowering=False, num_devices=1)
    aps = {k: nc.dram_tensor(f"in_{k}", v.shape, F32, kind="ExternalInput").ap() for k, v in arrays.items()}
    aps["out"] = nc.dram_tensor("out_tiles", (P, DT, SEQ), F32, kind="ExternalOutput").ap()
    build(nc, aps)
    r = run_bass_kernel_spmd(nc, [{f"in_{k}": v for k, v in arrays.items()}], core_ids=[0])
    out = r.results[0]["out_tiles"]
    return np.ascontiguousarray(out.transpose(2, 1, 0).reshape(1, SEQ, D))
```
